# Optimizing a Trainium2 kernel written in Bass

```python
import math
import jax, jax.numpy as jnp
from jax import lax
import numpy as np

D_MODEL = 1024
BATCH = 1
SEQ = 512
DEPTH = 2
DEC_BATCH = 8
DEC_SEQ = 1
PAST_LEN = 1024
PAGE_SIZE = 128

HEAD_DIM = 64
D_MIX = D_MODEL
SB_HEADS = D_MIX // (4 * HEAD_DIM)
RET_HEADS = D_MIX // (4 * HEAD_DIM)
NSA_HEADS = D_MIX // (2 * HEAD_DIM)
NSA_KV = NSA_HEADS // 4
NSA_REP = NSA_HEADS // NSA_KV
D_SB = SB_HEADS * HEAD_DIM
D_RET = RET_HEADS * HEAD_DIM
D_NSA = NSA_HEADS * HEAD_DIM
D_NSA_KV = NSA_KV * HEAD_DIM
D_FF = 4 * D_MODEL
ROPE_THETA = 500000.0
ROT_DIM = HEAD_DIM // 4
RET_THETA = 10000.0
RET_CHUNK = 128
Q_BLOCK = 128
BLK_CMP = 32
BLK_SEL = 64
TOP_N = 16
WINDOW = 512
FORCE_SCORE = 1.0e4
NEG = -1.0e30
EPS = 1e-6

kernel_name = 'hymba_style_sb_retention_nsa_decoder_step'

def rms_norm(x, g):
    xf = x.astype(jnp.float32)
    y = xf * lax.rsqrt(jnp.mean(xf * xf, axis=-1, keepdims=True) + EPS)
    return (y * g.astype(jnp.float32)).astype(x.dtype)

def rope(x, pos, rot_dim, theta):
    half = rot_dim // 2
    inv = jnp.exp(-math.log(theta) * jnp.arange(half, dtype=jnp.float32) / half)
    ang = pos.astype(jnp.float32)[:, None] * inv[None, :]
    cos = jnp.cos(ang)[None, :, None, :]
    sin = jnp.sin(ang)[None, :, None, :]
    xr = x[..., :rot_dim].astype(jnp.float32)
    x1, x2 = xr[..., :half], xr[..., half:]
    rot = jnp.concatenate([x1 * cos - x2 * sin, x2 * cos + x1 * sin], axis=-1).astype(x.dtype)
    return jnp.concatenate([rot, x[..., rot_dim:]], axis=-1)

def split_sizes():
    return [D_SB] * 3 + [D_RET] * 4 + [D_NSA] + [D_NSA_KV] * 6 + [3 * NSA_HEADS]

def project(xn, pos, w_in, q_norm_g, k_norm_g):
    b, t, _ = xn.shape
    cuts = [int(c) for c in np.cumsum(split_sizes())[:-1]]
    (sb_q, sb_k, sb_v, r_q, r_k, r_v, r_g, n_q, c_k, c_v, s_k, s_v, w_k, w_v,
     n_g) = jnp.split(xn @ w_in, cuts, axis=-1)
    hd = lambda a: a.reshape(b, t, -1, HEAD_DIM)
    nsa_qk = lambda a, g: rope(rms_norm(hd(a), g), pos, ROT_DIM, ROPE_THETA)
    return {
        'sb_q': hd(sb_q), 'sb_k': hd(sb_k), 'sb_v': hd(sb_v),
        'r_q': rope(hd(r_q), pos, HEAD_DIM, RET_THETA),
        'r_k': rope(hd(r_k), pos, HEAD_DIM, RET_THETA) * HEAD_DIM ** -0.5,
        'r_v': hd(r_v), 'r_g': hd(r_g),
        'n_q': nsa_qk(n_q, q_norm_g),
        'c_k': nsa_qk(c_k, k_norm_g[0]), 'c_v': hd(c_v),
        's_k': nsa_qk(s_k, k_norm_g[1]), 's_v': hd(s_v),
        'w_k': nsa_qk(w_k, k_norm_g[2]), 'w_v': hd(w_v),
        'n_g': jax.nn.sigmoid(n_g.reshape(b, t, NSA_HEADS, 3)),
    }

def map_query_blocks(fn, q, q_pos):
    b, t = q.shape[:2]
    nb = t // Q_BLOCK
    qb = q.reshape(b, nb, Q_BLOCK, *q.shape[2:]).swapaxes(0, 1)
    pb = q_pos.reshape(nb, Q_BLOCK)
    out = lax.map(lambda a: fn(a[0], a[1]), (qb, pb))
    return out.swapaxes(0, 1).reshape(b, t, *out.shape[3:])

def stick_breaking(q, k, v, q_pos, k_pos):
    z = jnp.einsum('bthd,bshd->bhts', q, k).astype(jnp.float32) / math.sqrt(HEAD_DIM)
    mask = (k_pos[None, :] < q_pos[:, None])[None, None]
    log_1m = jnp.where(mask, jax.nn.log_sigmoid(-z), 0.0)
    after = lax.cumsum(log_1m, axis=3, reverse=True) - log_1m
    w = jnp.where(mask, jnp.exp(jax.nn.log_sigmoid(z) + after), 0.0)
    return jnp.einsum('bhts,bshd->bthd', w.astype(v.dtype), v)

def retention_chunk(state, q, k, v, log_gamma):
    c = q.shape[1]
    idx = jnp.arange(c, dtype=jnp.float32)
    diff = idx[:, None] - idx[None, :]
    decay = jnp.where(diff >= 0, jnp.exp(jnp.maximum(diff, 0.0)[None] * log_gamma[:, None, None]), 0.0)
    qf, kf, vf = q.astype(jnp.float32), k.astype(jnp.float32), v.astype(jnp.float32)
    inner = jnp.einsum('bihd,bjhd->bhij', qf, kf) * decay[None]
    o_in = jnp.einsum('bhij,bjhe->bihe', inner, vf)
    q_dec = jnp.exp((idx[:, None] + 1.0) * log_gamma[None, :])
    o_cross = jnp.einsum('bihd,bhde->bihe', qf, state) * q_dec[None, :, :, None]
    k_dec = jnp.exp((c - 1.0 - idx)[:, None] * log_gamma[None, :])
    new_state = (state * jnp.exp(c * log_gamma)[None, :, None, None]
                 + jnp.einsum('bjhd,bjhe->bhde', kf * k_dec[None, :, :, None], vf))
    return new_state, o_in + o_cross

def retention_prompt(q, k, v, log_gamma):
    b, t, h, d = q.shape
    nc = t // RET_CHUNK
    to_c = lambda a: a.reshape(b, nc, RET_CHUNK, h, d).swapaxes(0, 1)
    state0 = jnp.zeros((b, h, d, d), jnp.float32)
    st, o = lax.scan(lambda s, xs: retention_chunk(s, xs[0], xs[1], xs[2], log_gamma),
                     state0, (to_c(q), to_c(k), to_c(v)))
    return o.swapaxes(0, 1).reshape(b, t, h, d), st

def pad_seq(a, before, after):
    return jnp.pad(a, ((0, 0), (before, after), (0, 0), (0, 0)))

def compress(k, w_pos, w_phi):
    kb = k.reshape(k.shape[0], -1, BLK_CMP, *k.shape[2:])
    return jnp.einsum('bnjgd,jd,de->bnge', kb, w_pos, w_phi)

def sel_blocks(k):
    return k.reshape(k.shape[0], -1, BLK_SEL, NSA_KV, HEAD_DIM).transpose(0, 3, 1, 2, 4)

def nsa_keys(c_k, c_v, s_k, s_v, pos_k, pos_v, phi_k, phi_v):
    extra = (-c_k.shape[1]) % BLK_SEL
    pad = lambda a: pad_seq(a, 0, extra)
    return (compress(pad(c_k), pos_k, phi_k), compress(pad(c_v), pos_v, phi_v),
            sel_blocks(pad(s_k)), sel_blocks(pad(s_v)))

def nsa_cmp_slc(q, q_pos, kcmp, vcmp, ks_blk, vs_blk):
    b, tq = q.shape[:2]
    scale = 1.0 / math.sqrt(HEAD_DIM)
    qg = q.reshape(b, tq, NSA_KV, NSA_REP, HEAD_DIM)
    nc = kcmp.shape[1]
    ns = ks_blk.shape[2]
    s = jnp.einsum('btgrd,bngd->btgrn', qg, kcmp).astype(jnp.float32) * scale
    valid = ((jnp.arange(nc) + 1) * BLK_CMP - 1)[None, :] <= q_pos[:, None]
    vmask = valid[None, :, None, None, :]
    p = jnp.where(vmask, jax.nn.softmax(jnp.where(vmask, s, NEG), axis=-1), 0.0)
    o_cmp = jnp.einsum('btgrn,bngd->btgrd', p.astype(vcmp.dtype), vcmp)
    imp = p.sum(axis=3).reshape(b, tq, NSA_KV, ns, BLK_SEL // BLK_CMP).sum(axis=-1)
    blk = jnp.arange(ns)
    forced = (blk[None, :] == 0) | (blk[None, :] == (q_pos // BLK_SEL)[:, None])
    future = (blk * BLK_SEL)[None, :] > q_pos[:, None]
    imp = jnp.where(forced[None, :, None, :], FORCE_SCORE,
                    jnp.where(future[None, :, None, :], -1.0, imp))
    _, idx = lax.top_k(imp, min(TOP_N, ns))
    b_ix = jnp.arange(b)[:, None, None, None]
    g_ix = jnp.arange(NSA_KV)[None, None, :, None]
    kg = ks_blk[b_ix, g_ix, idx]
    vg = vs_blk[b_ix, g_ix, idx]
    s2 = jnp.einsum('btgrd,btgnjd->btgrnj', qg, kg).astype(jnp.float32) * scale
    kpos = idx[..., None] * BLK_SEL + jnp.arange(BLK_SEL)
    m2 = (kpos <= q_pos[None, :, None, None, None])[:, :, :, None]
    s2 = jnp.where(m2, s2, NEG)
    p2 = jax.nn.softmax(s2.reshape(*s2.shape[:4], -1), axis=-1).reshape(s2.shape)
    o_slc = jnp.einsum('btgrnj,btgnjd->btgrd', p2.astype(vg.dtype), vg)
    return o_cmp.reshape(b, tq, NSA_HEADS, HEAD_DIM), o_slc.reshape(b, tq, NSA_HEADS, HEAD_DIM)

def window_attn(q, k, v, q_pos, k_pos):
    b, tq = q.shape[:2]
    qg = q.reshape(b, tq, NSA_KV, NSA_REP, HEAD_DIM)
    s = jnp.einsum('btgrd,bsgd->btgrs', qg, k).astype(jnp.float32) / math.sqrt(HEAD_DIM)
    d = q_pos[:, None] - k_pos[None, :]
    m = ((d >= 0) & (d <= WINDOW) & (k_pos[None, :] >= 0))[None, :, None, None, :]
    p = jax.nn.softmax(jnp.where(m, s, NEG), axis=-1)
    o = jnp.einsum('btgrs,bsgd->btgrd', p.astype(v.dtype), v)
    return o.reshape(b, tq, NSA_HEADS, HEAD_DIM)

def merge_heads(pr, o_sb, o_ret, o_nsa3, w_out):
    b, t = o_sb.shape[:2]
    of = o_ret.astype(jnp.float32)
    mu = jnp.mean(of, axis=-1, keepdims=True)
    var = jnp.mean(jnp.square(of - mu), axis=-1, keepdims=True)
    o_ret = ((of - mu) * lax.rsqrt(var + EPS)).astype(o_sb.dtype) * jax.nn.silu(pr['r_g'])
    o_nsa = jnp.sum(o_nsa3 * pr['n_g'][..., None].astype(o_nsa3.dtype), axis=-2)
    cat = jnp.concatenate([o_sb.reshape(b, t, -1), o_ret.reshape(b, t, -1),
                           o_nsa.reshape(b, t, -1)], axis=-1)
    return cat @ w_out

def sq_relu_mlp(x, g, w_up, w_down):
    h = jax.nn.relu(rms_norm(x, g) @ w_up)
    return (h * h) @ w_down

def setup_inputs(seed: int = 0) -> dict:
    key = jax.random.key(seed)
    ks = jax.random.split(key, 24)
    n_pages = PAST_LEN // PAGE_SIZE
    n_pool = (5 * DEC_BATCH * n_pages + 3) // 4
    wb = min(WINDOW, PAST_LEN)
    n_in = sum(split_sizes())
    nrm = lambda k, shape, scale=1.0: scale * jax.random.normal(k, shape, jnp.float32)
    gain = lambda k, shape: 1.0 + 0.05 * jax.random.normal(k, shape, jnp.float32)
    page_table = jax.random.permutation(ks[11], n_pool)[:DEC_BATCH * n_pages]
    page_table = page_table.reshape(DEC_BATCH, n_pages).astype(jnp.int32)
    return {
        'x_prompt': nrm(ks[0], (BATCH, SEQ, D_MODEL)),
        'x_sample': nrm(ks[1], (DEC_BATCH, DEC_SEQ, D_MODEL)),
        'cache_sb_k': nrm(ks[2], (DEPTH, n_pool, PAGE_SIZE, SB_HEADS, HEAD_DIM)),
        'cache_sb_v': nrm(ks[3], (DEPTH, n_pool, PAGE_SIZE, SB_HEADS, HEAD_DIM)),
        'cache_cmp_k': nrm(ks[4], (DEPTH, n_pool, PAGE_SIZE, NSA_KV, HEAD_DIM)),
        'cache_cmp_v': nrm(ks[5], (DEPTH, n_pool, PAGE_SIZE, NSA_KV, HEAD_DIM)),
        'cache_slc_k': nrm(ks[6], (DEPTH, n_pool, PAGE_SIZE, NSA_KV, HEAD_DIM)),
        'cache_slc_v': nrm(ks[7], (DEPTH, n_pool, PAGE_SIZE, NSA_KV, HEAD_DIM)),
        'state_win_k': nrm(ks[8], (DEPTH, DEC_BATCH, wb, NSA_KV, HEAD_DIM)),
        'state_win_v': nrm(ks[9], (DEPTH, DEC_BATCH, wb, NSA_KV, HEAD_DIM)),
        'state_ret': nrm(ks[10], (DEPTH, DEC_BATCH, RET_HEADS, HEAD_DIM, HEAD_DIM), 0.5),
        'page_table': page_table,
        'norm1_g': gain(ks[12], (DEPTH, D_MODEL)),
        'w_in': nrm(ks[13], (DEPTH, D_MODEL, n_in), D_MODEL ** -0.5),
        'nsa_q_norm': gain(ks[14], (DEPTH, HEAD_DIM)),
        'nsa_k_norm': gain(ks[15], (DEPTH, 3, HEAD_DIM)),
        'cmp_pos_k': (1.0 + 0.5 * jax.random.normal(ks[16], (DEPTH, BLK_CMP, HEAD_DIM), jnp.float32)) * BLK_CMP ** -0.5,
        'cmp_pos_v': (1.0 + 0.5 * jax.random.normal(ks[17], (DEPTH, BLK_CMP, HEAD_DIM), jnp.float32)) * BLK_CMP ** -0.5,
        'cmp_w_k': nrm(ks[18], (DEPTH, HEAD_DIM, HEAD_DIM), HEAD_DIM ** -0.5),
        'cmp_w_v': nrm(ks[19], (DEPTH, HEAD_DIM, HEAD_DIM), HEAD_DIM ** -0.5),
        'w_out': nrm(ks[20], (DEPTH, D_MIX, D_MODEL), D_MIX ** -0.5),
        'norm2_g': gain(ks[21], (DEPTH, D_MODEL)),
        'w_up': nrm(ks[22], (DEPTH, D_MODEL, D_FF), D_MODEL ** -0.5),
        'w_down': nrm(ks[23], (DEPTH, D_FF, D_MODEL), D_FF ** -0.5),
    }

def reference(x_prompt, x_sample, cache_sb_k, cache_sb_v, cache_cmp_k, cache_cmp_v,
              cache_slc_k, cache_slc_v, state_win_k, state_win_v, state_ret, page_table,
              norm1_g, w_in, nsa_q_norm, nsa_k_norm, cmp_pos_k, cmp_pos_v, cmp_w_k, cmp_w_v,
              w_out, norm2_g, w_up, w_down):
    log_gamma = jnp.log1p(-jnp.exp2(-5.0 - jnp.arange(RET_HEADS, dtype=jnp.float32)))
    seq = x_prompt.shape[1]
    n_new = x_sample.shape[1]
    past_len = page_table.shape[1] * cache_sb_k.shape[2]
    wb = state_win_k.shape[2]
    pos_p = jnp.arange(seq, dtype=jnp.int32)
    pos_s = past_len + jnp.arange(n_new, dtype=jnp.int32)
    kpos_s = jnp.arange(past_len + n_new, dtype=jnp.int32)
    wpos_s = past_len - wb + jnp.arange(wb + n_new, dtype=jnp.int32)
    xp, xs = x_prompt, x_sample
    new = {}
    put = lambda name, val: new.setdefault(name, []).append(val)
    for l in range(DEPTH):
        pr = project(rms_norm(xp, norm1_g[l]), pos_p, w_in[l], nsa_q_norm[l], nsa_k_norm[l])
        o_sb = map_query_blocks(
            lambda qb, pb: stick_breaking(qb, pr['sb_k'], pr['sb_v'], pb, pos_p), pr['sb_q'], pos_p)
        o_ret, ret_st = retention_prompt(pr['r_q'], pr['r_k'], pr['r_v'], log_gamma)
        kcmp, vcmp, ks_blk, vs_blk = nsa_keys(pr['c_k'], pr['c_v'], pr['s_k'], pr['s_v'],
                                              cmp_pos_k[l], cmp_pos_v[l], cmp_w_k[l], cmp_w_v[l])
        kw_pad = pad_seq(pr['w_k'], WINDOW, 0)
        vw_pad = pad_seq(pr['w_v'], WINDOW, 0)

        def nsa_block(qb, pb):
            o_c, o_s = nsa_cmp_slc(qb, pb, kcmp, vcmp, ks_blk, vs_blk)
            start = pb[0]
            kwb = lax.dynamic_slice_in_dim(kw_pad, start, WINDOW + Q_BLOCK, axis=1)
            vwb = lax.dynamic_slice_in_dim(vw_pad, start, WINDOW + Q_BLOCK, axis=1)
            kpos = start - WINDOW + jnp.arange(WINDOW + Q_BLOCK, dtype=jnp.int32)
            o_w = window_attn(qb, kwb, vwb, pb, kpos)
            return jnp.stack([o_c, o_s, o_w], axis=-2)

        o_nsa3 = map_query_blocks(nsa_block, pr['n_q'], pos_p)
        xp = xp + merge_heads(pr, o_sb, o_ret, o_nsa3, w_out[l])
        xp = xp + sq_relu_mlp(xp, norm2_g[l], w_up[l], w_down[l])
        keep = min(WINDOW, seq)
        put('p_sb_k', pr['sb_k']); put('p_sb_v', pr['sb_v'])
        put('p_cmp_k', pr['c_k']); put('p_cmp_v', pr['c_v'])
        put('p_slc_k', pr['s_k']); put('p_slc_v', pr['s_v'])
        put('p_win_k', pr['w_k'][:, seq - keep:]); put('p_win_v', pr['w_v'][:, seq - keep:])
        put('p_ret', ret_st)

        sr = project(rms_norm(xs, norm1_g[l]), pos_s, w_in[l], nsa_q_norm[l], nsa_k_norm[l])

        def past(cache):
            rows = cache[l][page_table]
            return rows.reshape(rows.shape[0], -1, *rows.shape[3:])

        sb_k_all = jnp.concatenate([past(cache_sb_k), sr['sb_k']], axis=1)
        sb_v_all = jnp.concatenate([past(cache_sb_v), sr['sb_v']], axis=1)
        o_sb_s = stick_breaking(sr['sb_q'], sb_k_all, sb_v_all, pos_s, kpos_s)
        ret_new, o_ret_s = retention_chunk(state_ret[l].astype(jnp.float32), sr['r_q'], sr['r_k'],
                                           sr['r_v'], log_gamma)
        kcmp_s, vcmp_s, ks_blk_s, vs_blk_s = nsa_keys(
            jnp.concatenate([past(cache_cmp_k), sr['c_k']], axis=1),
            jnp.concatenate([past(cache_cmp_v), sr['c_v']], axis=1),
            jnp.concatenate([past(cache_slc_k), sr['s_k']], axis=1),
            jnp.concatenate([past(cache_slc_v), sr['s_v']], axis=1),
            cmp_pos_k[l], cmp_pos_v[l], cmp_w_k[l], cmp_w_v[l])
        o_c_s, o_s_s = nsa_cmp_slc(sr['n_q'], pos_s, kcmp_s, vcmp_s, ks_blk_s, vs_blk_s)
        kw_all = jnp.concatenate([state_win_k[l], sr['w_k']], axis=1)
        vw_all = jnp.concatenate([state_win_v[l], sr['w_v']], axis=1)
        o_w_s = window_attn(sr['n_q'], kw_all, vw_all, pos_s, wpos_s)
        o_nsa3_s = jnp.stack([o_c_s, o_s_s, o_w_s], axis=-2)
        xs = xs + merge_heads(sr, o_sb_s, o_ret_s, o_nsa3_s, w_out[l])
        xs = xs + sq_relu_mlp(xs, norm2_g[l], w_up[l], w_down[l])
        put('s_sb_k', sr['sb_k']); put('s_sb_v', sr['sb_v'])
        put('s_cmp_k', sr['c_k']); put('s_cmp_v', sr['c_v'])
        put('s_slc_k', sr['s_k']); put('s_slc_v', sr['s_v'])
        put('s_win_k', kw_all[:, n_new:]); put('s_win_v', vw_all[:, n_new:])
        put('s_ret', ret_new)
    st = lambda name: jnp.stack(new[name])
    return (xp, xs,
            st('p_sb_k'), st('p_sb_v'), st('p_cmp_k'), st('p_cmp_v'), st('p_slc_k'), st('p_slc_v'),
            st('p_win_k'), st('p_win_v'), st('p_ret'),
            st('s_sb_k'), st('s_sb_v'), st('s_cmp_k'), st('s_cmp_v'), st('s_slc_k'), st('s_slc_v'),
            st('s_win_k'), st('s_win_v'), st('s_ret'))


_drawn_inputs = setup_inputs


def setup_inputs(seed=0):
    import zlib

    import numpy as np

    out = dict(_drawn_inputs(seed))
    spreads = {}
    factors = {'cache_slc_k': 2.93, 'nsa_q_norm': 5.263}
    for name, (base, spread) in spreads.items():
        noise = np.random.default_rng([zlib.crc32(name.encode()), seed]).standard_normal(out[name].shape)
        drawn = base * np.exp(spread * noise) if base else spread * noise
        out[name] = __import__('jax').numpy.asarray(drawn.astype(out[name].dtype))
    for name, factor in factors.items():
        out[name] = (out[name] * factor).astype(out[name].dtype)
    return out
```

```python
import math
from contextlib import ExitStack

import numpy as np
import concourse.bass as bass
from concourse import mybir

F32 = mybir.dt.float32
BF16 = mybir.dt.bfloat16
I32 = mybir.dt.int32
ALU = mybir.AluOpType
ACT = mybir.ActivationFunctionType
AXX = mybir.AxisListType.X

P = 128
D = 1024
KD = D // P
SEQ, NB, DEPTH = 512, 8, 2
PAST, PAGE, NPAGE = 1024, 128, 8
HD = 64
TILES = SEQ // P + 1
TOK = SEQ + NB
FF = 4 * D
EPS = 1e-6
NEG = -1.0e30
WIN = 512
N_IN = 3096
SB_Q, SB_K, SB_V = 0, 256, 512
R_Q, R_K, R_V, R_G = 768, 1024, 1280, 1536
N_Q, C_K, C_V, S_K, S_V, W_K, W_V, N_G = 1792, 2304, 2432, 2560, 2688, 2816, 2944, 3072
T_SBQ, T_SBK, T_RQ, T_RK, T_NQ, T_SK, T_WK = 0, 2, 4, 6, 8, 12, 13
PACK = {0: 0, 1: 512, 3: 896, 2: 1024}
PACKED = 1280
IT_WIN, IT_KW, IT_K, IT_VW, IT_V, IT_WO, IT_UP, IT_DN, N_ITEMS = 0, 6, 7, 15, 16, 24, 26, 34, 42
SLOTS = 3
SLOT = 4096

CONST_COLS = [("ident", 128), ("neg_suffix", 128), ("neg_ones", 128), ("sb_mask", 128), ("ret_mask", 128),
              ("cos_r", TILES * 32), ("sin_r", TILES * 32), ("cos_n", TILES * 8), ("sin_n", TILES * 8),
              ("decay", TILES * 8), ("gam_last", 4), ("gam_one", 2), ("blk_ind", 4), ("grp", 64),
              ("seq_ind", 8), ("blk_idx", 16), ("cmp_any", 1),
              ("sb_neg", 128), ("nsa_neg", 128), ("cmp_neg", 64)]
CONST_AT = {}
_at = 0
for _n, _w in CONST_COLS:
    CONST_AT[_n] = (_at, _w)
    _at += _w
N_CONST = _at
N_KEEP = CONST_AT["sb_neg"][0]


def shape_constants():
    c = np.zeros((P, N_CONST), np.float32)

    def put(name, a):
        s, w = CONST_AT[name]
        c[:, s:s + w] = np.asarray(a, np.float32).reshape(P, w)

    i = np.arange(P)
    put("ident", np.eye(P))
    put("neg_suffix", -(i[:, None] >= i[None, :]).astype(np.float32))
    put("neg_ones", -np.ones((P, P)))
    put("sb_mask", i[:, None] < i[None, :])
    put("ret_mask", i[:, None] <= i[None, :])
    put("sb_neg", np.where(i[:, None] < i[None, :], 0.0, NEG))
    put("nsa_neg", np.where(i[None, :] <= i[:, None], 0.0, NEG))
    pos = np.concatenate([np.arange(SEQ).reshape(4, P), np.full((1, P), PAST)]).astype(np.float32)
    for half, theta, cn, sn in ((32, 10000.0, "cos_r", "sin_r"), (8, 500000.0, "cos_n", "sin_n")):
        inv = np.exp(np.float32(-math.log(theta)) * np.arange(half, dtype=np.float32) / np.float32(half))
        ang = (pos[:, :, None] * inv.astype(np.float32)).astype(np.float32).transpose(1, 0, 2)
        put(cn, np.cos(ang))
        put(sn, np.sin(ang))
    lg = np.log1p(-np.exp2(-5.0 - np.arange(4)))
    dec = np.zeros((P, TILES, 8))
    for t in range(4):
        j = (t * P + i)[:, None]
        dec[:, t, 0:4] = np.exp(j * lg)
        dec[:, t, 4:8] = np.exp(-j * lg) / 8.0
    dec[:, 4, 0:4] = 1.0
    dec[:, 4, 4:8] = 1.0 / 8.0
    put("decay", dec)
    put("gam_last", np.broadcast_to(np.exp((SEQ - 1) * lg), (P, 4)))
    put("gam_one", np.exp(lg)[2 * np.arange(2)[None, :] + i[:, None] // 64])
    put("blk_ind", i[:, None] // 32 == np.arange(4)[None, :])
    put("grp", (i[:, None] // 4 == np.arange(64)[None, :] // 4))
    put("seq_ind", i[:, None] // 8 == np.arange(8)[None, :])
    put("blk_idx", np.broadcast_to(np.arange(16), (P, 16)))
    put("cmp_any", (i >= 31)[:, None])
    q = np.arange(4)[None, :, None] * P + i[:, None, None]
    put("cmp_neg", np.where((np.arange(16)[None, None, :] + 1) * 32 - 1 <= q, 0.0, NEG))
    return c


def build(nc, ins, outs, consts):
    with ExitStack() as ctx:
        Decoder(nc, ctx, ins, outs, consts).program()


def rows(t):
    return P if t < 4 else NB


def cols(t):
    return slice(t * P, t * P + rows(t))


class Decoder:
    def __init__(self, nc, ctx, ins, outs, consts):
        self.nc, self.ctx, self.ins, self.outs, self.consts = nc, ctx, ins, outs, consts
        sb = self.sb
        self.x_res = sb("x_res", [P, TILES, D])
        self.xt = sb("xt", [P, KD * TOK])
        self.big = sb("big", [P, (FF // P) * TOK])
        self.tt = sb("tt", [P, 14, TOK])
        self.ring = sb("ring", [P, SLOTS, SLOT])
        self.cst = sb("cst", [P, N_KEEP])
        self.ident_b = sb("ident_b", [P, P], BF16)
        self.sb_neg_b = sb("sb_neg_b", [P, P], BF16)
        self.nsa_neg_b = sb("nsa_neg_b", [P, P], BF16)
        self.cmp_neg_b = sb("cmp_neg_b", [P, 64], BF16)
        self.g1 = sb("g1", [P, KD])
        self.g2 = sb("g2", [P, KD])
        self.gq = sb("gq", [P, HD])
        self.gk = sb("gk", [P, 3, HD])
        self.pos_k = sb("pos_k", [P, HD])
        self.pos_v = sb("pos_v", [P, HD])
        self.phi_k = sb("phi_k", [P, P])
        self.phi_v = sb("phi_v", [P, P])
        self.w_tail = sb("w_tail", [P, KD, 24])
        self.gates = sb("gates", [P, TILES, 24])
        self.q_nsa = sb("q_nsa", [P, 576])
        self.q_sb = sb("q_sb", [P, 544])
        self.q_ret = sb("q_ret", [P, 544])
        self.small = sb("small", [P, 250])
        self.stat = sb("stat", [P, 75])
        self.scr = sb("scr", [P, 3200])
        self.pages = sb("pages", [1, NB * NPAGE], I32)
        self.ps = ctx.enter_context(nc.psum_tensor("ps", [P, 8, 512], F32))
        self.psf = self.ps[:].rearrange("p b n -> p (b n)")
        self.proj = self.big[:, 0:TILES * N_IN].rearrange("p (t n) -> p t n", n=N_IN)
        self.spare = self.big[:, TILES * N_IN:]
        self.hid = self.big[:].rearrange("p (f t) -> p f t", t=TOK)
        self.xtv = self.xt[:].rearrange("p (k t) -> p k t", t=TOK)
        self.layer_sems = []
        self.slot_ready = [self.sem(f"slot{s}_ready") for s in range(SLOTS)]
        self.outputs_done = self.sem("outputs_done")
        self.shift_done = self.sem("window_shift_done")
        self.small_ready = self.sem("small_ready")
        self.ret_state_in = self.sem("ret_state_in")
        self.n_out = 0
        self.freed = [None] * N_ITEMS
        self.issued = 0

    def sb(self, name, shape, dt=F32):
        return self.ctx.enter_context(self.nc.sbuf_tensor(name, shape, dt))

    def sem(self, name):
        s = self.ctx.enter_context(self.nc.semaphore(name))
        self.layer_sems.append(s)
        return s

    def c(self, name):
        s, w = CONST_AT[name]
        return self.cst[:, s:s + w]

    def loads_of(self, i):
        if IT_K <= i < IT_VW or IT_V <= i < IT_WO:
            return 3 * NPAGE
        if IT_WO <= i < IT_UP:
            return 3
        return 1

    def item_ready(self, i):
        return self.slot_ready[i % SLOTS], 16 * sum(self.loads_of(j) for j in range(i % SLOTS, i + 1, SLOTS))

    def slot(self, i):
        return self.ring[:, i % SLOTS, :]

    def issue_until(self, sp, l, last):
        while self.issued < min(last, N_ITEMS):
            i = self.issued
            if i >= SLOTS:
                s, v = self.freed[i - SLOTS]
                sp.wait_ge(s, v)
            ready, _ = self.item_ready(i)
            dst, a = self.slot(i), self.ins
            lay = bass.ds(l, 1)
            if i < IT_KW:
                src = a["w_in"][lay, :, i * 512:(i + 1) * 512].rearrange("o (k p) n -> p (o k) n", p=P)
                sp.dma_start(dst.rearrange("p (k n) -> p k n", k=KD), src).then_inc(ready, 16)
            elif i in (IT_KW, IT_VW):
                w = a["state_win_k" if i == IT_KW else "state_win_v"][lay]
                src = w.rearrange("o b (p j) g d -> p (o b) (j g d)", p=P)
                sp.dma_start(dst.rearrange("p (b n) -> p b n", b=NB), src).then_inc(ready, 16)
            elif i < IT_WO:
                kv = "k" if i < IT_VW else "v"
                b = i - (IT_K if kv == "k" else IT_V)
                for j in range(NPAGE):
                    page = sp.value_load(self.pages[0:1, b * NPAGE + j:b * NPAGE + j + 1], min_val=0,
                                         max_val=self.n_pool - 1)
                    at = l * self.n_pool + page
                    for cache, off, w in (("sb", 0, 256), ("slc", 2048, 128), ("cmp", 3072, 128)):
                        src = a[f"cache_{cache}_{kv}"].rearrange("l n t h d -> (l n) t (h d)")[bass.ds(at, 1)]
                        sp.dma_start(dst[:, off + j * w:off + (j + 1) * w],
                                     src.rearrange("o t n -> (o t) n")).then_inc(ready, 16)
            elif i < IT_UP:
                n = i - IT_WO
                w = a["w_out"][lay, :, n * 512:(n + 1) * 512]
                d3 = dst.rearrange("p (k n) -> p k n", k=KD)
                sp.dma_start(d3[:, 0:4, :], w[:, 0:512].rearrange("o (k p) n -> p (o k) n", p=P)).then_inc(ready, 16)
                for g in range(2):
                    src = w[:, 512 + g * 256:768 + g * 256].rearrange("o (r d) n -> d (o r) n", d=HD)
                    sp.dma_start(d3[g * HD:(g + 1) * HD, 4:8, :], src).then_inc(ready, 16)
            elif i < IT_DN:
                c = i - IT_UP
                src = a["w_up"][lay, :, c * 512:(c + 1) * 512].rearrange("o (k p) n -> p (o k) n", p=P)
                sp.dma_start(dst.rearrange("p (k n) -> p k n", k=KD), src).then_inc(ready, 16)
            else:
                n, q = divmod(i - IT_DN, 4)
                src = a["w_down"][lay, q * D:(q + 1) * D, n * 512:(n + 1) * 512]
                sp.dma_start(dst.rearrange("p (k n) -> p k n", k=KD),
                             src.rearrange("o (k p) n -> p (o k) n", p=P)).then_inc(ready, 16)
            self.issued += 1

    def program(self):
        nc = self.nc
        self.n_pool = self.ins["cache_sb_k"].shape[1]
        self.setup()
        with nc.Fori(0, DEPTH) as l:
            self.l = l
            self.norm("n1", self.g1, first=True)
            self.project()
            self.stick_breaking()
            self.retention()
            self.compress_prompt()
            self.nsa_prompt()
            self.retention_sample()
            self.sample_scores()
            self.sample_softmax()
            self.sample_values()
            self.output_projection()
            self.norm("n2", self.g2)
            self.mlp_up()
            self.mlp_down()
            for s in self.layer_sems:
                nc.sync.sem_clear(s)
            nc.all_engine_barrier()
        self.finish()

    def setup(self):
        nc, a = self.nc, self.ins
        loaded, zeroed = self.sem("setup_loaded"), self.sem("setup_zeroed")
        stage = self.xt[:, 0:N_CONST - N_KEEP]
        with nc.Block() as block:
            @block.sync
            def _(sp):
                sp.dma_start(self.cst[:], self.consts[:, 0:N_KEEP]).then_inc(loaded, 16)
                sp.dma_start(stage, self.consts[:, N_KEEP:N_CONST]).then_inc(loaded, 16)
                sp.dma_start(self.pages[:], a["page_table"].rearrange("b j -> (b j)").rearrange(
                    "(o n) -> o n", o=1)).then_inc(loaded, 16)
                sp.dma_start(self.x_res[:, 0:4, :], a["x_prompt"][0].rearrange("(t p) n -> p t n", p=P)
                             ).then_inc(loaded, 16)
                sp.dma_start(self.x_res[0:NB, 4, :], a["x_sample"].rearrange("b s n -> (b s) n")).then_inc(loaded, 16)
                sp.wait_ge(loaded, 80)

            @block.vector
            def _(dve):
                dve.memset(self.q_nsa[:], 0.0)
                dve.memset(self.q_sb[:], 0.0)
                dve.memset(self.q_ret[:], 0.0)
                dve.memset(self.phi_k[:], 0.0)
                dve.memset(self.phi_v[:], 0.0)
                dve.memset(self.stat[:], 1.0).then_inc(zeroed, 1)
                dve.wait_ge(loaded, 80)
                dve.tensor_copy(self.ident_b[:], self.c("ident"))
                dve.tensor_copy(self.sb_neg_b[:], stage[:, 0:128])
                dve.tensor_copy(self.nsa_neg_b[:], stage[:, 128:256])
                dve.tensor_copy(self.cmp_neg_b[:], stage[:, 256:320]).then_inc(zeroed, 1)
                dve.wait_ge(zeroed, 2)
        for s in self.layer_sems:
            nc.sync.sem_clear(s)
        nc.all_engine_barrier()

    def finish(self):
        nc, o = self.nc, self.outs
        stored = self.sem("result_stored")
        with nc.Block() as block:
            @block.sync
            def _(sp):
                sp.dma_start(o["y_prompt"][0].rearrange("(t p) n -> p t n", p=P), self.x_res[:, 0:4, :]
                             ).then_inc(stored, 16)
                sp.dma_start(o["y_sample"].rearrange("b s n -> (b s) n"), self.x_res[0:NB, 4, :]).then_inc(stored, 16)
                sp.wait_ge(stored, 32)

    def linker(self, eng, name):
        chain, n = self.sem(name), [0]

        def link(instr):
            n[0] += 1
            instr.then_inc(chain, 1)
            eng.wait_ge(chain, n[0])
        return link

    def refine_rsqrt(self, dve, link, r, v, tmp):
        link(dve.tensor_tensor(tmp, r, r, ALU.mult))
        link(dve.tensor_tensor(tmp, tmp, v, ALU.mult))
        link(dve.tensor_scalar(tmp, tmp, -0.5, 1.5, ALU.mult, ALU.add))
        link(dve.tensor_tensor(r, r, tmp, ALU.mult))

    def norm(self, name, gain, first=False):
        nc, l = self.nc, self.l
        x, ss = self.x_res, self.stat[:, 0:5]
        r, tmp = self.small[:, 8:13], self.small[:, 16:21]
        xn = self.scr[:, 0:2 * D].rearrange("p (i n) -> p i n", i=2)
        squares, var_ready, root = (self.sem(name + s) for s in ("_squares", "_var", "_root"))
        scaled, turned, copied = (self.sem(name + s) for s in ("_scaled", "_turned", "_copied"))
        with nc.Block() as block:
            if first:
                @block.sync
                def _(sp):
                    self.issued = 0
                    a, o, lay = self.ins, self.outs, bass.ds(l, 1)
                    n = 0
                    loads = [(self.g1[:], a["norm1_g"][lay].rearrange("o (k p) -> p (o k)", p=P)),
                             (self.g2[:], a["norm2_g"][lay].rearrange("o (k p) -> p (o k)", p=P)),
                             (self.w_tail[:], a["w_in"][lay, :, N_G:N_IN].rearrange("o (k p) n -> p (o k) n", p=P)),
                             (self.gq[:], a["nsa_q_norm"][lay].rearrange("o d -> (o d)").partition_broadcast(P)),
                             (self.gk[:].rearrange("p c d -> p (c d)"),
                              a["nsa_k_norm"][lay].rearrange("o c d -> (o c d)").partition_broadcast(P))]
                    for pos, phi, wp, wf in ((self.pos_k, self.phi_k, "cmp_pos_k", "cmp_w_k"),
                                             (self.pos_v, self.phi_v, "cmp_pos_v", "cmp_w_v")):
                        loads += [(pos[c * 32:(c + 1) * 32, :], a[wp][lay].rearrange("o j d -> (o j) d"))
                                  for c in range(4)]
                        loads += [(phi[g * HD:(g + 1) * HD, g * HD:(g + 1) * HD],
                                   a[wf][lay].rearrange("o d e -> (o d) e")) for g in range(2)]
                    with nc.allow_non_contiguous_dma("small gains"):
                        for dst, src in loads:
                            sp.dma_start(dst, src).then_inc(self.small_ready, 16)
                            n += 1
                    self.n_small = 16 * n
                    self.issue_until(sp, l, SLOTS)
                    for kv in "kv":
                        src = a[f"state_win_{kv}"][lay, :, 1:WIN].rearrange("o b w g d -> (o b) (w g d)")
                        dst = o[f"s_win_{kv}"][lay, :, 0:WIN - 1].rearrange("o b w g d -> (o b) (w g d)")
                        sp.dma_start(dst, src).then_inc(self.shift_done, 16)
                    sp.wait_ge(self.small_ready, self.n_small)

            @block.scalar
            def _(act):
                junk = self.psf[:, 3072:4096]
                for t in range(TILES):
                    n = rows(t)
                    if t >= 1:
                        act.wait_ge(squares, t)
                    act.activation(junk[0:n], x[0:n, t, :], ACT.Square, accum_out=ss[0:n, t:t + 1]
                                   ).then_inc(squares, 1)
                act.wait_ge(var_ready, 1)
                act.activation(r, ss, ACT.Ln).then_inc(root, 1)
                act.wait_ge(root, 1)
                act.activation(r, r, ACT.Exp, scale=-0.5).then_inc(root, 1)

            @block.vector
            def _(dve):
                link = self.linker(dve, name + "_dve_chain")
                dve.wait_ge(squares, TILES)
                dve.tensor_scalar(ss, ss, 1.0 / D, EPS, ALU.mult, ALU.add).then_inc(var_ready, 1)
                dve.wait_ge(root, 2)
                self.refine_rsqrt(dve, link, r, ss, tmp)
                if first:
                    dve.wait_ge(self.small_ready, self.n_small)
                for t in range(TILES + 1):
                    if t < TILES:
                        n = rows(t)
                        if t >= 2:
                            dve.wait_ge(turned, t - 1)
                        dve.tensor_scalar(xn[0:n, t % 2, :], x[0:n, t, :], r[0:n, t:t + 1], None, ALU.mult
                                          ).then_inc(scaled, 1)
                    if t >= 1:
                        s, n = t - 1, rows(t - 1)
                        dve.wait_ge(turned, s + 1)
                        for j in range(2):
                            src = self.ps[:, 2 * (s % 2) + j, :].rearrange("p (k n) -> p k n", k=4)[:, :, 0:n]
                            g = gain[:, 4 * j:4 * j + 4].unsqueeze(2).broadcast_to([P, 4, n])
                            ins = dve.tensor_tensor(self.xtv[:, 4 * j:4 * j + 4, cols(s)], src, g, ALU.mult)
                        ins.then_inc(copied, 1)

            @block.tensor
            def _(pe):
                ident = self.c("ident")
                for t in range(TILES):
                    n = rows(t)
                    pe.wait_ge(scaled, t + 1)
                    if t >= 2:
                        pe.wait_ge(copied, t - 1)
                    for k in range(KD):
                        ins = pe.transpose(self.ps[:, 2 * (t % 2) + k // 4, (k % 4) * P:(k % 4) * P + n],
                                           xn[0:n, t % 2, k * P:(k + 1) * P], ident[0:n, 0:n])
                    ins.then_inc(turned, 1)

    def rope(self, eng, link, x, half, cos, sin, tmp, shape):
        a, b = x[..., 0:half], x[..., half:2 * half]
        t = tmp
        eng.tensor_tensor(t[0], a, cos, ALU.mult)
        eng.tensor_tensor(t[1], b, sin, ALU.mult)
        eng.tensor_tensor(t[2], b, cos, ALU.mult)
        link(eng.tensor_tensor(t[3], a, sin, ALU.mult))
        eng.tensor_tensor(a, t[0], t[1], ALU.subtract)
        link(eng.tensor_tensor(b, t[2], t[3], ALU.add))

    def project(self):
        nc, l, pj = self.nc, self.l, self.proj
        mm_done, out_ready = self.sem("proj_mm"), self.sem("proj_out")
        turned, t_copied = self.sem("qk_turned"), self.sem("qk_copied")
        ret_ready, q_ready, k_ready = self.sem("ret_roped"), self.sem("nsa_q_ready"), self.sem("nsa_k_ready")
        exps, var_ready, root, rs_ready = (self.sem(s) for s in ("gate_exp", "head_var", "head_root", "head_rstd"))
        for c in range(6):
            self.freed[c] = (mm_done, TILES * (c + 1))
        ms = self.stat[:, 5:75]
        msv = ms.rearrange("p (t h) -> p t h", t=TILES)
        rs = self.small[:, 104:174]
        rsv = rs.rearrange("p (t h) -> p t h", t=TILES)
        tmp70 = self.small[:, 176:246]
        sq = self.spare[:, 0:896].rearrange("p (h d) -> p h d", d=HD)
        e_rg = self.scr[:, 0:1280].rearrange("p (t n) -> p t n", t=TILES)
        tq = [self.scr[:, 1280 + 256 * i:1536 + 256 * i] for i in range(4)]
        tk = [self.scr[:, 2304 + 48 * i:2352 + 48 * i] for i in range(4)]
        width = lambda c: 512 if c < 6 else 24

        def kview(t, n):
            return pj[0:n, t, C_K:N_G].rearrange("p (c x) -> p c x", c=3)[:, :, 0:P].rearrange(
                "p c (g d) -> p c g d", g=2)

        with nc.Block() as block:
            @block.sync
            def _(sp):
                self.issue_until(sp, l, IT_KW + SLOTS)

            @block.tensor
            def _(pe):
                ident = self.c("ident")
                v = 0

                def turn(t, blocks):
                    nonlocal v
                    n = rows(t)
                    if v >= 2:
                        pe.wait_ge(t_copied, v - 1)
                    for j, c0 in enumerate(blocks):
                        ins = pe.transpose(self.ps[:, 4 + v % 2, j * P:j * P + n], pj[0:n, t, c0:c0 + P],
                                           ident[0:n, 0:n])
                    ins.then_inc(turned, 1)
                    v += 1

                for c in range(7):
                    if c < 6:
                        s, val = self.item_ready(c)
                        pe.wait_ge(s, val)
                        w = self.slot(c).rearrange("p (k n) -> p k n", k=KD)
                    else:
                        w = self.w_tail
                    for t in range(TILES):
                        u, n = c * TILES + t, rows(t)
                        if u >= 4:
                            pe.wait_ge(out_ready, u - 3)
                        for k in range(KD):
                            ins = pe.matmul(self.ps[0:n, u % 4, 0:width(c)], self.xtv[:, k, cols(t)], w[:, k, :],
                                            start=(k == 0), stop=(k == KD - 1))
                        ins.then_inc(mm_done, 1)
                    if c == 2:
                        for t in range(TILES):
                            pe.wait_ge(out_ready, t + 1)
                            turn(t, [SB_Q, SB_Q + P, SB_K, SB_K + P])
                    if c == 4:
                        for t in range(TILES):
                            pe.wait_ge(ret_ready, t + 1)
                            turn(t, [R_Q, R_Q + P, R_K, R_K + P])
                for t in range(TILES):
                    pe.wait_ge(q_ready, t + 1)
                    turn(t, [N_Q + j * P for j in range(4)])
                    pe.wait_ge(k_ready, t + 1)
                    turn(t, [S_K, W_K])

            @block.scalar
            def _(act):
                v = 0

                def copy_turned(t, dst, nblk, scaled):
                    nonlocal v
                    n = rows(t)
                    act.wait_ge(turned, v + 1)
                    src = self.ps[:, 4 + v % 2, 0:nblk * P].rearrange("p (j n) -> p j n", j=nblk)[:, :, 0:n]
                    if scaled:
                        ins = act.activation(self.tt[:, dst:dst + scaled, cols(t)], src[:, 0:scaled, :], ACT.Copy,
                                             scale=HD ** -0.5)
                    if scaled < nblk:
                        ins = act.activation(self.tt[:, dst + scaled:dst + nblk, cols(t)], src[:, scaled:nblk, :],
                                             ACT.Copy)
                    ins.then_inc(t_copied, 1)
                    v += 1

                for c in range(7):
                    for t in range(TILES):
                        u, n = c * TILES + t, rows(t)
                        act.wait_ge(mm_done, u + 1)
                        src = self.ps[0:n, u % 4, :]
                        nq = pj[0:n, t, N_Q:N_Q + 512].rearrange("p (r g d) -> p r g d", r=4, g=2)
                        if c == 3:
                            act.activation(pj[0:n, t, R_G:R_G + 256], src[:, 0:256], ACT.Copy)
                            ins = act.activation(nq[:, :, 0, :], src[:, 256:512].rearrange("p (r d) -> p r d", r=4),
                                                 ACT.Copy)
                        elif c == 4:
                            act.activation(nq[:, :, 1, :], src[:, 0:256].rearrange("p (r d) -> p r d", r=4), ACT.Copy)
                            ins = act.activation(pj[0:n, t, C_K:C_K + 256], src[:, 256:512], ACT.Copy)
                        else:
                            ins = act.activation(pj[0:n, t, c * 512:c * 512 + width(c)], src[:, 0:width(c)], ACT.Copy)
                        ins.then_inc(out_ready, 1)
                    if c == 2:
                        for t in range(TILES):
                            copy_turned(t, T_SBQ, 4, 2)
                    if c == 4:
                        for t in range(TILES):
                            copy_turned(t, T_RQ, 4, 0)
                act.wait_ge(out_ready, 7 * TILES)
                for t in range(TILES):
                    n = rows(t)
                    act.activation(self.gates[0:n, t, :], pj[0:n, t, N_G:N_IN], ACT.Exp, scale=-1.0)
                    act.activation(e_rg[0:n, t, :], pj[0:n, t, R_G:R_G + 256], ACT.Exp, scale=-1.0).then_inc(exps, 1)
                act.wait_ge(var_ready, 1)
                act.activation(rs, ms, ACT.Ln).then_inc(root, 1)
                act.wait_ge(root, 1)
                act.activation(rs, rs, ACT.Exp, scale=-0.5).then_inc(root, 1)
                for t in range(TILES):
                    copy_turned(t, T_NQ, 4, 4)
                    copy_turned(t, T_SK, 2, 0)

            @block.vector
            def _(dve):
                link = self.linker(dve, "proj_dve_chain")
                cosr = self.c("cos_r").rearrange("p (t x) -> p t x", t=TILES)
                sinr = self.c("sin_r").rearrange("p (t x) -> p t x", t=TILES)
                cosn = self.c("cos_n").rearrange("p (t x) -> p t x", t=TILES)
                sinn = self.c("sin_n").rearrange("p (t x) -> p t x", t=TILES)
                dec = self.c("decay").rearrange("p (t x) -> p t x", t=TILES)
                for t in range(TILES):
                    n = rows(t)
                    dve.wait_ge(out_ready, 2 * TILES + t + 1)
                    x = pj[0:n, t, R_Q:R_V].rearrange("p (h d) -> p h d", d=HD)
                    self.rope(dve, link, x, 32, cosr[0:n, t, :].unsqueeze(1).broadcast_to([n, 8, 32]),
                              sinr[0:n, t, :].unsqueeze(1).broadcast_to([n, 8, 32]),
                              [q[0:n].rearrange("p (h d) -> p h d", h=8) for q in tq], [n, 8])
                    dve.tensor_tensor(x, x, dec[0:n, t, :].unsqueeze(2).broadcast_to([n, 8, HD]), ALU.mult
                                      ).then_inc(ret_ready, 1)
                for t in range(TILES):
                    n = rows(t)
                    dve.wait_ge(out_ready, 5 * TILES + t + 1)
                    q = pj[0:n, t, N_Q:N_Q + 512].rearrange("p (h d) -> p h d", d=HD)
                    kk = kview(t, n)
                    dve.tensor_tensor(sq[0:n, 0:8, :], q, q, ALU.mult)
                    link(dve.tensor_tensor(sq[0:n, 8:14, :].rearrange("p (c g) d -> p c g d", c=3), kk, kk, ALU.mult))
                    link(dve.tensor_reduce(msv[0:n, t, :], sq[0:n], AXX, ALU.add))
                dve.tensor_scalar(ms, ms, 1.0 / HD, EPS, ALU.mult, ALU.add).then_inc(var_ready, 1)
                dve.wait_ge(root, 2)
                self.refine_rsqrt(dve, link, rs, ms, tmp70)
                dve.tensor_scalar(rs, rs, 1.0, None, ALU.mult).then_inc(rs_ready, 1)
                dve.wait_ge(rs_ready, 1)
                for t in range(TILES):
                    n = rows(t)
                    q = pj[0:n, t, N_Q:N_Q + 512].rearrange("p (h d) -> p h d", d=HD)
                    link(dve.tensor_tensor(q, q, rsv[0:n, t, 0:8].unsqueeze(2).broadcast_to([n, 8, HD]), ALU.mult))
                    link(dve.tensor_tensor(q, q, self.gq[0:n].unsqueeze(1).broadcast_to([n, 8, HD]), ALU.mult))
                    self.rope(dve, link, q, 8, cosn[0:n, t, :].unsqueeze(1).broadcast_to([n, 8, 8]),
                              sinn[0:n, t, :].unsqueeze(1).broadcast_to([n, 8, 8]),
                              [z[0:n, 0:64].rearrange("p (h d) -> p h d", h=8) for z in tq], [n, 8])
                    dve.tensor_scalar(q, q, 1.0, None, ALU.mult).then_inc(q_ready, 1)
                dve.wait_ge(exps, TILES)
                for t in range(TILES):
                    n = rows(t)
                    dve.tensor_scalar(e_rg[0:n, t, :], e_rg[0:n, t, :], 1.0, None, ALU.add)
                    link(dve.tensor_scalar(self.gates[0:n, t, :], self.gates[0:n, t, :], 1.0, None, ALU.add))
                    dve.reciprocal(self.gates[0:n, t, :], self.gates[0:n, t, :])
                    link(dve.reciprocal(e_rg[0:n, t, :], e_rg[0:n, t, :]))
                    link(dve.tensor_tensor(pj[0:n, t, R_G:R_G + 256], pj[0:n, t, R_G:R_G + 256], e_rg[0:n, t, :],
                                           ALU.mult))

            @block.gpsimd
            def _(pool):
                link = self.linker(pool, "proj_pool_chain")
                cosn = self.c("cos_n").rearrange("p (t x) -> p t x", t=TILES)
                sinn = self.c("sin_n").rearrange("p (t x) -> p t x", t=TILES)
                pool.wait_ge(rs_ready, 1)
                for t in range(TILES):
                    n = rows(t)
                    for j in range(3):
                        kk = kview(t, n)[:, j]
                        r = rsv[0:n, t, 8 + 2 * j:10 + 2 * j].unsqueeze(2).broadcast_to([n, 2, HD])
                        link(pool.tensor_tensor(kk, kk, r, ALU.mult))
                        link(pool.tensor_tensor(kk, kk, self.gk[0:n, j].unsqueeze(1).broadcast_to([n, 2, HD]),
                                                ALU.mult))
                        self.rope(pool, link, kk, 8, cosn[0:n, t, :].unsqueeze(1).broadcast_to([n, 2, 8]),
                                  sinn[0:n, t, :].unsqueeze(1).broadcast_to([n, 2, 8]),
                                  [z[0:n, 0:16].rearrange("p (g d) -> p g d", g=2) for z in tk], [n, 2])
                    pool.tensor_copy(tk[0][0:n, 0:1], tk[1][0:n, 0:1]).then_inc(k_ready, 1)

    def store_heads(self, sp):
        o, l, pj = self.outs, self.l, self.proj
        lay = bass.ds(l, 1)
        for name, c0, w in (("sb_k", SB_K, 256), ("sb_v", SB_V, 256), ("cmp_k", C_K, P), ("cmp_v", C_V, P),
                            ("slc_k", S_K, P), ("slc_v", S_V, P), ("win_k", W_K, P), ("win_v", W_V, P)):
            dst = o["p_" + name][lay].rearrange("o b (t p) h d -> p (o b t) (h d)", p=P)
            sp.dma_start(dst, pj[:, 0:4, c0:c0 + w]).then_inc(self.outputs_done, 16)
            if name.startswith("win"):
                dst = o["s_" + name][lay, :, WIN - 1:WIN].rearrange("o b w h d -> (o b w) (h d)")
            else:
                dst = o["s_" + name][lay].rearrange("o b s h d -> (o b s) (h d)")
            sp.dma_start(dst, pj[0:NB, 4, c0:c0 + w]).then_inc(self.outputs_done, 16)

    def stick_breaking(self):
        nc, pj = self.nc, self.proj
        z_ready, abs_ready, ln_ready, l_ready = (self.sem(s) for s in ("sb_z", "sb_abs", "sb_ln", "sb_softplus"))
        e_ready, cum_ready, w_ready, pv_done = (self.sem(s) for s in ("sb_e", "sb_cum", "sb_w", "sb_pv"))
        lbuf = [self.xt[:, 0:PACKED], self.xt[:, PACKED:2 * PACKED]]
        wbuf = self.xt[:, 2 * PACKED:3 * PACKED]
        ebuf = [self.scr[:, 0:PACKED], self.scr[:, PACKED:2 * PACKED]]
        zb = lambda h: self.psf[:, (h % 2) * 1536:(h % 2) * 1536 + PACKED]

        with nc.Block() as block:
            @block.tensor
            def _(pe):
                for i in range(5):
                    if i < 4:
                        h, p0 = i, (i % 2) * HD
                        if h >= 2:
                            pe.wait_ge(w_ready, h - 1)
                        for jb in (0, 1, 3, 2):
                            n = SEQ - jb * P
                            ins = pe.matmul(zb(h)[:, PACK[jb]:PACK[jb] + n],
                                            self.tt[p0:p0 + HD, T_SBK + h // 2, jb * P:(jb + 1) * P],
                                            self.tt[p0:p0 + HD, T_SBQ + h // 2, jb * P:SEQ],
                                            start=(jb != 3), stop=True, skip_group_check=True)
                        ins.then_inc(z_ready, 1)
                    if i >= 1:
                        h = i - 1
                        pe.wait_ge(l_ready, h + 1)
                        for jb in range(4):
                            a = PACK[jb]
                            pe.matmul(zb(h)[:, a:a + P], self.ident_b[:], self.sb_neg_b[:], start=False, stop=True,
                                      skip_group_check=True)
                            ins = pe.matmul(zb(h)[:, a:a + SEQ - jb * P], self.c("neg_suffix"),
                                            lbuf[h % 2][:, a:a + SEQ - jb * P], start=False, stop=True,
                                            skip_group_check=True)
                            for j2 in range(jb + 1, 4):
                                n2 = SEQ - j2 * P
                                ins = pe.matmul(zb(h)[:, a + (j2 - jb) * P:a + SEQ - jb * P], self.c("neg_ones"),
                                                lbuf[h % 2][:, PACK[j2]:PACK[j2] + n2], start=False, stop=True,
                                                skip_group_check=True)
                        ins.then_inc(cum_ready, 1)
                        pe.wait_ge(w_ready, h + 1)
                        for qb in range(4):
                            for jb in range(qb + 1):
                                a = PACK[jb] + (qb - jb) * P
                                ins = pe.matmul(self.psf[:, 3072 + qb * 256 + h * HD:3072 + qb * 256 + (h + 1) * HD],
                                                wbuf[:, a:a + P], pj[:, jb, SB_V + h * HD:SB_V + (h + 1) * HD],
                                                start=(jb == 0), stop=(jb == qb), skip_group_check=True)
                        ins.then_inc(pv_done, 1)

            @block.vector
            def _(dve):
                link = self.linker(dve, "sb_dve_chain")

                for h in range(4):
                    dve.wait_ge(ln_ready, h + 1)
                    if h >= 2:
                        dve.wait_ge(cum_ready, h - 1)
                    link(dve.scalar_tensor_tensor(out=lbuf[h % 2], in0=zb(h), scalar=0.0, in1=ebuf[h % 2],
                                                  op0=ALU.max, op1=ALU.add))
                    for jb in range(4):
                        d = lbuf[h % 2][:, PACK[jb]:PACK[jb] + P]
                        ins = dve.tensor_tensor(d, d, self.c("sb_mask"), ALU.mult)
                    ins.then_inc(l_ready, 1)

            @block.scalar
            def _(act):
                def softplus_tail(h):
                    act.wait_ge(z_ready, h + 1)
                    if h >= 2:
                        act.wait_ge(l_ready, h - 1)
                    act.activation(ebuf[h % 2], zb(h), ACT.Abs).then_inc(abs_ready, 1)
                    act.wait_ge(abs_ready, h + 1)
                    act.activation(ebuf[h % 2], ebuf[h % 2], ACT.Exp, scale=-1.0).then_inc(e_ready, 1)
                    act.wait_ge(e_ready, h + 1)
                    act.activation(ebuf[h % 2], ebuf[h % 2], ACT.Ln, bias=1.0).then_inc(ln_ready, 1)

                softplus_tail(0)
                for h in range(4):
                    if h < 3:
                        softplus_tail(h + 1)
                    act.wait_ge(cum_ready, h + 1)
                    if h >= 1:
                        act.wait_ge(pv_done, h)
                    act.activation(wbuf, zb(h), ACT.Exp).then_inc(w_ready, 1)
                act.wait_ge(pv_done, 4)
                act.activation(pj[:, 0:4, SB_Q:SB_Q + 256],
                               self.psf[:, 3072:4096].rearrange("p (q n) -> p q n", q=4), ACT.Copy)

            @block.sync
            def _(sp):
                self.store_heads(sp)
                self.n_out = 16 * 16

    def retention(self):
        nc, pj, o = self.nc, self.proj, self.outs
        s_ready, copied, masked, pv_done = (self.sem(s) for s in ("ret_inner", "ret_copied", "ret_masked", "ret_pv"))
        st_mm, st_ready, var_ready, root = (self.sem(s) for s in ("ret_state_mm", "ret_state", "ret_var", "ret_root"))
        ibuf = [self.xt[:, 0:PACKED], self.xt[:, PACKED:2 * PACKED]]
        sq = self.xt[:, 2560:3584].rearrange("p (h d) -> p h d", d=HD)
        state = self.scr[0:HD, 0:256]
        mu, var, r, tmp = (self.small[:, 16 * i:16 * i + 16] for i in range(4))
        zb = lambda h: self.psf[:, (h % 2) * 1536:(h % 2) * 1536 + PACKED]
        with nc.Block() as block:
            @block.tensor
            def _(pe):
                for i in range(5):
                    if i < 4:
                        h, p0 = i, (i % 2) * HD
                        if h >= 2:
                            pe.wait_ge(copied, h - 1)
                        for jb in (0, 1, 3, 2):
                            n = SEQ - jb * P
                            ins = pe.matmul(zb(h)[:, PACK[jb]:PACK[jb] + n],
                                            self.tt[p0:p0 + HD, T_RK + h // 2, jb * P:(jb + 1) * P],
                                            self.tt[p0:p0 + HD, T_RQ + h // 2, jb * P:SEQ],
                                            start=(jb != 3), stop=True, skip_group_check=True)
                        ins.then_inc(s_ready, 1)
                    if i >= 1:
                        h = i - 1
                        pe.wait_ge(masked, h + 1)
                        for qb in range(4):
                            for jb in range(qb + 1):
                                a = PACK[jb] + (qb - jb) * P
                                ins = pe.matmul(self.psf[:, 3072 + qb * 256 + h * HD:3072 + qb * 256 + (h + 1) * HD],
                                                ibuf[h % 2][:, a:a + P], pj[:, jb, R_V + h * HD:R_V + (h + 1) * HD],
                                                start=(jb == 0), stop=(jb == qb), skip_group_check=True)
                        ins.then_inc(pv_done, 1)
                pe.wait_ge(copied, 4)
                for h in range(4):
                    for t in range(4):
                        ins = pe.matmul(self.ps[0:HD, 0, h * HD:(h + 1) * HD],
                                        pj[:, t, R_K + h * HD:R_K + (h + 1) * HD],
                                        pj[:, t, R_V + h * HD:R_V + (h + 1) * HD], start=(t == 0), stop=(t == 3),
                                        skip_group_check=True)
                ins.then_inc(st_mm, 1)

            @block.scalar
            def _(act):
                for h in range(4):
                    act.wait_ge(s_ready, h + 1)
                    if h >= 2:
                        act.wait_ge(pv_done, h - 1)
                    act.activation(ibuf[h % 2], zb(h), ACT.Copy).then_inc(copied, 1)
                act.wait_ge(var_ready, 1)
                act.activation(r, var, ACT.Ln).then_inc(root, 1)
                act.wait_ge(root, 1)
                act.activation(r, r, ACT.Exp, scale=-0.5).then_inc(root, 1)

            @block.vector
            def _(dve):
                link = self.linker(dve, "ret_dve_chain")
                for h in range(4):
                    dve.wait_ge(copied, h + 1)
                    for jb in range(4):
                        d = ibuf[h % 2][:, PACK[jb]:PACK[jb] + P]
                        ins = dve.tensor_tensor(d, d, self.c("ret_mask"), ALU.mult)
                    ins.then_inc(masked, 1)
                dve.wait_ge(pv_done, 4)
                acc = self.psf[:, 3072:4096].rearrange("p (h d) -> p h d", d=HD)
                link(dve.tensor_reduce(mu, acc, AXX, ALU.add))
                link(dve.tensor_scalar(mu, mu, 1.0 / HD, None, ALU.mult))
                link(dve.tensor_tensor(sq, acc, mu.unsqueeze(2).broadcast_to([P, 16, HD]), ALU.subtract))
                xc = pj[:, 0:4, R_Q:R_Q + 256].rearrange("p t (h d) -> p t h d", h=4)
                link(dve.tensor_copy(xc, sq.rearrange("p (t h) d -> p t h d", t=4)))
                link(dve.tensor_tensor(sq, sq, sq, ALU.mult))
                link(dve.tensor_reduce(var, sq, AXX, ALU.add))
                dve.tensor_scalar(var, var, 1.0 / HD, EPS, ALU.mult, ALU.add).then_inc(var_ready, 1)
                dve.wait_ge(st_mm, 1)
                dve.tensor_tensor(state.rearrange("p (h e) -> p h e", h=4),
                                  self.ps[0:HD, 0, 0:256].rearrange("p (h e) -> p h e", h=4),
                                  self.c("gam_last")[0:HD].unsqueeze(2).broadcast_to([HD, 4, HD]), ALU.mult
                                  ).then_inc(st_ready, 1)
                dve.wait_ge(root, 2)
                self.refine_rsqrt(dve, link, r, var, tmp)
                link(dve.tensor_tensor(xc, xc, r.rearrange("p (t h) -> p t h", t=4).unsqueeze(3).broadcast_to(
                    [P, 4, 4, HD]), ALU.mult))
                link(dve.tensor_tensor(pj[:, 0:4, R_Q:R_Q + 256], pj[:, 0:4, R_Q:R_Q + 256],
                                       pj[:, 0:4, R_G:R_G + 256], ALU.mult))

            @block.sync
            def _(sp):
                sp.wait_ge(st_ready, 1)
                dst = o["p_ret"][bass.ds(self.l, 1)].rearrange("o b h d e -> d (o b h) e")
                sp.dma_start(dst, state.rearrange("p (h e) -> p h e", h=4)).then_inc(self.outputs_done, 16)
                self.n_out += 16
                sp.wait_ge(self.outputs_done, self.n_out)

    def compress_prompt(self):
        nc, pj = self.nc, self.proj
        weighted, pooled, p_copied, mapped = (self.sem(s) for s in ("cp_weighted", "cp_pooled", "cp_copied",
                                                                    "cp_mapped"))
        kw = self.xt[:, 0:1024].rearrange("p (i n) -> p i n", i=8)
        pl = self.small[:, 0:32]
        self.kcmp_t = self.scr[:, 3168:3184]
        self.vcmp = self.scr[0:16, 3040:3168]
        with nc.Block() as block:
            @block.vector
            def _(dve):
                for i in range(8):
                    kv, t = divmod(i, 4)
                    src = pj[:, t, (C_K, C_V)[kv]:(C_K, C_V)[kv] + P].rearrange("p (g d) -> p g d", g=2)
                    pos = (self.pos_k, self.pos_v)[kv][:].unsqueeze(1).broadcast_to([P, 2, HD])
                    ins = dve.tensor_tensor(kw[:, i, :].rearrange("p (g d) -> p g d", g=2), src, pos, ALU.mult)
                ins.then_inc(weighted, 1)
                dve.wait_ge(pooled, 1)
                dve.tensor_copy(pl, self.ps[:, 0, 0:32]).then_inc(p_copied, 1)
                dve.wait_ge(mapped, 1)
                dve.tensor_copy(self.kcmp_t, self.ps[:, 1, 0:16])
                dve.tensor_copy(self.vcmp, self.ps[0:16, 2, 0:P])

            @block.tensor
            def _(pe):
                pe.wait_ge(weighted, 1)
                for i in range(8):
                    ins = pe.matmul(self.ps[:, 0, 4 * i:4 * i + 4], kw[:, i, :], self.c("blk_ind"), start=True,
                                    stop=True, skip_group_check=True)
                ins.then_inc(pooled, 1)
                pe.wait_ge(p_copied, 1)
                pe.matmul(self.ps[:, 1, 0:16], self.phi_k[:], pl[:, 0:16], start=True, stop=True)
                pe.matmul(self.ps[0:16, 2, 0:P], pl[:, 16:32], self.phi_v[:], start=True, stop=True
                          ).then_inc(mapped, 1)

    def nsa_prompt(self):
        nc, pj = self.nc, self.proj
        qk_done, nmax_ready, exp_done, turned = (self.sem(s) for s in ("ns_qk", "ns_negmax", "ns_exp", "ns_turned"))
        copied = [self.sem("ns_copied0"), self.sem("ns_copied1")]
        pv_done, o_read = self.sem("ns_pv"), self.sem("ns_o_read")
        prob = [self.xt[:, 0:1024].rearrange("p (i n) -> p i n", i=2),
                self.xt[:, 1024:2048].rearrange("p (i n) -> p i n", i=2)]
        pt = [self.xt[:, 2048:2560], self.xt[:, 2560:3072]]
        otmp = self.xt[:, 3072:3584]
        nmax = [self.small[:, 0:2], self.small[:, 2:4]]
        rsum = [self.small[:, 8:16], self.small[:, 16:24]]
        wgt = self.small[:, 24:32]
        units = [(qt, br, g, pr) for qt in range(4) for br in range(3) for g in range(2) for pr in range(2)]
        U = len(units)
        nkeys = lambda qt, br: 16 if br == 0 else (qt + 1) * P
        nblk = lambda qt, br: 1 if br == 0 else qt + 1

        with nc.Block() as block:
            @block.tensor
            def _(pe):
                for u in range(U + 1):
                    if u < U:
                        qt, br, g, pr = units[u]
                        nk = nkeys(qt, br)
                        if u >= 2:
                            pe.wait_ge(exp_done, 2 * u - 2)
                        for i in range(2):
                            s = self.ps[:, 2 * (u % 2) + i, :]
                            if br == 0:
                                mask = self.cmp_neg_b[:, qt * 16:qt * 16 + 16]
                                keys = self.kcmp_t[g * HD:(g + 1) * HD, :]
                            else:
                                mask = self.nsa_neg_b[:]
                                keys = self.tt[g * HD:(g + 1) * HD, (T_SK, T_WK)[br - 1], 0:nk]
                            m0 = nk - mask.shape[1]
                            pe.matmul(s[:, m0:nk], self.ident_b[:], mask, start=True, stop=True,
                                      skip_group_check=True)
                            ins = pe.matmul(s[:, 0:nk],
                                            self.tt[g * HD:(g + 1) * HD, T_NQ + 2 * pr + i, qt * P:(qt + 1) * P],
                                            keys, start=False, stop=True, skip_group_check=True)
                        ins.then_inc(qk_done, 1)
                    if u >= 1:
                        w = u - 1
                        qt, br, g, pr = units[w]
                        for i in range(2):
                            pe.wait_ge(exp_done, 2 * w + i + 1)
                            if w >= 1:
                                pe.wait_ge(copied[i], w)
                            for b in range(nblk(qt, br)):
                                k = 16 if br == 0 else P
                                ins = pe.transpose(self.ps[0:k, 4 + i, b * P:(b + 1) * P],
                                                   prob[w % 2][:, i, b * P:b * P + k], self.c("ident"))
                            ins.then_inc(turned, 1)
                        for i in range(2):
                            h = 4 * g + 2 * pr + i
                            grp = w // 4
                            pe.wait_ge(copied[i], w + 1)
                            if w % 4 == 0 and i == 0 and grp >= 2:
                                pe.wait_ge(o_read, grp - 1)
                            out = self.ps[:, 6 + grp % 2, h * HD:(h + 1) * HD]
                            if br == 0:
                                ins = pe.matmul(out, pt[i][0:16, 0:P], self.vcmp[:, g * HD:(g + 1) * HD], start=True,
                                                stop=True, skip_group_check=True)
                            else:
                                v0 = (S_V, W_V)[br - 1] + g * HD
                                for b in range(qt + 1):
                                    ins = pe.matmul(out, pt[i][:, b * P:(b + 1) * P], pj[:, b, v0:v0 + HD],
                                                    start=(b == 0), stop=(b == qt), skip_group_check=True)
                            ins.then_inc(pv_done, 1)

            def copy_probs(eng, w, i):
                qt, br, _, _ = units[w]
                eng.wait_ge(turned, 2 * w + i + 1)
                if w >= 1:
                    eng.wait_ge(pv_done, 2 * (w - 1) + i + 1)
                k, n = (16, P) if br == 0 else (P, (qt + 1) * P)
                if i == 0:
                    eng.tensor_copy(pt[i][0:k, 0:n], self.ps[0:k, 4 + i, 0:n]).then_inc(copied[i], 1)
                else:
                    eng.activation(pt[i][0:k, 0:n], self.ps[0:k, 4 + i, 0:n], ACT.Copy).then_inc(copied[i], 1)

            @block.scalar
            def _(act):
                for u in range(U + 1):
                    if u < U:
                        qt, br, g, pr = units[u]
                        nk = nkeys(qt, br)
                        act.wait_ge(nmax_ready, u + 1)
                        if u >= 2:
                            act.wait_ge(turned, 2 * (u - 1))
                        grp = u // 4
                        if u % 4 == 0 and grp >= 2:
                            act.wait_ge(o_read, grp - 1)
                        for i in range(2):
                            h = 4 * g + 2 * pr + i
                            act.activation(prob[u % 2][:, i, 0:nk], self.ps[:, 2 * (u % 2) + i, 0:nk], ACT.Exp,
                                           bias=nmax[u % 2][:, i:i + 1],
                                           accum_out=rsum[grp % 2][:, h:h + 1]).then_inc(exp_done, 1)
                    if u >= 1:
                        copy_probs(act, u - 1, 1)

            @block.vector
            def _(dve):
                link = self.linker(dve, "ns_dve_chain")
                for u in range(U + 1):
                    if u < U:
                        qt, br, g, pr = units[u]
                        nk = nkeys(qt, br)
                        dve.wait_ge(qk_done, u + 1)
                        if u >= 2:
                            dve.wait_ge(exp_done, 2 * u - 2)
                        link(dve.tensor_reduce(nmax[u % 2], self.ps[:, 2 * (u % 2):2 * (u % 2) + 2, 0:nk], AXX,
                                               ALU.max))
                        dve.tensor_scalar(nmax[u % 2], nmax[u % 2], -1.0, None, ALU.mult).then_inc(nmax_ready, 1)
                    if u >= 1:
                        w = u - 1
                        copy_probs(dve, w, 0)
                        if w % 4 == 3:
                            qt, br, _, _ = units[w]
                            grp = w // 4
                            gate = self.gates[:, qt, :].rearrange("p (h c) -> p h c", c=3)[:, :, br]
                            dve.wait_ge(exp_done, 2 * w + 2)
                            link(dve.reciprocal(wgt, rsum[grp % 2]))
                            if br == 0 and qt == 0:
                                link(dve.tensor_scalar(wgt, wgt, self.c("cmp_any"), None, ALU.mult))
                            link(dve.tensor_tensor(wgt, wgt, gate, ALU.mult))
                            dve.wait_ge(pv_done, 2 * (w + 1))
                            acc = pj[:, qt, N_Q:N_Q + 512].rearrange("p (r g d) -> p g r d", r=4, g=2)
                            src = self.ps[:, 6 + grp % 2, :].rearrange("p (g r d) -> p g r d", g=2, r=4)
                            wb = wgt.rearrange("p (g r) -> p g r", g=2).unsqueeze(3).broadcast_to([P, 2, 4, HD])
                            ot = otmp.rearrange("p (g r d) -> p g r d", g=2, r=4)
                            if br == 0:
                                ins = dve.tensor_tensor(acc, src, wb, ALU.mult)
                                link(ins)
                            else:
                                link(dve.tensor_tensor(ot, src, wb, ALU.mult))
                                link(dve.tensor_tensor(acc, acc, ot, ALU.add))
                            dve.tensor_copy(otmp[:, 0:1], wgt[:, 0:1]).then_inc(o_read, 1)
                            dve.wait_ge(o_read, grp + 1)

    def retention_sample(self):
        nc, pj, o, a, l = self.nc, self.proj, self.outs, self.ins, self.l
        lay = bass.ds(l, 1)
        built, v_stored, v_read, st_new, o_mm, o_copied, o_stored, o_read, var_ready, root = (
            self.sem(s) for s in ("rs_queries", "rs_v_stored", "rs_v_read", "rs_state", "rs_mm", "rs_copied",
                                  "rs_o_stored", "rs_o_read", "rs_var", "rs_root"))
        st = self.xt[:, 0:1024].rearrange("p (b x e) -> p b x e", b=NB, x=2)
        vb = self.xt[:, 1024:2048].rearrange("p (b x e) -> p b x e", b=NB, x=2)
        osb = self.scr[0:32, 0:HD]
        orow = self.scr[0:NB, 128:384]
        sq = self.scr[0:NB, 384:640]
        mu, var, r, tmp = (self.small[0:NB, 4 * i:4 * i + 4] for i in range(4))
        s_v = self.nc.dram_tensor("scratch_ret_v", [NB, 256], F32, kind="Internal").ap()
        s_o = self.nc.dram_tensor("scratch_ret_o", [32, HD], F32, kind="Internal").ap()
        s_g = self.nc.dram_tensor("scratch_gates", [NB, 24], F32, kind="Internal").ap()
        self.s_g = s_g
        with nc.Block() as block:
            @block.sync
            def _(sp):
                src = a["state_ret"][lay].rearrange("o b (x h) d e -> (h d) (o b) x e", h=2)
                for x in range(2):
                    sp.dma_start(st[:, :, x, :], src[:, :, x, :]).then_inc(self.ret_state_in, 16)
                sp.dma_start(s_v, pj[0:NB, 4, R_V:R_V + 256]).then_inc(v_stored, 16)
                sp.dma_start(s_g, self.gates[0:NB, 4, :]).then_inc(v_stored, 16)
                sp.wait_ge(v_stored, 32)
                for h in range(2):
                    src = s_v.rearrange("b (x h e) -> h (b x) e", x=2, h=2)[h]
                    sp.dma_start(self.xt[h * HD:(h + 1) * HD, 1024:2048].rearrange("p (y e) -> p y e", e=HD),
                                 src.partition_broadcast(HD)).then_inc(v_read, 16)
                sp.wait_ge(st_new, 1)
                dst = o["s_ret"][lay].rearrange("o b (x h) d e -> (h d) (o b) x e", h=2)
                for x in range(2):
                    sp.dma_start(dst[:, :, x, :], st[:, :, x, :]).then_inc(self.outputs_done, 16)
                    self.n_out += 16
                sp.wait_ge(o_copied, 1)
                sp.dma_start(s_o, osb).then_inc(o_stored, 16)
                sp.wait_ge(o_stored, 16)
                sp.dma_start(orow, s_o.rearrange("(b h) d -> b (h d)", b=NB)).then_inc(o_read, 16)
                sp.wait_ge(o_read, 16)
                sp.wait_ge(self.outputs_done, self.n_out)

            @block.gpsimd
            def _(pool):
                for g in range(2):
                    p = slice(g * HD, (g + 1) * HD)
                    dst = self.q_nsa[p, :].rearrange("p (b x) -> p b x", x=72)[:, :, g * 4:g * 4 + 4]
                    pool.tensor_copy(dst, self.tt[p, T_NQ:T_NQ + 4, SEQ:TOK].rearrange("p r b -> p b r"))
                    for buf, blk in ((self.q_sb, T_SBQ), (self.q_ret, T_RQ)):
                        for x in range(2):
                            dst = buf[p, x * 256:x * 256 + 288].rearrange("p (b y) -> p b y", y=36)[:, :, 2 * x + g]
                            ins = pool.tensor_copy(dst, self.tt[p, blk + x, SEQ:TOK])
                ins.then_inc(built, 1)

            @block.vector
            def _(dve):
                link = self.linker(dve, "rs_dve_chain")
                dve.wait_ge(v_read, 32)
                kt = self.tt[:, T_RK:T_RK + 2, SEQ:TOK].rearrange("p x b -> p b x").unsqueeze(3).broadcast_to(
                    [P, NB, 2, HD])
                link(dve.tensor_tensor(vb, vb, kt, ALU.mult))
                dve.wait_ge(self.ret_state_in, 32)
                for x in range(2):
                    ins = dve.scalar_tensor_tensor(out=st[:, :, x, :], in0=st[:, :, x, :],
                                                   scalar=self.c("gam_one")[:, x:x + 1], in1=vb[:, :, x, :],
                                                   op0=ALU.mult, op1=ALU.add)
                ins.then_inc(st_new, 1)
                dve.wait_ge(o_mm, 1)
                dve.tensor_copy(osb, self.ps[0:32, 0, 0:HD]).then_inc(o_copied, 1)
                dve.wait_ge(o_read, 16)
                ov = orow.rearrange("p (h d) -> p h d", h=4)
                sv = sq.rearrange("p (h d) -> p h d", h=4)
                link(dve.tensor_reduce(mu, ov, AXX, ALU.add))
                link(dve.tensor_scalar(mu, mu, 1.0 / HD, None, ALU.mult))
                link(dve.tensor_tensor(ov, ov, mu.unsqueeze(2).broadcast_to([NB, 4, HD]), ALU.subtract))
                link(dve.tensor_tensor(sq, orow, orow, ALU.mult))
                link(dve.tensor_reduce(var, sv, AXX, ALU.add))
                dve.tensor_scalar(var, var, 1.0 / HD, EPS, ALU.mult, ALU.add).then_inc(var_ready, 1)
                dve.wait_ge(root, 2)
                self.refine_rsqrt(dve, link, r, var, tmp)
                link(dve.tensor_tensor(ov, ov, r.unsqueeze(2).broadcast_to([NB, 4, HD]), ALU.mult))
                link(dve.tensor_tensor(pj[0:NB, 4, R_Q:R_Q + 256], orow, pj[0:NB, 4, R_G:R_G + 256], ALU.mult))

            @block.scalar
            def _(act):
                act.wait_ge(var_ready, 1)
                act.activation(r, var, ACT.Ln).then_inc(root, 1)
                act.wait_ge(root, 1)
                act.activation(r, r, ACT.Exp, scale=-0.5).then_inc(root, 1)

            @block.tensor
            def _(pe):
                pe.wait_ge(built, 1)
                pe.wait_ge(st_new, 1)
                for b in range(NB):
                    for x in range(2):
                        ins = pe.matmul(self.ps[0:32, 0, 0:HD], self.q_ret[:, x * 256 + b * 32:x * 256 + b * 32 + 32],
                                        st[:, b, x, :], start=(b == 0 and x == 0), stop=(b == NB - 1 and x == 1))
                ins.then_inc(o_mm, 1)

    def sample_scores(self):
        nc, l = self.nc, self.l
        turned, scored, item_done = self.sem("sk_turned"), self.sem("sk_scored"), self.sem("sk_item_done")
        copied = [self.sem("sk_copied_dve"), self.sem("sk_copied_act")]
        weighted, pooled, p_copied, k_mapped, k_copied = (
            self.sem(s) for s in ("sk_weighted", "sk_pooled", "sk_pool_copied", "sk_mapped", "sk_map_copied"))
        for i in range(IT_KW, IT_VW):
            self.freed[i] = (item_done, i - IT_KW + 1)
        kt = [self.scr[:, 0:512], self.scr[:, 512:1024]]
        kw = self.scr[:, 1024:2048]
        plk = self.scr[:, 2048:2304]
        kct = self.scr[:, 2304:2560]
        units = []
        for b in range(NB):
            s = self.slot(IT_KW)
            units.append((IT_KW, self.ps[0:64, 4, :], self.q_nsa[:, b * 64:b * 64 + 64], b == 0, b == NB - 1,
                          [s[:, (b * 4 + j) * P:(b * 4 + j + 1) * P] for j in range(4)], b == NB - 1, None))
        for b in range(NB):
            s = self.slot(IT_K + b)
            for half in range(2):
                for x in range(2):
                    units.append((IT_K + b, self.ps[0:32, half, :],
                                  self.q_sb[:, x * 256 + b * 32:x * 256 + b * 32 + 32], b == 0 and x == 0,
                                  b == NB - 1 and x == 1,
                                  [s[:, (4 * half + j) * 256 + x * P:(4 * half + j) * 256 + (x + 1) * P]
                                   for j in range(4)], False, None))
            for half in range(2):
                units.append((IT_K + b, self.ps[0:64, 2 + half, :], self.q_nsa[:, b * 64:b * 64 + 64], b == 0,
                              b == NB - 1,
                              [s[:, 2048 + (4 * half + j) * P:2048 + (4 * half + j + 1) * P] for j in range(4)],
                              False, b if half == 1 else None))
        U = len(units)
        with nc.Block() as block:
            @block.sync
            def _(sp):
                self.issue_until(sp, l, IT_VW + SLOTS)

            @block.tensor
            def _(pe):
                for u in range(U + 1):
                    if u < U:
                        item, _, _, _, _, pieces, last_read, pool_b = units[u]
                        s, v = self.item_ready(item)
                        pe.wait_ge(s, v)
                        if u >= 2:
                            pe.wait_ge(copied[u % 2], u // 2)
                        for j, piece in enumerate(pieces):
                            ins = pe.transpose(self.ps[:, 6 + u % 2, j * P:(j + 1) * P], piece, self.c("ident"))
                        ins.then_inc(turned, 1)
                        if last_read:
                            pe.wait_ge(turned, u + 1)
                            pe.matmul(self.ps[0:4, 5, 508:512], self.c("ident")[:, 0:4], self.c("ident")[:, 0:4],
                                      start=True, stop=True, skip_group_check=True).then_inc(item_done, 1)
                    if u >= 1:
                        w = u - 1
                        _, out, q, first, last, _, _, pool_b = units[w]
                        pe.wait_ge(copied[w % 2], w // 2 + 1)
                        pe.matmul(out, q, kt[w % 2], start=first, stop=last, skip_group_check=True
                                  ).then_inc(scored, 1)
                        if pool_b is not None:
                            pe.wait_ge(weighted, pool_b + 1)
                            for j in range(NPAGE):
                                c0 = 128 + pool_b * 32 + j * 4
                                ins = pe.matmul(self.ps[:, 5, c0:c0 + 4], kw[:, j * P:(j + 1) * P],
                                                self.c("blk_ind"), start=True, stop=True, skip_group_check=True)
                            ins.then_inc(item_done, 1)
                pe.wait_ge(p_copied, 1)
                pe.matmul(self.ps[:, 6, 0:256], self.phi_k[:], plk, start=True, stop=True,
                          skip_group_check=True).then_inc(k_mapped, 1)
                pe.wait_ge(k_copied, 1)
                for b in range(NB):
                    pe.matmul(self.ps[0:64, 5, 0:32], self.q_nsa[:, b * 64:b * 64 + 64], kct[:, b * 32:b * 32 + 32],
                              start=(b == 0), stop=(b == NB - 1), skip_group_check=True)
                for j, blk in enumerate((T_SK, T_WK)):
                    for b in range(NB):
                        pe.matmul(self.ps[0:64, 5, 32 + j:33 + j], self.q_nsa[:, b * 64:b * 64 + 64],
                                  self.tt[:, blk, SEQ + b:SEQ + b + 1], start=(b == 0), stop=(b == NB - 1),
                                  skip_group_check=True)

            @block.vector
            def _(dve):
                for u in range(0, U, 2):
                    dve.wait_ge(turned, u + 1)
                    if u >= 2:
                        dve.wait_ge(scored, u - 1)
                    dve.tensor_copy(kt[0], self.ps[:, 6, :]).then_inc(copied[0], 1)
                dve.wait_ge(item_done, 1 + NB)
                dve.tensor_copy(plk, self.ps[:, 5, 128:384]).then_inc(p_copied, 1)
                dve.wait_ge(k_mapped, 1)
                dve.tensor_copy(kct, self.ps[:, 6, 0:256]).then_inc(k_copied, 1)

            @block.scalar
            def _(act):
                for u in range(1, U, 2):
                    act.wait_ge(turned, u + 1)
                    if u >= 3:
                        act.wait_ge(scored, u - 1)
                    act.activation(kt[1], self.ps[:, 7, :], ACT.Copy).then_inc(copied[1], 1)

            @block.gpsimd
            def _(pool):
                for b in range(NB):
                    s, v = self.item_ready(IT_K + b)
                    pool.wait_ge(s, v)
                    if b >= 1:
                        pool.wait_ge(item_done, 1 + b)
                    pool.tensor_tensor(kw.rearrange("p (y d) -> p y d", d=HD),
                                       self.slot(IT_K + b)[:, 3072:4096].rearrange("p (y d) -> p y d", d=HD),
                                       self.pos_k[:].unsqueeze(1).broadcast_to([P, 16, HD]), ALU.mult
                                       ).then_inc(weighted, 1)

    def sample_softmax(self):
        nc = self.nc
        gates_in = self.sem("sx_gates")
        cmax, cexp, c_norm, imp_mm = (self.sem(s) for s in ("sx_cmp_max", "sx_cmp_exp", "sx_cmp_norm", "sx_imp"))
        w_max, w_exp, s_max, s_exp = (self.sem(s) for s in ("sx_win_max", "sx_win_exp", "sx_slc_max", "sx_slc_exp"))
        z_copied, z_turned, abs_r, e_r, ln_r, l_r, cum_r = (
            self.sem(s) for s in ("sx_z_copied", "sx_z_turned", "sx_abs", "sx_e", "sx_ln", "sx_softplus", "sx_cum"))
        p_ready, pt_done = self.sem("sx_probs"), self.sem("sx_turned")
        act_chain = self.sem("sx_act_chain")
        R = 64
        s_slc, s_win = self.psf[0:R, 1024:2048], self.ps[0:R, 4, :]
        few = self.xt[0:R, 2944:2978]
        s_cmp, s_new = few[:, 0:32], few[:, 32:34]
        pslc = self.xt[0:R, 0:1025]
        pwin = self.xt[0:R, 1088:1601]
        zrow = self.xt[0:32, 1664:2688]
        pen = self.xt[0:R, 2688:2704]
        pcmp = self.xt[0:R, 2720:2752]
        imp = self.xt[0:R, 2752:2768]
        t16 = self.xt[0:R, 2768:2784]
        d_slc, d_win = self.xt[0:R, 2816:2880], self.xt[0:R, 2880:2944]
        lsb = self.xt[:, 3072:3328]
        esb = self.xt[:, 3328:3584]
        sm = lambda i: self.small[0:R, i:i + 1]
        self.pt_slc = self.scr[:, 0:512]
        self.pt_win = self.scr[:, 512:768]
        self.pt_cmp = self.scr[0:32, 768:832]
        self.p_new = self.scr[0:NB, 832:960]
        self.w_sb = self.scr[:, 960:1216]
        gt = self.small[0:R, 20:23]
        with nc.Block() as block:
            @block.sync
            def _(sp):
                with nc.allow_non_contiguous_dma("sample gates"):
                    sp.dma_start(gt, self.s_g.rearrange("b (h c) -> (b h) c", c=3)).then_inc(gates_in, 16)
                sp.wait_ge(gates_in, 16)

            @block.vector
            def _(dve):
                link = self.linker(dve, "sx_dve_chain")
                link(dve.tensor_copy(few, self.ps[0:R, 5, 0:34]))
                link(dve.tensor_reduce(sm(0), s_cmp, AXX, ALU.max))
                dve.tensor_scalar(sm(1), sm(0), -1.0, None, ALU.mult).then_inc(cmax, 1)
                link(dve.tensor_reduce(sm(2), s_win, AXX, ALU.max))
                link(dve.tensor_tensor(sm(2), sm(2), s_new[:, 1:2], ALU.max))
                dve.tensor_scalar(sm(3), sm(2), -1.0, None, ALU.mult).then_inc(w_max, 1)
                dve.wait_ge(cexp, 1)
                link(dve.reciprocal(sm(4), sm(5)))
                link(dve.tensor_scalar(pcmp, pcmp, sm(4), None, ALU.mult))
                link(dve.tensor_reduce(t16, pcmp.rearrange("p (n c) -> p n c", c=2), AXX, ALU.add))
                dve.tensor_copy(imp, t16).then_inc(c_norm, 1)
                dve.wait_ge(gates_in, 16)
                dve.wait_ge(c_norm, 1)
                link(dve.tensor_scalar(pcmp, pcmp, gt[:, 0:1], None, ALU.mult))
                dve.wait_ge(imp_mm, 1)
                link(dve.tensor_copy(imp, self.ps[0:R, 6, 0:16]))
                link(dve.tensor_reduce(sm(6), imp[:, 1:16], AXX, ALU.min))
                link(dve.tensor_scalar(t16[:, 1:16], imp[:, 1:16], sm(6), None, ALU.is_le))
                link(dve.tensor_tensor(t16[:, 1:16], t16[:, 1:16], self.c("blk_idx")[0:R, 1:16], ALU.mult))
                link(dve.tensor_reduce(sm(7), t16[:, 1:16], AXX, ALU.max))
                link(dve.tensor_scalar(pen, self.c("blk_idx")[0:R], sm(7), NEG, ALU.is_equal, ALU.mult))
                link(dve.tensor_tensor(pslc[:, 0:1024].rearrange("p (n j) -> p n j", j=64),
                                       s_slc.rearrange("p (n j) -> p n j", j=64),
                                       pen.unsqueeze(2).broadcast_to([R, 16, 64]), ALU.add))
                link(dve.tensor_copy(pslc[:, 1024:1025], s_new[:, 0:1]))
                link(dve.tensor_reduce(sm(8), pslc, AXX, ALU.max))
                dve.tensor_scalar(sm(9), sm(8), -1.0, None, ALU.mult).then_inc(s_max, 1)
                dve.wait_ge(ln_r, 1)
                dve.scalar_tensor_tensor(out=lsb, in0=self.ps[:, 7, 0:256], scalar=0.0, in1=esb, op0=ALU.max,
                                         op1=ALU.add).then_inc(l_r, 1)
                dve.wait_ge(w_exp, 2)
                link(dve.tensor_tensor(sm(10), sm(11), sm(12), ALU.add))
                link(dve.reciprocal(sm(10), sm(10)))
                link(dve.tensor_tensor(sm(10), sm(10), gt[:, 2:3], ALU.mult))
                link(dve.tensor_scalar(pwin, pwin, sm(10), None, ALU.mult))
                dve.wait_ge(s_exp, 1)
                link(dve.reciprocal(sm(13), sm(14)))
                link(dve.tensor_tensor(sm(13), sm(13), gt[:, 1:2], ALU.mult))
                link(dve.tensor_scalar(pslc, pslc, sm(13), None, ALU.mult))
                dve.tensor_scalar(d_slc, self.c("ident")[0:R, 0:R], pslc[:, 1024:1025], None, ALU.mult)
                dve.tensor_scalar(d_win, self.c("ident")[0:R, 0:R], pwin[:, 512:513], None, ALU.mult
                                  ).then_inc(p_ready, 1)
                dve.wait_ge(pt_done, 1)
                dve.tensor_copy(self.pt_slc, self.ps[:, 0, :])
                dve.tensor_copy(self.pt_win, self.ps[:, 1, 0:256])
                dve.tensor_copy(self.pt_cmp, self.ps[0:32, 2, 0:R])
                dve.tensor_copy(self.p_new, self.ps[0:NB, 3, 0:128])

            @block.scalar
            def _(act):
                act.activation(zrow, self.psf[0:32, 0:1024], ACT.Copy).then_inc(z_copied, 1)
                act.wait_ge(cmax, 1)
                act.activation(pcmp, s_cmp, ACT.Exp, bias=sm(1), accum_out=sm(5)).then_inc(cexp, 1)
                act.wait_ge(w_max, 1)
                act.activation(pwin[:, 0:512], s_win, ACT.Exp, bias=sm(3), accum_out=sm(11)).then_inc(w_exp, 1)
                act.activation(pwin[:, 512:513], s_new[:, 1:2], ACT.Exp, bias=sm(3), accum_out=sm(12)
                               ).then_inc(w_exp, 1)
                act.wait_ge(s_max, 1)
                act.activation(pslc, pslc, ACT.Exp, bias=sm(9), accum_out=sm(14)).then_inc(s_exp, 1)
                act.wait_ge(z_turned, 1)
                act.activation(esb, self.ps[:, 7, 0:256], ACT.Abs).then_inc(abs_r, 1)
                act.wait_ge(abs_r, 1)
                act.activation(esb, esb, ACT.Exp, scale=-1.0).then_inc(e_r, 1)
                act.wait_ge(e_r, 1)
                act.activation(esb, esb, ACT.Ln, bias=1.0).then_inc(ln_r, 1)
                act.wait_ge(cum_r, 1)
                act.activation(self.w_sb, self.ps[:, 7, 0:256], ACT.Exp)

            @block.tensor
            def _(pe):
                ident = self.c("ident")
                pe.wait_ge(z_copied, 1)
                for j in range(NPAGE):
                    ins = pe.transpose(self.ps[:, 7, j * 32:(j + 1) * 32], zrow[:, j * P:(j + 1) * P],
                                       ident[0:32, 0:32])
                ins.then_inc(z_turned, 1)
                pe.wait_ge(c_norm, 1)
                pe.matmul(self.ps[0:R, 6, 0:16], self.c("grp")[0:R], imp, start=True, stop=True
                          ).then_inc(imp_mm, 1)
                pe.wait_ge(l_r, 1)
                pe.matmul(self.ps[:, 7, 0:256], self.c("neg_suffix"), lsb, start=False, stop=True,
                          skip_group_check=True)
                for j in range(1, NPAGE):
                    ins = pe.matmul(self.ps[:, 7, 0:j * 32], self.c("neg_ones"),
                                    lsb[:, j * 32:(j + 1) * 32].unsqueeze(1).broadcast_to([P, j, 32]), start=False,
                                    stop=True, skip_group_check=True)
                ins.then_inc(cum_r, 1)
                pe.wait_ge(p_ready, 1)
                for j in range(NPAGE):
                    pe.transpose(self.ps[:, 0, j * R:(j + 1) * R], pslc[:, j * P:(j + 1) * P], ident[0:R, 0:R])
                for j in range(4):
                    pe.transpose(self.ps[:, 1, j * R:(j + 1) * R], pwin[:, j * P:(j + 1) * P], ident[0:R, 0:R])
                pe.transpose(self.ps[0:32, 2, 0:R], pcmp, ident[0:R, 0:R])
                for j, dg in enumerate((d_slc, d_win)):
                    ins = pe.matmul(self.ps[0:NB, 3, j * R:(j + 1) * R], self.c("seq_ind")[0:R], dg, start=True,
                                    stop=True, skip_group_check=True)
                ins.then_inc(pt_done, 1)

    def sample_values(self):
        nc, l, pj = self.nc, self.l, self.proj
        item_done, weighted, pooled, p_copied, mapped, m_copied, all_done = (
            self.sem(s) for s in ("sv_item_done", "sv_weighted", "sv_pooled", "sv_pool_copied", "sv_mapped",
                                  "sv_map_copied", "sv_all_done"))
        for i in range(IT_VW, IT_WO):
            self.freed[i] = (item_done, i - IT_VW + 1)
        kw = self.scr[:, 1216:2240]
        plv = self.scr[:, 2240:2272]
        vc = self.scr[0:32, 2272:2400]
        on = self.ps[:, 0, 0:64]
        with nc.Block() as block:
            @block.sync
            def _(sp):
                self.issue_until(sp, l, IT_WO + SLOTS)

            @block.tensor
            def _(pe):
                pe.matmul(on, pj[0:NB, 4, S_V:S_V + P], self.p_new[:, 0:64], start=True, stop=False,
                          skip_group_check=True)
                pe.matmul(on, pj[0:NB, 4, W_V:W_V + P], self.p_new[:, 64:128], start=False, stop=False,
                          skip_group_check=True)
                s, v = self.item_ready(IT_VW)
                pe.wait_ge(s, v)
                w = self.slot(IT_VW)
                for b in range(NB):
                    for j in range(4):
                        ins = pe.matmul(on[:, b * 8:b * 8 + 8], w[:, (b * 4 + j) * P:(b * 4 + j + 1) * P],
                                        self.pt_win[:, j * 64 + b * 8:j * 64 + b * 8 + 8], start=False, stop=False,
                                        skip_group_check=True)
                ins.then_inc(item_done, 1)
                for b in range(NB):
                    s, v = self.item_ready(IT_V + b)
                    pe.wait_ge(s, v)
                    w = self.slot(IT_V + b)
                    pe.wait_ge(weighted, b + 1)
                    for j in range(NPAGE):
                        ins = pe.matmul(self.ps[:, 2, j * 4:j * 4 + 4], kw[:, j * P:(j + 1) * P],
                                        self.c("blk_ind"), start=True, stop=True, skip_group_check=True)
                    ins.then_inc(pooled, 1)
                    for x in range(2):
                        for j in range(NPAGE):
                            pe.matmul(self.ps[:, 1, x * 32 + b * 4:x * 32 + b * 4 + 4],
                                      w[:, j * 256 + x * P:j * 256 + (x + 1) * P],
                                      self.w_sb[:, j * 32 + b * 4:j * 32 + b * 4 + 4], start=(j == 0),
                                      stop=(j == NPAGE - 1), skip_group_check=True)
                    pe.wait_ge(p_copied, b + 1)
                    pe.matmul(self.ps[0:32, 3, 0:P], plv, self.phi_v[:], start=True, stop=True,
                              skip_group_check=True).then_inc(mapped, 1)
                    for j in range(NPAGE):
                        ins = pe.matmul(on[:, b * 8:b * 8 + 8], w[:, 2048 + j * P:2048 + (j + 1) * P],
                                        self.pt_slc[:, j * 64 + b * 8:j * 64 + b * 8 + 8], start=False, stop=False,
                                        skip_group_check=True)
                    ins.then_inc(item_done, 1)
                    pe.wait_ge(m_copied, b + 1)
                    ins = pe.matmul(on[:, b * 8:b * 8 + 8], vc, self.pt_cmp[:, b * 8:b * 8 + 8], start=False,
                                    stop=(b == NB - 1), skip_group_check=True)
                ins.then_inc(all_done, 1)

            @block.gpsimd
            def _(pool):
                for b in range(NB):
                    s, v = self.item_ready(IT_V + b)
                    pool.wait_ge(s, v)
                    if b >= 1:
                        pool.wait_ge(pooled, b)
                    pool.tensor_tensor(kw.rearrange("p (y d) -> p y d", d=HD),
                                       self.slot(IT_V + b)[:, 3072:4096].rearrange("p (y d) -> p y d", d=HD),
                                       self.pos_v[:].unsqueeze(1).broadcast_to([P, 16, HD]), ALU.mult
                                       ).then_inc(weighted, 1)

            @block.scalar
            def _(act):
                for b in range(NB):
                    act.wait_ge(pooled, b + 1)
                    if b >= 1:
                        act.wait_ge(mapped, b)
                    act.activation(plv, self.ps[:, 2, 0:32], ACT.Copy).then_inc(p_copied, 1)
                    act.wait_ge(mapped, b + 1)
                    if b >= 1:
                        act.wait_ge(pooled, b + 1)
                    act.activation(vc, self.ps[0:32, 3, 0:P], ACT.Copy).then_inc(m_copied, 1)

            @block.vector
            def _(dve):
                dve.wait_ge(all_done, 1)
                for g in range(2):
                    p = slice(g * HD, (g + 1) * HD)
                    src = self.ps[p, 0, 0:64].rearrange("p (b h) -> p h b", b=NB)[:, g * 4:g * 4 + 4, :]
                    dve.tensor_copy(self.xtv[p, 4:8, SEQ:TOK], src)
                    for x in range(2):
                        src = self.ps[p, 1, x * 32:(x + 1) * 32].rearrange("p (b h) -> p h b", b=NB)[:, 2 * x + g, :]
                        dve.tensor_copy(self.xtv[p, x, SEQ:TOK], src)

    def output_projection(self):
        nc, l, pj = self.nc, self.l, self.proj
        turned, t_copied, mm_done, added = (self.sem(s) for s in ("op_turned", "op_copied", "op_mm", "op_added"))
        for n in range(2):
            self.freed[IT_WO + n] = (mm_done, TILES * (n + 1))
        src_cols = [SB_Q, SB_Q + P, R_Q, R_Q + P] + [N_Q + j * P for j in range(4)]
        with nc.Block() as block:
            @block.sync
            def _(sp):
                self.issue_until(sp, l, IT_UP + SLOTS)
                sp.wait_ge(self.shift_done, 32)

            @block.tensor
            def _(pe):
                ident = self.c("ident")
                for t in range(4):
                    if t >= 2:
                        pe.wait_ge(t_copied, 2 * (t - 1))
                    for k in range(KD):
                        ins = pe.transpose(self.ps[:, 2 * (t % 2) + k // 4, (k % 4) * P:(k % 4 + 1) * P],
                                           pj[:, t, src_cols[k]:src_cols[k] + P], ident)
                    ins.then_inc(turned, 1)
                pe.wait_ge(t_copied, 6)
                for x in range(2):
                    ins = pe.transpose(self.ps[:, 0, x * P:x * P + NB], pj[0:NB, 4, R_Q + x * P:R_Q + (x + 1) * P],
                                       ident[0:NB, 0:NB])
                ins.then_inc(turned, 1)
                pe.wait_ge(t_copied, 9)
                for n in range(2):
                    s, v = self.item_ready(IT_WO + n)
                    pe.wait_ge(s, v)
                    w = self.slot(IT_WO + n).rearrange("p (k n) -> p k n", k=KD)
                    for t in range(TILES):
                        u, m = n * TILES + t, rows(t)
                        if u >= 4:
                            pe.wait_ge(added, u - 3)
                        for k in range(KD):
                            ins = pe.matmul(self.ps[0:m, 4 + u % 4, :], self.xtv[:, k, cols(t)], w[:, k, :],
                                            start=(k == 0), stop=(k == KD - 1))
                        ins.then_inc(mm_done, 1)

            @block.scalar
            def _(act):
                for t in range(4):
                    act.wait_ge(turned, t + 1)
                    for j in range(2):
                        act.activation(self.xtv[:, 4 * j:4 * j + 4, cols(t)],
                                       self.ps[:, 2 * (t % 2) + j, :].rearrange("p (k n) -> p k n", k=4), ACT.Copy
                                       ).then_inc(t_copied, 1)
                act.wait_ge(turned, 5)
                act.activation(self.xtv[:, 2:4, SEQ:TOK],
                               self.ps[:, 0, 0:256].rearrange("p (k n) -> p k n", k=2)[:, :, 0:NB], ACT.Copy
                               ).then_inc(t_copied, 1)

            @block.vector
            def _(dve):
                for n in range(2):
                    for t in range(TILES):
                        u, m = n * TILES + t, rows(t)
                        dve.wait_ge(mm_done, u + 1)
                        x = self.x_res[0:m, t, n * 512:(n + 1) * 512]
                        dve.tensor_tensor(x, x, self.ps[0:m, 4 + u % 4, :], ALU.add).then_inc(added, 1)

    def mlp_up(self):
        nc, l = self.nc, self.l
        mm_done, relu_done, sq_done = (self.sem(s) for s in ("up_mm", "up_relu", "up_square"))
        H = TOK // 2
        for c in range(8):
            self.freed[IT_UP + c] = (mm_done, 4 * (c + 1))
        rbuf = [self.scr[:, 0:TOK], self.scr[:, TOK:2 * TOK]]
        with nc.Block() as block:
            @block.sync
            def _(sp):
                self.issue_until(sp, l, IT_DN + SLOTS)

            @block.tensor
            def _(pe):
                for u in range(FF // P):
                    c, f = divmod(u, 4)
                    if f == 0:
                        s, v = self.item_ready(IT_UP + c)
                        pe.wait_ge(s, v)
                    if u >= 4:
                        pe.wait_ge(relu_done, u - 3)
                    w = self.slot(IT_UP + c).rearrange("p (k n) -> p k n", k=KD)
                    for half in range(2):
                        for k in range(KD):
                            ins = pe.matmul(self.ps[:, 2 * (u % 4) + half, 0:H], w[:, k, f * P:(f + 1) * P],
                                            self.xtv[:, k, half * H:(half + 1) * H], start=(k == 0),
                                            stop=(k == KD - 1))
                    ins.then_inc(mm_done, 1)

            @block.scalar
            def _(act):
                for u in range(FF // P):
                    act.wait_ge(mm_done, u + 1)
                    if u >= 2:
                        act.wait_ge(sq_done, u - 1)
                    act.activation(rbuf[u % 2].rearrange("p (x n) -> p x n", x=2),
                                   self.ps[:, 2 * (u % 4):2 * (u % 4) + 2, 0:H], ACT.Relu).then_inc(relu_done, 1)

            @block.vector
            def _(dve):
                for u in range(FF // P):
                    dve.wait_ge(relu_done, u + 1)
                    dve.tensor_tensor(self.hid[:, u, :], rbuf[u % 2], rbuf[u % 2], ALU.mult).then_inc(sq_done, 1)

    def mlp_down(self):
        nc, l = self.nc, self.l
        mm_done, added = self.sem("dn_mm"), self.sem("dn_added")
        part = self.sem("dn_part")
        for i in range(8):
            self.freed[IT_DN + i] = (part, i + 1)
        bank = lambda n, t: (5 * n + t) % 8
        with nc.Block() as block:
            @block.sync
            def _(sp):
                self.issue_until(sp, l, N_ITEMS)

            @block.tensor
            def _(pe):
                for n in range(2):
                    for q in range(4):
                        i = IT_DN + 4 * n + q
                        s, v = self.item_ready(i)
                        pe.wait_ge(s, v)
                        w = self.slot(i).rearrange("p (k n) -> p k n", k=8)
                        for t in range(TILES):
                            m = rows(t)
                            if n == 1 and q == 0 and t >= 3:
                                pe.wait_ge(added, t - 2)
                            for k in range(8):
                                ins = pe.matmul(self.ps[0:m, bank(n, t), :], self.hid[:, q * 8 + k, cols(t)],
                                                w[:, k, :], start=(q == 0 and k == 0), stop=(q == 3 and k == 7),
                                                skip_group_check=True)
                            if q == 3 and t < TILES - 1:
                                ins.then_inc(mm_done, 1)
                        ins.then_inc(part, 1)

            @block.vector
            def _(dve):
                for n in range(2):
                    for t in range(TILES):
                        m = rows(t)
                        if t < TILES - 1:
                            dve.wait_ge(mm_done, 4 * n + t + 1)
                        else:
                            dve.wait_ge(part, 4 * (n + 1))
                        x = self.x_res[0:m, t, n * 512:(n + 1) * 512]
                        dve.tensor_tensor(x, x, self.ps[0:m, bank(n, t), :], ALU.add).then_inc(added, 1)


_INS = ['x_prompt', 'x_sample', 'cache_sb_k', 'cache_sb_v', 'cache_cmp_k', 'cache_cmp_v', 'cache_slc_k',
        'cache_slc_v', 'state_win_k', 'state_win_v', 'state_ret', 'page_table', 'norm1_g', 'w_in', 'nsa_q_norm',
        'nsa_k_norm', 'cmp_pos_k', 'cmp_pos_v', 'cmp_w_k', 'cmp_w_v', 'w_out', 'norm2_g', 'w_up', 'w_down']
_OUTS = ([("y_prompt", (1, SEQ, D)), ("y_sample", (NB, 1, D))]
         + [(f"p_sb_{x}", (DEPTH, 1, SEQ, 4, HD)) for x in "kv"]
         + [(f"p_{n}_{x}", (DEPTH, 1, SEQ, 2, HD)) for n in ("cmp", "slc", "win") for x in "kv"]
         + [("p_ret", (DEPTH, 1, 4, HD, HD))]
         + [(f"s_sb_{x}", (DEPTH, NB, 1, 4, HD)) for x in "kv"]
         + [(f"s_{n}_{x}", (DEPTH, NB, 1, 2, HD)) for n in ("cmp", "slc") for x in "kv"]
         + [(f"s_win_{x}", (DEPTH, NB, WIN, 2, HD)) for x in "kv"]
         + [("s_ret", (DEPTH, NB, 4, HD, HD))])


def kernel(**inputs):
    import numpy as _np
    import concourse.bacc as _bacc
    from concourse import mybir as _mybir
    from concourse.bass_utils import run_bass_kernel_spmd as _run

    nc = _bacc.Bacc("TRN2", target_bir_lowering=False, num_devices=1)
    arrays, ins, outs = {}, {}, {}
    for name in _INS:
        a = _np.ascontiguousarray(inputs[name])
        arrays[f"in_{name}"] = a
        ins[name] = nc.dram_tensor(f"in_{name}", a.shape, _mybir.dt.from_np(a.dtype), kind="ExternalInput").ap()
    c = shape_constants()
    arrays["in_consts"] = c
    consts = nc.dram_tensor("in_consts", c.shape, _mybir.dt.from_np(c.dtype), kind="ExternalInput").ap()
    for name, shape in _OUTS:
        outs[name] = nc.dram_tensor(f"out_{name}", shape, F32, kind="ExternalOutput").ap()
    build(nc, ins, outs, consts)
    r = _run(nc, [arrays], core_ids=[0])
    return tuple(r.results[0][f"out_{name}"] for name, _ in _OUTS)
```

```python
import math
from contextlib import ExitStack

import numpy as np
import concourse.bass as bass
from concourse import mybir

F32 = mybir.dt.float32
BF16 = mybir.dt.bfloat16
I32 = mybir.dt.int32
ALU = mybir.AluOpType
ACT = mybir.ActivationFunctionType
AXX = mybir.AxisListType.X

P = 128
D = 1024
KD = D // P
SEQ, NB, DEPTH = 512, 8, 2
PAST, PAGE, NPAGE = 1024, 128, 8
HD = 64
TILES = SEQ // P + 1
TOK = SEQ + NB
FF = 4 * D
EPS = 1e-6
NEG = -1.0e30
WIN = 512
N_IN = 3096
SB_Q, SB_K, SB_V = 0, 256, 512
R_Q, R_K, R_V, R_G = 768, 1024, 1280, 1536
N_Q, C_K, C_V, S_K, S_V, W_K, W_V, N_G = 1792, 2304, 2432, 2560, 2688, 2816, 2944, 3072
T_SBQ, T_SBK, T_RQ, T_RK, T_NQ, T_SK, T_WK = 0, 2, 4, 6, 8, 12, 13
PACK = {0: 0, 1: 512, 3: 896, 2: 1024}
PACKED = 1280
IT_WIN, IT_KW, IT_K, IT_VW, IT_V, IT_WO, IT_UP, IT_DN, N_ITEMS = 0, 6, 7, 15, 16, 24, 26, 34, 42
CHUNKS = (3, 4, 5, 6, 1, 2, 0)
SLOTS = 3
SLOT = 4096

CONST_COLS = [("ident", 128), ("neg_suffix", 128), ("neg_later", 128), ("neg_ones", 128), ("sb_mask", 128), ("ret_mask", 128),
              ("cos_r", TILES * 32), ("sin_r", TILES * 32), ("cos_n", TILES * 8), ("sin_n", TILES * 8),
              ("decay", TILES * 8), ("gam_last", 4), ("gam_one", 2), ("blk_ind", 4), ("blk_ind32", 32), ("sub_row", 1), ("grp", 64),
              ("seq_ind", 8), ("blk_idx", 16), ("cmp_any", 1), ("own_head", 6), ("pick_head", 16),
              ("sb_neg", 128), ("nsa_neg", 128), ("cmp_neg", 64)]
CONST_AT = {}
_at = 0
for _n, _w in CONST_COLS:
    CONST_AT[_n] = (_at, _w)
    _at += _w
N_CONST = _at
N_KEEP = CONST_AT["sb_neg"][0]


def shape_constants():
    c = np.zeros((P, N_CONST), np.float32)

    def put(name, a):
        s, w = CONST_AT[name]
        c[:, s:s + w] = np.asarray(a, np.float32).reshape(P, w)

    i = np.arange(P)
    put("ident", np.eye(P))
    put("neg_suffix", -(i[:, None] >= i[None, :]).astype(np.float32))
    put("neg_later", -(i[:, None] > i[None, :]).astype(np.float32))
    put("neg_ones", -np.ones((P, P)))
    put("sb_mask", i[:, None] < i[None, :])
    put("ret_mask", i[:, None] <= i[None, :])
    put("sb_neg", np.where(i[:, None] < i[None, :], 0.0, NEG))
    put("nsa_neg", np.where(i[None, :] <= i[:, None], 0.0, NEG))
    pos = np.concatenate([np.arange(SEQ).reshape(4, P), np.full((1, P), PAST)]).astype(np.float32)
    for half, theta, cn, sn in ((32, 10000.0, "cos_r", "sin_r"), (8, 500000.0, "cos_n", "sin_n")):
        inv = np.exp(np.float32(-math.log(theta)) * np.arange(half, dtype=np.float32) / np.float32(half))
        ang = (pos[:, :, None] * inv.astype(np.float32)).astype(np.float32).transpose(1, 0, 2)
        put(cn, np.cos(ang))
        put(sn, np.sin(ang))
    lg = np.log1p(-np.exp2(-5.0 - np.arange(4)))
    dec = np.zeros((P, TILES, 8))
    for t in range(4):
        j = (t * P + i)[:, None]
        dec[:, t, 0:4] = np.exp(j * lg)
        dec[:, t, 4:8] = np.exp(-j * lg) / 8.0
    dec[:, 4, 0:4] = 1.0
    dec[:, 4, 4:8] = 1.0 / 8.0
    put("decay", dec)
    put("gam_last", np.broadcast_to(np.exp((SEQ - 1) * lg), (P, 4)))
    put("gam_one", np.exp(lg)[2 * np.arange(2)[None, :] + i[:, None] // 64])
    put("blk_ind", i[:, None] // 32 == np.arange(4)[None, :])
    put("blk_ind32", i[:, None] // 4 == np.arange(32)[None, :])
    put("sub_row", (i % 16)[:, None])
    put("grp", (i[:, None] // 4 == np.arange(64)[None, :] // 4))
    put("seq_ind", i[:, None] // 8 == np.arange(8)[None, :])
    put("blk_idx", np.broadcast_to(np.arange(16), (P, 16)))
    put("cmp_any", (i >= 31)[:, None])
    put("own_head", np.concatenate([i[:, None] % 32 == np.arange(4), i[:, None] % 32 // 4 == np.arange(2)], axis=1))
    put("pick_head", (i[:, None] // 32 == np.arange(16) % 4) & (i[:, None] % 4 == np.arange(16) // 4)
        & (i[:, None] % 32 < 8))
    q = np.arange(4)[None, :, None] * P + i[:, None, None]
    put("cmp_neg", np.where((np.arange(16)[None, None, :] + 1) * 32 - 1 <= q, 0.0, NEG))
    return c


def build(nc, ins, outs, consts):
    with ExitStack() as ctx:
        Decoder(nc, ctx, ins, outs, consts).program()


def rows(t):
    return P if t < 4 else NB


def cols(t):
    return slice(t * P, t * P + rows(t))


class Decoder:
    def __init__(self, nc, ctx, ins, outs, consts):
        self.nc, self.ctx, self.ins, self.outs, self.consts = nc, ctx, ins, outs, consts
        sb = self.sb
        self.x_res = sb("x_res", [P, TILES, D])
        self.xt = sb("xt", [P, KD * TOK])
        self.big = sb("big", [P, (FF // P) * TOK])
        self.tt = sb("tt", [P, 14, TOK])
        self.ring = sb("ring", [P, SLOTS, SLOT])
        self.cst = sb("cst", [P, N_KEEP])
        self.ident_b = sb("ident_b", [P, P], BF16)
        self.sb_neg_b = sb("sb_neg_b", [P, P], BF16)
        self.nsa_neg_b = sb("nsa_neg_b", [P, P], BF16)
        self.cmp_neg_b = sb("cmp_neg_b", [P, 64], BF16)
        self.g1 = sb("g1", [P, KD])
        self.g2 = sb("g2", [P, KD])
        self.gq = sb("gq", [P, HD])
        self.gk = sb("gk", [P, 3, HD])
        self.pos_k = sb("pos_k", [P, HD])
        self.pos_v = sb("pos_v", [P, HD])
        self.phi_k = sb("phi_k", [P, P])
        self.phi_v = sb("phi_v", [P, P])
        self.w_tail = sb("w_tail", [P, KD, 24])
        self.gates = sb("gates", [P, TILES, 24])
        self.pos8_k = sb("pos8_k", [P, 8, HD])
        self.pos8_v = sb("pos8_v", [P, 8, HD])
        self.q_nsa = sb("q_nsa", [P, NB, 8])
        self.q_wide = sb("q_wide", [P, 544])
        self.small = sb("small", [P, 104])
        self.few = sb("few", [P, 82])
        self.gate_rows = sb("gate_rows", [NB * 8, 3])
        self.stat = sb("stat", [P, 75])
        self.scr = sb("scr", [P, 3200])
        self.pages = sb("pages", [P, NB], I32)
        self.row_f = sb("row_f", [P, NB])
        self.row_i = sb("row_i", [P, NB], mybir.dt.uint32)
        self.ps = ctx.enter_context(nc.psum_tensor("ps", [P, 8, 512], F32))
        self.psf = self.ps[:].rearrange("p b n -> p (b n)")
        self.proj = self.big[:, 0:TILES * N_IN].rearrange("p (t n) -> p t n", n=N_IN)
        self.spare = self.big[:, TILES * N_IN:]
        self.hid = self.big[:].rearrange("p (f t) -> p f t", t=TOK)
        self.xtv = self.xt[:].rearrange("p (k t) -> p k t", t=TOK)
        self.layer_sems = []
        self.slot_ready = [self.sem(f"slot{s}_ready") for s in range(SLOTS)]
        self.gathered = [[self.sem(f"slot{s}_{kind}_gathered") for kind in ("sb", "slc", "cmp")]
                         for s in range(SLOTS)]
        self.outputs_done = self.sem("outputs_done")
        self.shift_done = self.sem("window_shift_done")
        self.small_ready = self.sem("small_ready")
        self.ret_state_in = self.sem("ret_state_in")
        self.n_out = 0
        self.freed = [None] * N_ITEMS
        self.issued = 0

    def sb(self, name, shape, dt=F32):
        return self.ctx.enter_context(self.nc.sbuf_tensor(name, shape, dt))

    def sem(self, name):
        s = self.ctx.enter_context(self.nc.semaphore(name))
        self.layer_sems.append(s)
        return s

    def c(self, name):
        s, w = CONST_AT[name]
        return self.cst[:, s:s + w]

    def is_gather(self, i):
        return IT_K <= i < IT_VW or IT_V <= i < IT_WO

    def loads_of(self, i):
        return 0 if self.is_gather(i) else 3 if IT_WO <= i < IT_UP else 1

    def wait_item(self, eng, i, kinds=(0, 1, 2)):
        s = i % SLOTS
        if self.is_gather(i):
            n = sum(self.is_gather(j) for j in range(s, i + 1, SLOTS))
            for kind in kinds:
                eng.wait_ge(self.gathered[s][kind], 16 * n)
        else:
            eng.wait_ge(self.slot_ready[s], 16 * sum(self.loads_of(j) for j in range(s, i + 1, SLOTS)))

    def slot(self, i):
        return self.ring[:, i % SLOTS, :]

    def issue_until(self, sp, l, last):
        while self.issued < min(last, N_ITEMS):
            i = self.issued
            self.issued += 1
            if self.is_gather(i):
                continue
            if i >= SLOTS:
                for s, v in self.freed[i - SLOTS]:
                    sp.wait_ge(s, v)
            ready = self.slot_ready[i % SLOTS]
            dst, a = self.slot(i), self.ins
            lay = bass.ds(l, 1)
            if i < IT_KW:
                c = [c for c in CHUNKS if c < 6][i]
                src = a["w_in"][lay, :, c * 512:(c + 1) * 512].rearrange("o (k p) n -> p (o k) n", p=P)
                sp.dma_start(dst.rearrange("p (k n) -> p k n", k=KD), src).then_inc(ready, 16)
            elif i in (IT_KW, IT_VW):
                w = a["state_win_k" if i == IT_KW else "state_win_v"][lay]
                src = w.rearrange("o b (p j) g d -> p (o b) (j g d)", p=P)
                sp.dma_start(dst.rearrange("p (b n) -> p b n", b=NB), src).then_inc(ready, 16)
            elif i < IT_UP:
                n = i - IT_WO
                w = a["w_out"][lay, :, n * 512:(n + 1) * 512]
                d3 = dst.rearrange("p (k n) -> p k n", k=KD)
                sp.dma_start(d3[:, 0:4, :], w[:, 0:512].rearrange("o (k p) n -> p (o k) n", p=P)).then_inc(ready, 16)
                for g in range(2):
                    src = w[:, 512 + g * 256:768 + g * 256].rearrange("o (r d) n -> d (o r) n", d=HD)
                    sp.dma_start(d3[g * HD:(g + 1) * HD, 4:8, :], src).then_inc(ready, 16)
            elif i < IT_DN:
                c = i - IT_UP
                src = a["w_up"][lay, :, c * 512:(c + 1) * 512].rearrange("o (k p) n -> p (o k) n", p=P)
                sp.dma_start(dst.rearrange("p (k n) -> p k n", k=KD), src).then_inc(ready, 16)
            else:
                n, q = divmod(i - IT_DN, 4)
                src = a["w_down"][lay, q * D:(q + 1) * D, n * 512:(n + 1) * 512]
                sp.dma_start(dst.rearrange("p (k n) -> p k n", k=KD),
                             src.rearrange("o (k p) n -> p (o k) n", p=P)).then_inc(ready, 16)

    def gather(self, pool, i):
        for s, v in self.freed[i - SLOTS]:
            pool.wait_ge(s, v)
        kv = "k" if i < IT_VW else "v"
        b = i - (IT_K if kv == "k" else IT_V)
        for kind, (cache, off, w) in enumerate((("sb", 0, 256), ("slc", 2048, 128), ("cmp", 3072, 128))):
            src = self.ins[f"cache_{cache}_{kv}"].rearrange("l n (s i) h d -> (l n s) (i h d)", s=16)
            pool.indirect_dma_start(out=self.slot(i)[:, off:off + 8 * w], out_offset=None, in_=src,
                                    in_offset=bass.IndirectOffsetOnAxis(ap=self.row_i[:, b:b + 1], axis=0)
                                    ).then_inc(self.gathered[i % SLOTS][kind], 16)

    def program(self):
        nc = self.nc
        self.n_pool = self.ins["cache_sb_k"].shape[1]
        self.setup()
        with nc.Fori(0, DEPTH) as l:
            self.l = l
            self.norm("n1", self.g1, first=True)
            self.project()
            self.stick_breaking()
            self.retention()
            self.sparse_attention()
            self.output_projection()
            self.norm("n2", self.g2)
            self.mlp_up()
            self.mlp_down()
            nc.gpsimd.dma_reset()
            nc.all_engine_barrier()
            for s in self.layer_sems:
                nc.sync.sem_clear(s)
            nc.all_engine_barrier()
        self.finish()

    def setup(self):
        nc, a = self.nc, self.ins
        loaded, zeroed = self.sem("setup_loaded"), self.sem("setup_zeroed")
        stage = self.xt[:, 0:N_CONST - N_KEEP]
        with nc.Block() as block:
            @block.sync
            def _(sp):
                sp.dma_start(self.cst[:], self.consts[:, 0:N_KEEP]).then_inc(loaded, 16)
                sp.dma_start(stage, self.consts[:, N_KEEP:N_CONST]).then_inc(loaded, 16)
                with nc.allow_non_contiguous_dma("page table"):
                    for j in range(NPAGE):
                        sp.dma_start(self.pages[16 * j:16 * (j + 1), :],
                                     a["page_table"].rearrange("b j -> j b")[j].partition_broadcast(16)
                                     ).then_inc(loaded, 16)
                sp.dma_start(self.x_res[:, 0:4, :], a["x_prompt"][0].rearrange("(t p) n -> p t n", p=P)
                             ).then_inc(loaded, 16)
                sp.dma_start(self.x_res[0:NB, 4, :], a["x_sample"].rearrange("b s n -> (b s) n")).then_inc(loaded, 16)
                sp.wait_ge(loaded, 192)

            @block.vector
            def _(dve):
                dve.memset(self.q_nsa[:], 0.0)
                dve.memset(self.phi_k[:], 0.0)
                dve.memset(self.phi_v[:], 0.0)
                dve.memset(self.stat[:], 1.0).then_inc(zeroed, 1)
                dve.wait_ge(loaded, 192)
                dve.tensor_copy(self.ident_b[:], self.c("ident"))
                dve.tensor_copy(self.sb_neg_b[:], stage[:, 0:128])
                dve.tensor_copy(self.nsa_neg_b[:], stage[:, 128:256])
                dve.tensor_copy(self.row_f[:], self.pages[:])
                dve.tensor_copy(self.cmp_neg_b[:], stage[:, 256:320]).then_inc(zeroed, 1)
                dve.wait_ge(zeroed, 2)
                dve.tensor_scalar(self.row_f[:], self.row_f[:], 16.0, self.c("sub_row"), ALU.mult, ALU.add
                                  ).then_inc(zeroed, 1)
                dve.wait_ge(zeroed, 3)
        for s in self.layer_sems:
            nc.sync.sem_clear(s)
        nc.all_engine_barrier()

    def finish(self):
        nc, o = self.nc, self.outs
        stored = self.sem("result_stored")
        with nc.Block() as block:
            @block.sync
            def _(sp):
                sp.dma_start(o["y_prompt"][0].rearrange("(t p) n -> p t n", p=P), self.x_res[:, 0:4, :]
                             ).then_inc(stored, 16)
                sp.dma_start(o["y_sample"].rearrange("b s n -> (b s) n"), self.x_res[0:NB, 4, :]).then_inc(stored, 16)
                sp.wait_ge(stored, 32)

    def linker(self, eng, name):
        chain, n = self.sem(name), [0]

        def link(instr):
            n[0] += 1
            instr.then_inc(chain, 1)
            eng.wait_ge(chain, n[0])
        return link

    def refine_rsqrt(self, dve, link, r, v, tmp):
        link(dve.tensor_tensor(tmp, r, r, ALU.mult))
        link(dve.tensor_tensor(tmp, tmp, v, ALU.mult))
        link(dve.tensor_scalar(tmp, tmp, -0.5, 1.5, ALU.mult, ALU.add))
        link(dve.tensor_tensor(r, r, tmp, ALU.mult))

    def norm(self, name, gain, first=False):
        nc, l = self.nc, self.l
        x, ss = self.x_res, self.stat[:, 0:5]
        r, tmp = self.small[:, 8:13], self.small[:, 16:21]
        xn = self.scr[:, 0:2 * D].rearrange("p (i n) -> p i n", i=2)
        squares, var_ready, root = (self.sem(name + s) for s in ("_squares", "_var", "_root"))
        scaled, turned, copied = (self.sem(name + s) for s in ("_scaled", "_turned", "_copied"))
        with nc.Block() as block:
            if first:
                @block.sync
                def _(sp):
                    self.issued = 0
                    a, o, lay = self.ins, self.outs, bass.ds(l, 1)
                    n = 0
                    loads = [(self.g1[:], a["norm1_g"][lay].rearrange("o (k p) -> p (o k)", p=P)),
                             (self.g2[:], a["norm2_g"][lay].rearrange("o (k p) -> p (o k)", p=P)),
                             (self.w_tail[:], a["w_in"][lay, :, N_G:N_IN].rearrange("o (k p) n -> p (o k) n", p=P)),
                             (self.gq[:], a["nsa_q_norm"][lay].rearrange("o d -> (o d)").partition_broadcast(P)),
                             (self.gk[:].rearrange("p c d -> p (c d)"),
                              a["nsa_k_norm"][lay].rearrange("o c d -> (o c d)").partition_broadcast(P))]
                    for pos, pos8, phi, wp, wf in ((self.pos_k, self.pos8_k, self.phi_k, "cmp_pos_k", "cmp_w_k"),
                                                   (self.pos_v, self.pos8_v, self.phi_v, "cmp_pos_v", "cmp_w_v")):
                        loads += [(pos8[q:P:4].rearrange("p i d -> p (i d)"),
                                   a[wp][lay, 8 * q:8 * q + 8].rearrange("o i d -> (o i d)").partition_broadcast(32))
                                  for q in range(4)]
                        loads += [(pos[c * 32:(c + 1) * 32, :], a[wp][lay].rearrange("o j d -> (o j) d"))
                                  for c in range(4)]
                        loads += [(phi[g * HD:(g + 1) * HD, g * HD:(g + 1) * HD],
                                   a[wf][lay].rearrange("o d e -> (o d) e")) for g in range(2)]
                    with nc.allow_non_contiguous_dma("small gains"):
                        for dst, src in loads:
                            sp.dma_start(dst, src).then_inc(self.small_ready, 16)
                            n += 1
                    self.n_small = 16 * n
                    self.issue_until(sp, l, SLOTS)
                    for kv in "kv":
                        src = a[f"state_win_{kv}"][lay, :, 1:WIN].rearrange("o b w g d -> (o b) (w g d)")
                        dst = o[f"s_win_{kv}"][lay, :, 0:WIN - 1].rearrange("o b w g d -> (o b) (w g d)")
                        sp.dma_start(dst, src).then_inc(self.shift_done, 16)
                    sp.wait_ge(self.small_ready, self.n_small)

            @block.scalar
            def _(act):
                junk = self.psf[:, 3072:4096]
                for t in range(TILES):
                    n = rows(t)
                    if t >= 1:
                        act.wait_ge(squares, t)
                    act.activation(junk[0:n], x[0:n, t, :], ACT.Square, accum_out=ss[0:n, t:t + 1]
                                   ).then_inc(squares, 1)
                act.wait_ge(var_ready, 1)
                act.activation(r, ss, ACT.Ln).then_inc(root, 1)
                act.wait_ge(root, 1)
                act.activation(r, r, ACT.Exp, scale=-0.5).then_inc(root, 1)

            @block.vector
            def _(dve):
                link = self.linker(dve, name + "_dve_chain")
                if first:
                    link(dve.tensor_copy(self.row_i[:], self.row_f[:]))
                    dve.tensor_scalar(self.row_f[:], self.row_f[:], float(16 * self.n_pool), None, ALU.add)
                dve.wait_ge(squares, TILES)
                dve.tensor_scalar(ss, ss, 1.0 / D, EPS, ALU.mult, ALU.add).then_inc(var_ready, 1)
                dve.wait_ge(root, 2)
                self.refine_rsqrt(dve, link, r, ss, tmp)
                if first:
                    dve.wait_ge(self.small_ready, self.n_small)
                for t in range(TILES + 1):
                    if t < TILES:
                        n = rows(t)
                        if t >= 2:
                            dve.wait_ge(turned, t - 1)
                        dve.tensor_scalar(xn[0:n, t % 2, :], x[0:n, t, :], r[0:n, t:t + 1], None, ALU.mult
                                          ).then_inc(scaled, 1)
                    if t >= 1:
                        s, n = t - 1, rows(t - 1)
                        dve.wait_ge(turned, s + 1)
                        for j in range(2):
                            src = self.ps[:, 2 * (s % 2) + j, :].rearrange("p (k n) -> p k n", k=4)[:, :, 0:n]
                            g = gain[:, 4 * j:4 * j + 4].unsqueeze(2).broadcast_to([P, 4, n])
                            ins = dve.tensor_tensor(self.xtv[:, 4 * j:4 * j + 4, cols(s)], src, g, ALU.mult)
                        ins.then_inc(copied, 1)

            @block.tensor
            def _(pe):
                ident = self.c("ident")
                for t in range(TILES):
                    n = rows(t)
                    pe.wait_ge(scaled, t + 1)
                    if t >= 2:
                        pe.wait_ge(copied, t - 1)
                    for k in range(KD):
                        ins = pe.transpose(self.ps[:, 2 * (t % 2) + k // 4, (k % 4) * P:(k % 4) * P + n],
                                           xn[0:n, t % 2, k * P:(k + 1) * P], ident[0:n, 0:n])
                    ins.then_inc(turned, 1)

    def rope(self, eng, link, x, half, cos, sin, tmp, shape):
        a, b = x[..., 0:half], x[..., half:2 * half]
        t = tmp
        eng.tensor_tensor(t[0], a, cos, ALU.mult)
        eng.tensor_tensor(t[1], b, sin, ALU.mult)
        eng.tensor_tensor(t[2], b, cos, ALU.mult)
        link(eng.tensor_tensor(t[3], a, sin, ALU.mult))
        eng.tensor_tensor(a, t[0], t[1], ALU.subtract)
        link(eng.tensor_tensor(b, t[2], t[3], ALU.add))

    def project(self):
        nc, l, pj = self.nc, self.l, self.proj
        mm_done, out_ready = self.sem("proj_mm"), self.sem("proj_out")
        turned, t_copied = self.sem("qk_turned"), self.sem("qk_copied")
        ret_ready, q_ready, k_ready = self.sem("ret_roped"), self.sem("nsa_q_ready"), self.sem("nsa_k_ready")
        exps, var_ready, root, rs_ready = (self.sem(s) for s in ("gate_exp", "head_var", "head_root", "head_rstd"))
        item_of = {c: i for i, c in enumerate(c for c in CHUNKS if c < 6)}
        done_at = {c: i for i, c in enumerate(CHUNKS)}
        for c in range(6):
            self.freed[item_of[c]] = ((mm_done, TILES * (done_at[c] + 1)),)
        ms = self.stat[:, 5:75]
        msv = ms.rearrange("p (t h) -> p t h", t=TILES)
        rs = self.scr[:, 2576:2646]
        rsv = rs.rearrange("p (t h) -> p t h", t=TILES)
        tmp70 = self.scr[:, 2496:2566]
        sq = self.spare[:, 0:896].rearrange("p (h d) -> p h d", d=HD)
        e_rg = self.scr[:, 0:1280].rearrange("p (t n) -> p t n", t=TILES)
        tq = [self.scr[:, 1280 + 256 * i:1536 + 256 * i] for i in range(4)]
        tk = [self.scr[:, 2304 + 48 * i:2352 + 48 * i] for i in range(4)]
        width = lambda c: 512 if c < 6 else 24

        def kview(t, n):
            return pj[0:n, t, C_K:N_G].rearrange("p (c x) -> p c x", c=3)[:, :, 0:P].rearrange(
                "p c (g d) -> p c g d", g=2)

        with nc.Block() as block:
            @block.sync
            def _(sp):
                self.issue_until(sp, l, IT_KW + SLOTS)

            @block.tensor
            def _(pe):
                ident = self.c("ident")
                v = 0

                def turn(t, blocks):
                    nonlocal v
                    n = rows(t)
                    if v >= 2:
                        pe.wait_ge(t_copied, v - 1)
                    for j, c0 in enumerate(blocks):
                        ins = pe.transpose(self.ps[:, 4 + v % 2, j * P:j * P + n], pj[0:n, t, c0:c0 + P],
                                           ident[0:n, 0:n])
                    ins.then_inc(turned, 1)
                    v += 1

                for i, c in enumerate(CHUNKS):
                    if c < 6:
                        self.wait_item(pe, item_of[c])
                        w = self.slot(item_of[c]).rearrange("p (k n) -> p k n", k=KD)
                    else:
                        w = self.w_tail
                    for t in range(TILES):
                        u, n = i * TILES + t, rows(t)
                        if u >= 4:
                            pe.wait_ge(out_ready, u - 3)
                        for k in range(KD):
                            ins = pe.matmul(self.ps[0:n, u % 4, 0:width(c)], self.xtv[:, k, cols(t)], w[:, k, :],
                                            start=(k == 0), stop=(k == KD - 1))
                        ins.then_inc(mm_done, 1)
                    if i == 5:
                        for t in range(TILES):
                            pe.wait_ge(q_ready, t + 1)
                            turn(t, [N_Q + j * P for j in range(4)])
                            pe.wait_ge(k_ready, t + 1)
                            turn(t, [S_K, W_K])
                for t in range(TILES):
                    pe.wait_ge(ret_ready, t + 1)
                    turn(t, [R_Q, R_Q + P, R_K, R_K + P])
                for t in range(TILES):
                    pe.wait_ge(out_ready, TILES * done_at[0] + t + 1)
                    turn(t, [SB_Q, SB_Q + P, SB_K, SB_K + P])

            @block.scalar
            def _(act):
                v = 0

                def copy_turned(t, dst, nblk, scaled):
                    nonlocal v
                    n = rows(t)
                    act.wait_ge(turned, v + 1)
                    src = self.ps[:, 4 + v % 2, 0:nblk * P].rearrange("p (j n) -> p j n", j=nblk)[:, :, 0:n]
                    if scaled:
                        ins = act.activation(self.tt[:, dst:dst + scaled, cols(t)], src[:, 0:scaled, :], ACT.Copy,
                                             scale=HD ** -0.5)
                    if scaled < nblk:
                        ins = act.activation(self.tt[:, dst + scaled:dst + nblk, cols(t)], src[:, scaled:nblk, :],
                                             ACT.Copy)
                    ins.then_inc(t_copied, 1)
                    v += 1

                for i, c in enumerate(CHUNKS):
                    for t in range(TILES):
                        u, n = i * TILES + t, rows(t)
                        act.wait_ge(mm_done, u + 1)
                        src = self.ps[0:n, u % 4, :]
                        nq = pj[0:n, t, N_Q:N_Q + 512].rearrange("p (r g d) -> p r g d", r=4, g=2)
                        if c == 3:
                            act.activation(pj[0:n, t, R_G:R_G + 256], src[:, 0:256], ACT.Copy)
                            ins = act.activation(nq[:, :, 0, :], src[:, 256:512].rearrange("p (r d) -> p r d", r=4),
                                                 ACT.Copy)
                        elif c == 4:
                            act.activation(nq[:, :, 1, :], src[:, 0:256].rearrange("p (r d) -> p r d", r=4), ACT.Copy)
                            ins = act.activation(pj[0:n, t, C_K:C_K + 256], src[:, 256:512], ACT.Copy)
                        else:
                            ins = act.activation(pj[0:n, t, c * 512:c * 512 + width(c)], src[:, 0:width(c)], ACT.Copy)
                        ins.then_inc(out_ready, 1)
                    if c == 6:
                        act.wait_ge(out_ready, (i + 1) * TILES)
                        for t in range(TILES):
                            n = rows(t)
                            act.activation(self.gates[0:n, t, :], pj[0:n, t, N_G:N_IN], ACT.Exp, scale=-1.0)
                            act.activation(e_rg[0:n, t, :], pj[0:n, t, R_G:R_G + 256], ACT.Exp, scale=-1.0
                                           ).then_inc(exps, 1)
                        act.wait_ge(var_ready, 1)
                        act.activation(rs, ms, ACT.Ln).then_inc(root, 1)
                        act.wait_ge(root, 1)
                        act.activation(rs, rs, ACT.Exp, scale=-0.5).then_inc(root, 1)
                    if i == 5:
                        for t in range(TILES):
                            copy_turned(t, T_NQ, 4, 4)
                            copy_turned(t, T_SK, 2, 0)
                for t in range(TILES):
                    copy_turned(t, T_RQ, 4, 0)
                for t in range(TILES):
                    copy_turned(t, T_SBQ, 4, 2)

            @block.vector
            def _(dve):
                link = self.linker(dve, "proj_dve_chain")
                cosr = self.c("cos_r").rearrange("p (t x) -> p t x", t=TILES)
                sinr = self.c("sin_r").rearrange("p (t x) -> p t x", t=TILES)
                cosn = self.c("cos_n").rearrange("p (t x) -> p t x", t=TILES)
                sinn = self.c("sin_n").rearrange("p (t x) -> p t x", t=TILES)
                dec = self.c("decay").rearrange("p (t x) -> p t x", t=TILES)
                for t in range(TILES):
                    n = rows(t)
                    dve.wait_ge(out_ready, TILES * done_at[5] + t + 1)
                    q = pj[0:n, t, N_Q:N_Q + 512].rearrange("p (h d) -> p h d", d=HD)
                    kk = kview(t, n)
                    dve.tensor_tensor(sq[0:n, 0:8, :], q, q, ALU.mult)
                    link(dve.tensor_tensor(sq[0:n, 8:14, :].rearrange("p (c g) d -> p c g d", c=3), kk, kk, ALU.mult))
                    link(dve.tensor_reduce(msv[0:n, t, :], sq[0:n], AXX, ALU.add))
                dve.tensor_scalar(ms, ms, 1.0 / HD, EPS, ALU.mult, ALU.add).then_inc(var_ready, 1)
                dve.wait_ge(root, 2)
                self.refine_rsqrt(dve, link, rs, ms, tmp70)
                dve.tensor_scalar(rs, rs, 1.0, None, ALU.mult).then_inc(rs_ready, 1)
                dve.wait_ge(rs_ready, 1)
                for t in range(TILES):
                    n = rows(t)
                    q = pj[0:n, t, N_Q:N_Q + 512].rearrange("p (h d) -> p h d", d=HD)
                    link(dve.tensor_tensor(q, q, rsv[0:n, t, 0:8].unsqueeze(2).broadcast_to([n, 8, HD]), ALU.mult))
                    link(dve.tensor_tensor(q, q, self.gq[0:n].unsqueeze(1).broadcast_to([n, 8, HD]), ALU.mult))
                    self.rope(dve, link, q, 8, cosn[0:n, t, :].unsqueeze(1).broadcast_to([n, 8, 8]),
                              sinn[0:n, t, :].unsqueeze(1).broadcast_to([n, 8, 8]),
                              [z[0:n, 0:64].rearrange("p (h d) -> p h d", h=8) for z in tq], [n, 8])
                    dve.tensor_scalar(q, q, 1.0, None, ALU.mult).then_inc(q_ready, 1)
                dve.wait_ge(exps, TILES)
                for t in range(TILES):
                    n = rows(t)
                    dve.tensor_scalar(e_rg[0:n, t, :], e_rg[0:n, t, :], 1.0, None, ALU.add)
                    link(dve.tensor_scalar(self.gates[0:n, t, :], self.gates[0:n, t, :], 1.0, None, ALU.add))
                    dve.reciprocal(self.gates[0:n, t, :], self.gates[0:n, t, :])
                    link(dve.reciprocal(e_rg[0:n, t, :], e_rg[0:n, t, :]))
                    link(dve.tensor_tensor(pj[0:n, t, R_G:R_G + 256], pj[0:n, t, R_G:R_G + 256], e_rg[0:n, t, :],
                                           ALU.mult))
                for t in range(TILES):
                    n = rows(t)
                    dve.wait_ge(out_ready, TILES * done_at[2] + t + 1)
                    x = pj[0:n, t, R_Q:R_V].rearrange("p (h d) -> p h d", d=HD)
                    self.rope(dve, link, x, 32, cosr[0:n, t, :].unsqueeze(1).broadcast_to([n, 8, 32]),
                              sinr[0:n, t, :].unsqueeze(1).broadcast_to([n, 8, 32]),
                              [q[0:n].rearrange("p (h d) -> p h d", h=8) for q in tq], [n, 8])
                    dve.tensor_tensor(x, x, dec[0:n, t, :].unsqueeze(2).broadcast_to([n, 8, HD]), ALU.mult
                                      ).then_inc(ret_ready, 1)

            @block.gpsimd
            def _(pool):
                link = self.linker(pool, "proj_pool_chain")
                cosn = self.c("cos_n").rearrange("p (t x) -> p t x", t=TILES)
                sinn = self.c("sin_n").rearrange("p (t x) -> p t x", t=TILES)
                pool.wait_ge(rs_ready, 1)
                for t in range(TILES):
                    n = rows(t)
                    for j in range(3):
                        kk = kview(t, n)[:, j]
                        r = rsv[0:n, t, 8 + 2 * j:10 + 2 * j].unsqueeze(2).broadcast_to([n, 2, HD])
                        link(pool.tensor_tensor(kk, kk, r, ALU.mult))
                        link(pool.tensor_tensor(kk, kk, self.gk[0:n, j].unsqueeze(1).broadcast_to([n, 2, HD]),
                                                ALU.mult))
                        self.rope(pool, link, kk, 8, cosn[0:n, t, :].unsqueeze(1).broadcast_to([n, 2, 8]),
                                  sinn[0:n, t, :].unsqueeze(1).broadcast_to([n, 2, 8]),
                                  [z[0:n, 0:16].rearrange("p (g d) -> p g d", g=2) for z in tk], [n, 2])
                    pool.tensor_copy(tk[0][0:n, 0:1], tk[1][0:n, 0:1]).then_inc(k_ready, 1)

    def store_heads(self, sp):
        o, l, pj = self.outs, self.l, self.proj
        lay = bass.ds(l, 1)
        for name, c0, w in (("sb_k", SB_K, 256), ("sb_v", SB_V, 256), ("cmp_k", C_K, P), ("cmp_v", C_V, P),
                            ("slc_k", S_K, P), ("slc_v", S_V, P), ("win_k", W_K, P), ("win_v", W_V, P)):
            dst = o["p_" + name][lay].rearrange("o b (t p) h d -> p (o b t) (h d)", p=P)
            sp.dma_start(dst, pj[:, 0:4, c0:c0 + w]).then_inc(self.outputs_done, 16)
            if name.startswith("win"):
                dst = o["s_" + name][lay, :, WIN - 1:WIN].rearrange("o b w h d -> (o b w) (h d)")
            else:
                dst = o["s_" + name][lay].rearrange("o b s h d -> (o b s) (h d)")
            sp.dma_start(dst, pj[0:NB, 4, c0:c0 + w]).then_inc(self.outputs_done, 16)

    def stick_breaking(self):
        nc, pj = self.nc, self.proj
        z_ready, abs_ready, ln_ready, l_ready = (self.sem(s) for s in ("sb_z", "sb_abs", "sb_ln", "sb_softplus"))
        e_ready, cum_ready, w_ready, pv_done = (self.sem(s) for s in ("sb_e", "sb_cum", "sb_w", "sb_pv"))
        lbuf = [self.xt[:, 0:PACKED], self.xt[:, PACKED:2 * PACKED]]
        wbuf = self.xt[:, 2 * PACKED:3 * PACKED]
        ebuf = [self.scr[:, 0:PACKED], self.scr[:, PACKED:2 * PACKED]]
        zb = lambda h: self.psf[:, (h % 2) * 1536:(h % 2) * 1536 + PACKED]

        with nc.Block() as block:
            @block.tensor
            def _(pe):
                for i in range(5):
                    if i < 4:
                        h, p0 = i, (i % 2) * HD
                        if h >= 2:
                            pe.wait_ge(w_ready, h - 1)
                        for jb in (0, 1, 3, 2):
                            n = SEQ - jb * P
                            ins = pe.matmul(zb(h)[:, PACK[jb]:PACK[jb] + n],
                                            self.tt[p0:p0 + HD, T_SBK + h // 2, jb * P:(jb + 1) * P],
                                            self.tt[p0:p0 + HD, T_SBQ + h // 2, jb * P:SEQ],
                                            start=(jb != 3), stop=True, skip_group_check=True)
                        ins.then_inc(z_ready, 1)
                    if i >= 1:
                        h = i - 1
                        pe.wait_ge(l_ready, h + 1)
                        for jb in range(4):
                            a = PACK[jb]
                            pe.matmul(zb(h)[:, a:a + P], self.ident_b[:], self.sb_neg_b[:], start=False, stop=True,
                                      skip_group_check=True)
                            ins = pe.matmul(zb(h)[:, a:a + SEQ - jb * P], self.c("neg_suffix"),
                                            lbuf[h % 2][:, a:a + SEQ - jb * P], start=False, stop=True,
                                            skip_group_check=True)
                            for j2 in range(jb + 1, 4):
                                n2 = SEQ - j2 * P
                                ins = pe.matmul(zb(h)[:, a + (j2 - jb) * P:a + SEQ - jb * P], self.c("neg_ones"),
                                                lbuf[h % 2][:, PACK[j2]:PACK[j2] + n2], start=False, stop=True,
                                                skip_group_check=True)
                        ins.then_inc(cum_ready, 1)
                        pe.wait_ge(w_ready, h + 1)
                        for qb in range(4):
                            for jb in range(qb + 1):
                                a = PACK[jb] + (qb - jb) * P
                                ins = pe.matmul(self.psf[:, 3072 + qb * 256 + h * HD:3072 + qb * 256 + (h + 1) * HD],
                                                wbuf[:, a:a + P], pj[:, jb, SB_V + h * HD:SB_V + (h + 1) * HD],
                                                start=(jb == 0), stop=(jb == qb), skip_group_check=True)
                        ins.then_inc(pv_done, 1)

            @block.vector
            def _(dve):
                link = self.linker(dve, "sb_dve_chain")

                for h in range(4):
                    dve.wait_ge(ln_ready, h + 1)
                    if h >= 2:
                        dve.wait_ge(cum_ready, h - 1)
                    link(dve.scalar_tensor_tensor(out=lbuf[h % 2], in0=zb(h), scalar=0.0, in1=ebuf[h % 2],
                                                  op0=ALU.max, op1=ALU.add))
                    for jb in range(4):
                        d = lbuf[h % 2][:, PACK[jb]:PACK[jb] + P]
                        ins = dve.tensor_tensor(d, d, self.c("sb_mask"), ALU.mult)
                    ins.then_inc(l_ready, 1)

            @block.scalar
            def _(act):
                def softplus_tail(h):
                    act.wait_ge(z_ready, h + 1)
                    if h >= 2:
                        act.wait_ge(l_ready, h - 1)
                    act.activation(ebuf[h % 2], zb(h), ACT.Abs).then_inc(abs_ready, 1)
                    act.wait_ge(abs_ready, h + 1)
                    act.activation(ebuf[h % 2], ebuf[h % 2], ACT.Exp, scale=-1.0).then_inc(e_ready, 1)
                    act.wait_ge(e_ready, h + 1)
                    act.activation(ebuf[h % 2], ebuf[h % 2], ACT.Ln, bias=1.0).then_inc(ln_ready, 1)

                softplus_tail(0)
                for h in range(4):
                    if h < 3:
                        softplus_tail(h + 1)
                    act.wait_ge(cum_ready, h + 1)
                    if h >= 1:
                        act.wait_ge(pv_done, h)
                    act.activation(wbuf, zb(h), ACT.Exp).then_inc(w_ready, 1)
                act.wait_ge(pv_done, 4)
                act.activation(pj[:, 0:4, SB_Q:SB_Q + 256],
                               self.psf[:, 3072:4096].rearrange("p (q n) -> p q n", q=4), ACT.Copy)

            @block.sync
            def _(sp):
                self.store_heads(sp)
                self.n_out = 16 * 16

            @block.gpsimd
            def _(pool):
                self.gather(pool, IT_K)
                self.gather(pool, IT_K + 1)

    def retention(self):
        nc, pj, o, a = self.nc, self.proj, self.outs, self.ins
        lay = bass.ds(self.l, 1)
        s_ready, copied, masked, pv_done = (self.sem(s) for s in ("ret_inner", "ret_copied", "ret_masked", "ret_pv"))
        st_mm, st_ready, var_ready, root = (self.sem(s) for s in ("ret_state_mm", "ret_state", "ret_var", "ret_root"))
        cleared, built, v_stored, v_read, st_new, o_mm, o_copied, o_stored, o_read, s_var_ready, s_root = (
            self.sem(s) for s in ("rs_cleared", "rs_queries", "rs_v_stored", "rs_v_read", "rs_state", "rs_mm",
                                  "rs_copied", "rs_o_stored", "rs_o_read", "rs_var", "rs_root"))
        weighted, pooled, p_copied, mapped = (self.sem(s) for s in ("cp_weighted", "cp_pooled", "cp_copied",
                                                                    "cp_mapped"))
        ibuf = [self.xt[:, 0:PACKED], self.xt[:, PACKED:2 * PACKED]]
        sq = self.xt[:, 2560:3584].rearrange("p (h d) -> p h d", d=HD)
        state = self.scr[0:HD, 0:256]
        mu, var, r, tmp = (self.small[:, 16 * i:16 * i + 16] for i in range(4))
        zb = lambda h: self.psf[:, (h % 2) * 1536:(h % 2) * 1536 + PACKED]
        unused = self.tt[:, 0:4, :].rearrange("p j t -> p (j t)")
        st = unused[:, 0:1024].rearrange("p (b x e) -> p b x e", b=NB, x=2)
        v_rows = unused[:, 1024:2048]
        vb = v_rows.rearrange("p (b x e) -> p b x e", b=NB, x=2)
        osb = self.scr[0:32, 256:320]
        orow = self.scr[0:NB, 384:640]
        s_sq = self.scr[0:NB, 640:896]
        s_mu, s_var, s_r, s_tmp = (self.small[0:NB, 64 + 4 * i:68 + 4 * i] for i in range(4))
        s_v = nc.dram_tensor("scratch_ret_v", [NB, 256], F32, kind="Internal").ap()
        s_o = nc.dram_tensor("scratch_ret_o", [32, HD], F32, kind="Internal").ap()
        s_g = nc.dram_tensor("scratch_gates", [NB, 24], F32, kind="Internal").ap()
        self.s_q = nc.dram_tensor("scratch_sb_q", [NB, 256], F32, kind="Internal").ap()
        kw = self.spare[:, 0:1024].rearrange("p (i n) -> p i n", i=8)
        pl = self.spare[:, 1024:1056]
        self.kcmp_t = self.scr[:, 2912:2928]
        self.vcmp = self.scr[0:16, 3072:3200]

        with nc.Block() as block:
            @block.tensor
            def _(pe):
                for i in range(5):
                    if i < 4:
                        h, p0 = i, (i % 2) * HD
                        if h >= 2:
                            pe.wait_ge(copied, h - 1)
                        for jb in (0, 1, 3, 2):
                            n = SEQ - jb * P
                            ins = pe.matmul(zb(h)[:, PACK[jb]:PACK[jb] + n],
                                            self.tt[p0:p0 + HD, T_RK + h // 2, jb * P:(jb + 1) * P],
                                            self.tt[p0:p0 + HD, T_RQ + h // 2, jb * P:SEQ],
                                            start=(jb != 3), stop=True, skip_group_check=True)
                        ins.then_inc(s_ready, 1)
                    if i >= 1:
                        h = i - 1
                        pe.wait_ge(masked, h + 1)
                        for qb in range(4):
                            for jb in range(qb + 1):
                                a0 = PACK[jb] + (qb - jb) * P
                                ins = pe.matmul(self.psf[:, 3072 + qb * 256 + h * HD:3072 + qb * 256 + (h + 1) * HD],
                                                ibuf[h % 2][:, a0:a0 + P], pj[:, jb, R_V + h * HD:R_V + (h + 1) * HD],
                                                start=(jb == 0), stop=(jb == qb), skip_group_check=True)
                        ins.then_inc(pv_done, 1)
                pe.wait_ge(copied, 4)
                for h in range(4):
                    for t in range(4):
                        ins = pe.matmul(self.ps[0:HD, 0, h * HD:(h + 1) * HD],
                                        pj[:, t, R_K + h * HD:R_K + (h + 1) * HD],
                                        pj[:, t, R_V + h * HD:R_V + (h + 1) * HD], start=(t == 0), stop=(t == 3),
                                        skip_group_check=True)
                ins.then_inc(st_mm, 1)
                pe.wait_ge(built, 1)
                pe.wait_ge(st_new, 1)
                for b in range(NB):
                    for x in range(2):
                        ins = pe.matmul(self.ps[0:32, 4, 0:HD], self.q_wide[:, x * 256 + b * 32:x * 256 + b * 32 + 32],
                                        st[:, b, x, :], start=(b == 0 and x == 0), stop=(b == NB - 1 and x == 1))
                ins.then_inc(o_mm, 1)
                pe.wait_ge(weighted, 1)
                for i in range(8):
                    ins = pe.matmul(self.ps[:, 1, 4 * i:4 * i + 4], kw[:, i, :], self.c("blk_ind"), start=True,
                                    stop=True, skip_group_check=True)
                ins.then_inc(pooled, 1)
                pe.wait_ge(p_copied, 1)
                pe.matmul(self.ps[:, 2, 0:16], self.phi_k[:], pl[:, 0:16], start=True, stop=True)
                pe.matmul(self.ps[0:16, 3, 0:P], pl[:, 16:32], self.phi_v[:], start=True, stop=True
                          ).then_inc(mapped, 1)

            @block.scalar
            def _(act):
                for h in range(4):
                    act.wait_ge(s_ready, h + 1)
                    if h >= 2:
                        act.wait_ge(pv_done, h - 1)
                    act.activation(ibuf[h % 2], zb(h), ACT.Copy).then_inc(copied, 1)
                act.wait_ge(var_ready, 1)
                act.activation(r, var, ACT.Ln).then_inc(root, 1)
                act.wait_ge(root, 1)
                act.activation(r, r, ACT.Exp, scale=-0.5).then_inc(root, 1)
                act.wait_ge(s_var_ready, 1)
                act.activation(s_r, s_var, ACT.Ln).then_inc(s_root, 1)
                act.wait_ge(s_root, 1)
                act.activation(s_r, s_r, ACT.Exp, scale=-0.5).then_inc(s_root, 1)

            @block.vector
            def _(dve):
                link = self.linker(dve, "ret_dve_chain")
                for i in range(8):
                    kv, t = divmod(i, 4)
                    src = pj[:, t, (C_K, C_V)[kv]:(C_K, C_V)[kv] + P].rearrange("p (g d) -> p g d", g=2)
                    pos = (self.pos_k, self.pos_v)[kv][:].unsqueeze(1).broadcast_to([P, 2, HD])
                    ins = dve.tensor_tensor(kw[:, i, :].rearrange("p (g d) -> p g d", g=2), src, pos, ALU.mult)
                ins.then_inc(weighted, 1)
                for h in range(4):
                    dve.wait_ge(copied, h + 1)
                    for jb in range(4):
                        d = ibuf[h % 2][:, PACK[jb]:PACK[jb] + P]
                        ins = dve.tensor_tensor(d, d, self.c("ret_mask"), ALU.mult)
                    ins.then_inc(masked, 1)
                dve.wait_ge(v_read, 48)
                kt = self.tt[:, T_RK:T_RK + 2, SEQ:TOK].rearrange("p x b -> p b x").unsqueeze(3).broadcast_to(
                    [P, NB, 2, HD])
                link(dve.tensor_tensor(vb, vb, kt, ALU.mult))
                dve.wait_ge(self.ret_state_in, 32)
                for x in range(2):
                    ins = dve.scalar_tensor_tensor(out=st[:, :, x, :], in0=st[:, :, x, :],
                                                   scalar=self.c("gam_one")[:, x:x + 1], in1=vb[:, :, x, :],
                                                   op0=ALU.mult, op1=ALU.add)
                ins.then_inc(st_new, 1)
                dve.wait_ge(pv_done, 4)
                acc = self.psf[:, 3072:4096].rearrange("p (h d) -> p h d", d=HD)
                link(dve.tensor_reduce(mu, acc, AXX, ALU.add))
                link(dve.tensor_scalar(mu, mu, 1.0 / HD, None, ALU.mult))
                link(dve.tensor_tensor(sq, acc, mu.unsqueeze(2).broadcast_to([P, 16, HD]), ALU.subtract))
                dve.wait_ge(o_mm, 1)
                dve.tensor_copy(osb, self.ps[0:32, 4, 0:HD]).then_inc(o_copied, 1)
                xc = pj[:, 0:4, R_Q:R_Q + 256].rearrange("p t (h d) -> p t h d", h=4)
                link(dve.tensor_copy(xc, sq.rearrange("p (t h) d -> p t h d", t=4)))
                link(dve.tensor_tensor(sq, sq, sq, ALU.mult))
                link(dve.tensor_reduce(var, sq, AXX, ALU.add))
                dve.tensor_scalar(var, var, 1.0 / HD, EPS, ALU.mult, ALU.add).then_inc(var_ready, 1)
                dve.wait_ge(pooled, 1)
                dve.tensor_copy(pl, self.ps[:, 1, 0:32]).then_inc(p_copied, 1)
                dve.wait_ge(st_mm, 1)
                dve.tensor_tensor(state.rearrange("p (h e) -> p h e", h=4),
                                  self.ps[0:HD, 0, 0:256].rearrange("p (h e) -> p h e", h=4),
                                  self.c("gam_last")[0:HD].unsqueeze(2).broadcast_to([HD, 4, HD]), ALU.mult
                                  ).then_inc(st_ready, 1)
                dve.wait_ge(root, 2)
                self.refine_rsqrt(dve, link, r, var, tmp)
                link(dve.tensor_tensor(xc, xc, r.rearrange("p (t h) -> p t h", t=4).unsqueeze(3).broadcast_to(
                    [P, 4, 4, HD]), ALU.mult))
                link(dve.tensor_tensor(pj[:, 0:4, R_Q:R_Q + 256], pj[:, 0:4, R_Q:R_Q + 256],
                                       pj[:, 0:4, R_G:R_G + 256], ALU.mult))
                dve.wait_ge(mapped, 1)
                dve.tensor_copy(self.kcmp_t, self.ps[:, 2, 0:16])
                dve.tensor_copy(self.vcmp, self.ps[0:16, 3, 0:P])
                dve.wait_ge(o_read, 16)
                ov = orow.rearrange("p (h d) -> p h d", h=4)
                sv = s_sq.rearrange("p (h d) -> p h d", h=4)
                link(dve.tensor_reduce(s_mu, ov, AXX, ALU.add))
                link(dve.tensor_scalar(s_mu, s_mu, 1.0 / HD, None, ALU.mult))
                link(dve.tensor_tensor(ov, ov, s_mu.unsqueeze(2).broadcast_to([NB, 4, HD]), ALU.subtract))
                link(dve.tensor_tensor(s_sq, orow, orow, ALU.mult))
                link(dve.tensor_reduce(s_var, sv, AXX, ALU.add))
                dve.tensor_scalar(s_var, s_var, 1.0 / HD, EPS, ALU.mult, ALU.add).then_inc(s_var_ready, 1)
                dve.wait_ge(s_root, 2)
                self.refine_rsqrt(dve, link, s_r, s_var, s_tmp)
                link(dve.tensor_tensor(ov, ov, s_r.unsqueeze(2).broadcast_to([NB, 4, HD]), ALU.mult))
                link(dve.tensor_tensor(pj[0:NB, 4, R_Q:R_Q + 256], orow, pj[0:NB, 4, R_G:R_G + 256], ALU.mult))

            @block.sync
            def _(sp):
                src = a["state_ret"][lay].rearrange("o b (x h) d e -> (h d) (o b) x e", h=2)
                for x in range(2):
                    sp.dma_start(st[:, :, x, :], src[:, :, x, :]).then_inc(self.ret_state_in, 16)
                sp.dma_start(s_v, pj[0:NB, 4, R_V:R_V + 256]).then_inc(v_stored, 16)
                sp.dma_start(s_g, self.gates[0:NB, 4, :]).then_inc(v_stored, 16)
                sp.dma_start(self.s_q, pj[0:NB, 4, SB_Q:SB_Q + 256]).then_inc(v_stored, 16)
                sp.wait_ge(v_stored, 48)
                for h in range(2):
                    src = s_v.rearrange("b (x h e) -> h (b x) e", x=2, h=2)[h]
                    sp.dma_start(v_rows[h * HD:(h + 1) * HD].rearrange("p (y e) -> p y e", e=HD),
                                 src.partition_broadcast(HD)).then_inc(v_read, 16)
                with nc.allow_non_contiguous_dma("sample gates"):
                    sp.dma_start(self.gate_rows[:], s_g.rearrange("b (h c) -> (b h) c", c=3)).then_inc(v_read, 16)
                sp.wait_ge(v_read, 48)
                sp.wait_ge(st_new, 1)
                dst = o["s_ret"][lay].rearrange("o b (x h) d e -> (h d) (o b) x e", h=2)
                for x in range(2):
                    sp.dma_start(dst[:, :, x, :], st[:, :, x, :]).then_inc(self.outputs_done, 16)
                sp.wait_ge(o_copied, 1)
                sp.dma_start(s_o, osb).then_inc(o_stored, 16)
                sp.wait_ge(o_stored, 16)
                sp.dma_start(orow, s_o.rearrange("(b h) d -> b (h d)", b=NB)).then_inc(o_read, 16)
                sp.wait_ge(st_ready, 1)
                dst = o["p_ret"][lay].rearrange("o b h d e -> d (o b h) e")
                sp.dma_start(dst, state.rearrange("p (h e) -> p h e", h=4)).then_inc(self.outputs_done, 16)
                self.n_out += 48
                sp.wait_ge(o_read, 16)
                sp.wait_ge(self.outputs_done, self.n_out)

            @block.gpsimd
            def _(pool):
                pool.memset(self.q_wide[:], 0.0).then_inc(cleared, 1)
                pool.wait_ge(cleared, 1)
                for g in range(2):
                    p = slice(g * HD, (g + 1) * HD)
                    pool.tensor_copy(self.q_nsa[p, :, 4 * g:4 * g + 4],
                                     self.tt[p, T_NQ:T_NQ + 4, SEQ:TOK].rearrange("p r b -> p b r"))
                    for x in range(2):
                        dst = self.q_wide[p, x * 256:x * 256 + 288].rearrange("p (b y) -> p b y", y=36)[:, :, 2 * x + g]
                        ins = pool.tensor_copy(dst, self.tt[p, T_RQ + x, SEQ:TOK])
                ins.then_inc(built, 1)

    def sparse_attention(self):
        nc, l = self.nc, self.l
        prompt, sample = self.prompt_sparse(), self.sample_cached()

        def in_turn(eng, name):
            a, b = prompt[name](eng), sample[name](eng)
            live = [a, b]
            while live:
                for g in list(live):
                    if next(g, live) is live:
                        live.remove(g)

        with nc.Block() as block:
            @block.sync
            def _(sp):
                sp.dma_start(self.q_everywhere, self.s_q.rearrange("b n -> (b n)").partition_broadcast(P)
                             ).then_inc(self.q_spread, 16)
                self.issue_until(sp, l, IT_WO + SLOTS)

            @block.tensor
            def _(pe):
                in_turn(pe, "pe")

            @block.scalar
            def _(act):
                in_turn(act, "act")

            @block.vector
            def _(dve):
                in_turn(dve, "dve")

            @block.gpsimd
            def _(pool):
                for _ in sample["pool"](pool):
                    pass

    def prompt_sparse(self):
        pj = self.proj
        qk_done, nmax_ready, exp_done, turned = (self.sem(s) for s in ("ns_qk", "ns_negmax", "ns_exp", "ns_turned"))
        copied = [self.sem("ns_copied_dve"), self.sem("ns_copied_act")]
        pv_done, o_read = self.sem("ns_pv"), self.sem("ns_o_read")
        prob = [self.xt[:, 0:512], self.xt[:, 512:1024]]
        pt = [self.xt[:, 1024:1536], self.xt[:, 1536:2048]]
        otmp = self.xt[:, 2048:2560]
        nmax = [self.small[:, 0:1], self.small[:, 1:2]]
        rsum = [self.small[:, 8:16], self.small[:, 16:24]]
        wgt = self.small[:, 24:32]
        units = [(qt, br, h) for qt in (3, 2, 1, 0) for br in range(3) for h in range(8)]
        U = len(units)
        nkeys = lambda qt, br: 16 if br == 0 else (qt + 1) * P

        def copied_of(u):
            return copied[u % 2], u // 2 + 1

        def pe_steps(pe):
            for u in range(U + 2):
                if u < U:
                    qt, br, h = units[u]
                    g, r, nk = h // 4, h % 4, nkeys(qt, br)
                    s = self.ps[:, u % 2, :]
                    if br == 0:
                        mask = self.cmp_neg_b[:, qt * 16:qt * 16 + 16]
                        keys = self.kcmp_t[g * HD:(g + 1) * HD, :]
                    else:
                        mask = self.nsa_neg_b[:]
                        keys = self.tt[g * HD:(g + 1) * HD, (T_SK, T_WK)[br - 1], 0:nk]
                    if u >= 2:
                        pe.wait_ge(exp_done, u - 1)
                    pe.matmul(s[:, nk - mask.shape[1]:nk], self.ident_b[:], mask, start=True, stop=True,
                              skip_group_check=True)
                    pe.matmul(s[:, 0:nk], self.tt[g * HD:(g + 1) * HD, T_NQ + r, qt * P:(qt + 1) * P], keys,
                              start=False, stop=True, skip_group_check=True).then_inc(qk_done, 1)
                if 1 <= u <= U:
                    w = u - 1
                    qt, br, h = units[w]
                    pe.wait_ge(exp_done, w + 1)
                    if w >= 1:
                        pe.wait_ge(*copied_of(w - 1))
                    k = 16 if br == 0 else P
                    for b in range(1 if br == 0 else qt + 1):
                        ins = pe.transpose(self.ps[0:k, 2, b * P:(b + 1) * P], prob[w % 2][:, b * P:b * P + k],
                                           self.c("ident"))
                    ins.then_inc(turned, 1)
                if u >= 2:
                    w = u - 2
                    qt, br, h = units[w]
                    g, grp = h // 4, w // 8
                    pe.wait_ge(*copied_of(w))
                    if h == 0 and grp >= 1:
                        pe.wait_ge(o_read, grp)
                    out = self.ps[:, 3, h * HD:(h + 1) * HD]
                    if br == 0:
                        ins = pe.matmul(out, pt[w % 2][0:16, 0:P], self.vcmp[:, g * HD:(g + 1) * HD], start=True,
                                        stop=True, skip_group_check=True)
                    else:
                        v0 = (S_V, W_V)[br - 1] + g * HD
                        for b in range(qt + 1):
                            ins = pe.matmul(out, pt[w % 2][:, b * P:(b + 1) * P], pj[:, b, v0:v0 + HD],
                                            start=(b == 0), stop=(b == qt), skip_group_check=True)
                    ins.then_inc(pv_done, 1)
                yield

        def copy_probs(eng, w):
            qt, br, _ = units[w]
            eng.wait_ge(turned, w + 1)
            if w >= 2:
                eng.wait_ge(pv_done, w - 1)
            k, n = (16, P) if br == 0 else (P, (qt + 1) * P)
            dst, src = pt[w % 2][0:k, 0:n], self.ps[0:k, 2, 0:n]
            if w % 2 == 0:
                eng.tensor_copy(dst, src).then_inc(copied[0], 1)
            else:
                eng.activation(dst, src, ACT.Copy).then_inc(copied[1], 1)

        def act_steps(act):
            for u in range(U + 2):
                if u < U:
                    qt, br, h = units[u]
                    nk, grp = nkeys(qt, br), u // 8
                    act.wait_ge(nmax_ready, u + 1)
                    if u >= 2:
                        act.wait_ge(turned, u - 1)
                    if h == 0 and grp >= 2:
                        act.wait_ge(o_read, grp - 1)
                    act.activation(prob[u % 2][:, 0:nk], self.ps[:, u % 2, 0:nk], ACT.Exp, bias=nmax[u % 2],
                                   accum_out=rsum[grp % 2][:, h:h + 1]).then_inc(exp_done, 1)
                if 1 <= u <= U and (u - 1) % 2 == 1:
                    copy_probs(act, u - 1)
                yield

        def dve_steps(dve):
            link = self.linker(dve, "ns_dve_chain")
            for u in range(U + 2):
                if u < U:
                    qt, br, h = units[u]
                    dve.wait_ge(qk_done, u + 1)
                    if u >= 2:
                        dve.wait_ge(exp_done, u - 1)
                    link(dve.tensor_reduce(nmax[u % 2], self.ps[:, u % 2, 0:nkeys(qt, br)], AXX, ALU.max))
                    dve.tensor_scalar(nmax[u % 2], nmax[u % 2], -1.0, None, ALU.mult).then_inc(nmax_ready, 1)
                if 1 <= u <= U and (u - 1) % 2 == 0:
                    copy_probs(dve, u - 1)
                if u >= 2 and (u - 2) % 8 == 7:
                    w = u - 2
                    qt, br, _ = units[w]
                    grp = w // 8
                    gate = self.gates[:, qt, :].rearrange("p (h c) -> p h c", c=3)[:, :, br]
                    dve.wait_ge(exp_done, w + 1)
                    link(dve.reciprocal(wgt, rsum[grp % 2]))
                    if br == 0 and qt == 0:
                        link(dve.tensor_scalar(wgt, wgt, self.c("cmp_any"), None, ALU.mult))
                    link(dve.tensor_tensor(wgt, wgt, gate, ALU.mult))
                    dve.wait_ge(pv_done, w + 1)
                    acc = pj[:, qt, N_Q:N_Q + 512].rearrange("p (r g d) -> p g r d", r=4, g=2)
                    src = self.ps[:, 3, :].rearrange("p (g r d) -> p g r d", g=2, r=4)
                    wb = wgt.rearrange("p (g r) -> p g r", g=2).unsqueeze(3).broadcast_to([P, 2, 4, HD])
                    ot = otmp.rearrange("p (g r d) -> p g r d", g=2, r=4)
                    if br == 0:
                        dve.tensor_tensor(acc, src, wb, ALU.mult).then_inc(o_read, 1)
                        dve.wait_ge(o_read, grp + 1)
                    else:
                        dve.tensor_tensor(ot, src, wb, ALU.mult).then_inc(o_read, 1)
                        dve.wait_ge(o_read, grp + 1)
                        link(dve.tensor_tensor(acc, acc, ot, ALU.add))
                yield

        return {"pe": pe_steps, "act": act_steps, "dve": dve_steps}

    def sample_cached(self):
        l, pj, ident = self.l, self.proj, self.c("ident")
        sem = self.sem
        turned, scored, pooled = sem("sk_turned"), sem("sk_scored"), sem("sk_pooled")
        copied = [sem("sk_copied_dve"), sem("sk_copied_act")]
        q_cleared, q_built, win_read = sem("sk_q_cleared"), sem("sk_q_built"), sem("sk_win_read")
        multiplied, z_read = sem("sk_multiplied"), sem("sk_z_summed")
        self.q_spread = sem("sk_q_spread")
        weighted, summed, pool_copied, mapped, map_copied, few_mm, few_read = (
            sem(n) for n in ("sk_weighted", "sk_summed", "sk_pool_copied", "sk_mapped", "sk_map_copied", "sk_few",
                             "sk_few_read"))
        slc_read, z_ready, cum_added = sem("sx_slc_read"), sem("sx_z"), sem("sx_cum_added")
        cmax, cexp, c_norm, imp_mm = sem("sx_cmp_max"), sem("sx_cmp_exp"), sem("sx_cmp_norm"), sem("sx_importance")
        w_max, w_exp, s_max, s_exp = sem("sx_win_max"), sem("sx_win_exp"), sem("sx_slc_max"), sem("sx_slc_exp")
        abs_r, e_r, ln_r, l_r, cum_r, w_r = (sem(n) for n in ("sx_abs", "sx_e", "sx_ln", "sx_softplus", "sx_cum",
                                                              "sx_sb_w"))
        p_ready, pt_done, pt_read = sem("sx_probs"), sem("sx_pt"), sem("sx_pt_read")
        v_weighted, v_summed, v_pooled, v_pool_copied, v_mapped, v_map_copied, v_item_done, all_done, kept, picked = (
            sem(n) for n in ("sv_weighted", "sv_summed", "sv_pooled", "sv_pool_copied", "sv_mapped",
                             "sv_map_copied", "sv_item_done", "sv_all_done", "sv_kept", "sv_picked"))
        opened = sem("sx_zeroed")
        self.freed[IT_KW] = ((turned, NB),)
        self.freed[IT_VW] = ((v_item_done, 1),)
        for b in range(NB):
            self.freed[IT_K + b] = ((turned, NB + 2 * (b + 1)), (weighted, b + 1), (multiplied, 2 * (b + 1)))
            self.freed[IT_V + b] = ((v_item_done, b + 2), (v_weighted, b + 1))

        scr = self.scr
        kt = [scr[:, 0:512], scr[:, 512:1024]]
        kw = scr[:, 1024:2048]
        kw_sum = scr[:, 2048:2176]
        plk, kct = scr[:, 2048:2304], scr[:, 2304:2560]
        R = NB * 8
        xs = self.xt[:, 2560:4160]
        pslc, pwin = xs[0:R, 0:1025], xs[0:R, 1026:1539]
        d_slc, d_win = scr[0:R, 2944:3008], scr[0:R, 3008:3072]
        pcmp, few = self.few[0:R, 0:32], self.few[0:R, 32:34]
        imp, t16, pen = self.few[0:R, 34:50], self.few[0:R, 50:66], self.few[0:R, 66:82]
        masked = scr[0:R, 2048:2304]
        z, lsb, esb = scr[:, 2560:2816], scr[:, 2304:2560], scr[:, 0:256]
        pt_slc = scr[:, 0:512]
        pt_win = scr[:, 512:768]
        w_sb = scr[:, 2048:2304]
        vw_sum = scr[:, 2432:2560]
        sm = lambda i: self.small[0:R, 40 + i:41 + i]
        gt = self.gate_rows
        cum = self.ps[:, 5, 0:256]
        self.o_sample = scr[:, 960:1008]
        unused = self.tt[:, 0:8, :].rearrange("p j t -> p (j t)")
        prod = [unused[:, 0:1024], unused[:, 1024:2048]]
        self.q_everywhere = unused[:, 2048:4096]
        pcmp_own = unused[0:R, 0:256]
        p_new = unused[0:NB, 256:768]
        pt_cmp = unused[:, 768:1024]
        plv = [unused[:, 1024:1152], unused[:, 1152:1280]]
        vc = [unused[:, 1280:1408], unused[:, 1408:1536]]
        o_kept = unused[:, 1536:2304]
        out_sb = lambda b, m: self.ps[32 * (b % 4):32 * (b % 4) + m, 4 + b // 4, 0:256]
        out_nsa = lambda b, m: self.ps[32 * (b % 4):32 * (b % 4) + m, 4 + b // 4, 256:384]
        q_slc = self.q_wide[:, 0:512].rearrange("p (b n) -> p b n", b=NB)

        units = []
        for b in range(NB):
            s = self.slot(IT_KW)
            units.append((IT_KW, [s[:, (b * 4 + j) * P:(b * 4 + j + 1) * P] for j in range(4)], 6, b, None))
        for b in range(NB):
            s = self.slot(IT_K + b)
            for half in range(2):
                units.append((IT_K + b, [s[:, 2048 + i * P:2048 + (i + 1) * P]
                                         for i in range(4 * half, 4 * half + 4)], 4 + half, b,
                              b if half == 1 else None))
        U = len(units)

        def key_copied(u):
            return copied[u % 2], u // 2 + 1

        def pe_steps(pe):
            for u in range(U + 1):
                if u < U:
                    item, pieces = units[u][:2]
                    self.wait_item(pe, item, (1,))
                    if u >= 1:
                        pe.wait_ge(*key_copied(u - 1))
                    for j, piece in enumerate(pieces):
                        ins = pe.transpose(self.ps[:, 7, j * P:(j + 1) * P], piece, ident)
                    ins.then_inc(turned, 1)
                if u == 1:
                    pe.wait_ge(q_built, 1)
                if u >= 1:
                    w = u - 1
                    _, _, bank, b, pool_b = units[w]
                    pe.wait_ge(*key_copied(w))
                    pe.matmul(self.ps[0:R, bank, :], q_slc[:, b, :], kt[w % 2], start=(b == 0), stop=(b == NB - 1),
                              skip_group_check=True).then_inc(scored, 1)
                    if pool_b is not None:
                        if pool_b == 0:
                            pe.wait_ge(win_read, 1)
                        pe.wait_ge(summed, pool_b + 1)
                        pe.matmul(self.ps[:, 6, pool_b * 32:(pool_b + 1) * 32], kw_sum, self.c("blk_ind32"),
                                  start=True, stop=True, skip_group_check=True).then_inc(pooled, 1)
                yield
            pe.wait_ge(pool_copied, 1)
            pe.matmul(self.ps[:, 6, 256:512], self.phi_k[:], plk, start=True, stop=True,
                      skip_group_check=True).then_inc(mapped, 1)
            yield
            q64 = self.q_nsa[:].rearrange("p b h -> p (b h)")
            pe.wait_ge(map_copied, 1)
            pe.matmul(self.ps[0:R, 6, 0:256], q64, kct, start=True, stop=True, skip_group_check=True)
            for j, blk in enumerate((T_SK, T_WK)):
                ins = pe.matmul(self.ps[0:R, 6, 256 + 8 * j:264 + 8 * j], q64, self.tt[:, blk, SEQ:TOK], start=True,
                                stop=True, skip_group_check=True)
            ins.then_inc(few_mm, 1)
            yield
            yield
            pe.wait_ge(c_norm, 1)
            pe.wait_ge(few_read, 1)
            pe.matmul(self.ps[0:R, 6, 0:16], self.c("grp")[0:R], imp, start=True, stop=True,
                      skip_group_check=True).then_inc(imp_mm, 1)
            yield
            pe.wait_ge(l_r, 1)
            pe.wait_ge(slc_read, 1)
            for i in range(7, -1, -1):
                row = lsb[:, i * 32:(i + 1) * 32].unsqueeze(1)
                ins = pe.matmul(cum[:, 0:(i + 1) * 32], self.c("neg_suffix"), row.broadcast_to([P, i + 1, 32]),
                                start=(i == 7), stop=True, skip_group_check=True)
                if i < 7:
                    ins = pe.matmul(cum[:, (i + 1) * 32:256], self.c("neg_later"), row.broadcast_to([P, 7 - i, 32]),
                                    start=False, stop=True, skip_group_check=True)
            ins.then_inc(cum_r, 1)
            yield
            pe.wait_ge(p_ready, 1)
            for i in range(8):
                ins = pe.transpose(self.ps[:, 7, i * R:(i + 1) * R], pslc[:, i * P:(i + 1) * P], ident[0:R, 0:R])
            ins.then_inc(pt_done, 1)
            yield
            pe.wait_ge(pt_read, 1)
            for j in range(4):
                pe.transpose(self.ps[:, 7, j * R:(j + 1) * R], pwin[:, j * P:(j + 1) * P], ident[0:R, 0:R])
            for half in range(2):
                pe.transpose(self.ps[:, 7, 256 + half * R:256 + (half + 1) * R],
                             pcmp_own[:, half * P:(half + 1) * P], ident[0:R, 0:R])
            for j, dg in enumerate((d_slc, d_win)):
                ins = pe.matmul(self.ps[0:NB, 7, 384 + j * R:384 + (j + 1) * R], self.c("seq_ind")[0:R], dg,
                                start=True, stop=True, skip_group_check=True)
            ins.then_inc(pt_done, 1)
            yield
            pe.wait_ge(pt_read, 2)
            pe.wait_ge(w_r, 1)
            zero_row = self.c("neg_later")[0:1]
            for half in range(2):
                pe.matmul(self.ps[:, 4 + half, 0:384], zero_row, zero_row.unsqueeze(1).broadcast_to([1, 3, P]),
                          start=True, stop=False, skip_group_check=True)
                for k, v0 in enumerate((S_V, W_V)):
                    pe.matmul(self.ps[:, 4 + half, 256:384], p_new[:, k * 256 + half * P:k * 256 + (half + 1) * P],
                              pj[0:NB, 4, v0:v0 + P], start=False, stop=False, skip_group_check=True)
            self.wait_item(pe, IT_VW)
            w = self.slot(IT_VW)
            for b in range(NB):
                for j in range(4):
                    ins = pe.matmul(out_nsa(b, 8), pt_win[:, j * 64 + b * 8:j * 64 + b * 8 + 8],
                                    w[:, (b * 4 + j) * P:(b * 4 + j + 1) * P], start=False, stop=False,
                                    skip_group_check=True)
                if b == 3:
                    yield
            ins.then_inc(v_item_done, 1)
            yield
            for step in range(2 * NB + 2):
                b, part = divmod(step, 2)
                half = b // 4 - 1
                if b % 4 == 0 and half >= 0 and part == 0:
                    pe.wait_ge(v_pool_copied, half + 1)
                    pe.matmul(self.ps[:, 7, 0:P], plv[half], self.phi_v[:], start=True, stop=True,
                              skip_group_check=True).then_inc(v_mapped, 1)
                if b % 4 == 0 and half >= 0 and part == 1:
                    pe.wait_ge(v_map_copied, half + 1)
                    ins = pe.matmul(self.ps[:, 4 + half, 256:384], pt_cmp[:, half * P:(half + 1) * P], vc[half],
                                    start=False, stop=(half == 1), skip_group_check=True)
                    if half == 1:
                        ins.then_inc(all_done, 1)
                if b < NB:
                    self.wait_item(pe, IT_V + b, (0, 1))
                    w = self.slot(IT_V + b)
                    for i in range(4 * part, 4 * part + 4):
                        pe.matmul(out_sb(b, 4), w_sb[:, i * 32 + b * 4:i * 32 + b * 4 + 4],
                                  w[:, i * 256:(i + 1) * 256], start=False, stop=False, skip_group_check=True)
                        ins = pe.matmul(out_nsa(b, 8), pt_slc[:, i * 64 + b * 8:i * 64 + b * 8 + 8],
                                        w[:, 2048 + i * P:2048 + (i + 1) * P], start=False, stop=False,
                                        skip_group_check=True)
                    if part == 1:
                        ins.then_inc(v_item_done, 1)
                        pe.wait_ge(v_summed, b + 1)
                        if b == 4:
                            pe.wait_ge(v_pool_copied, 1)
                        pe.matmul(self.ps[:, 6, b * 32:(b + 1) * 32], vw_sum, self.c("blk_ind32"), start=True,
                                  stop=True, skip_group_check=True).then_inc(v_pooled, 1)
                yield
            yield
            pe.wait_ge(kept, 1)
            for half in range(2):
                k0, c0 = half * 384, half * 24
                for x in range(2):
                    pe.matmul(self.ps[:, 6, c0 + 4 * x:c0 + 4 * x + 4], o_kept[:, k0 + x * P:k0 + (x + 1) * P],
                              self.c("blk_ind"), start=True, stop=True, skip_group_check=True)
                ins = pe.matmul(self.ps[:, 6, c0 + 8:c0 + 24], o_kept[:, k0 + 256:k0 + 384], self.c("pick_head"),
                                start=True, stop=True, skip_group_check=True)
            ins.then_inc(picked, 1)
            yield

        def copy_keys(eng, u):
            eng.wait_ge(turned, u + 1)
            if u >= 2:
                eng.wait_ge(scored, u - 1)
            if u % 2 == 0:
                eng.tensor_copy(kt[0], self.ps[:, 7, :]).then_inc(copied[0], 1)
            else:
                eng.activation(kt[1], self.ps[:, 7, :], ACT.Copy).then_inc(copied[1], 1)

        def sum_products(dve, b, half):
            dve.wait_ge(multiplied, 2 * b + half + 1)
            dst = z.rearrange("p (i b h) -> p i b h", i=8, b=NB)[:, 4 * half:4 * half + 4, b, :]
            dve.tensor_reduce(dst, prod[half].rearrange("p (i h d) -> p i h d", i=4, h=4), AXX, ALU.add
                              ).then_inc(z_read, 1)

        def dve_steps(dve):
            link = self.linker(dve, "sx_dve_chain")
            for u in range(U + 1):
                if u < U and u % 2 == 0:
                    copy_keys(dve, u)
                if u == NB:
                    dve.wait_ge(scored, NB)
                    dve.tensor_copy(pwin[:, 0:512], self.ps[0:R, 6, :]).then_inc(win_read, 1)
                b, odd = divmod(u - NB, 2)
                if u > NB and odd == 0:
                    sum_products(dve, b - 1, 1)
                if u > NB and odd == 1:
                    self.wait_item(dve, IT_K + b, (2,))
                    dve.tensor_tensor(kw.rearrange("p (i g d) -> p i g d", i=8, g=2),
                                      self.slot(IT_K + b)[:, 3072:4096].rearrange("p (i g d) -> p i g d", i=8, g=2),
                                      self.pos8_k[:].unsqueeze(2).broadcast_to([P, 8, 2, HD]), ALU.mult
                                      ).then_inc(weighted, 1)
                    dve.wait_ge(weighted, b + 1)
                    if b >= 1:
                        dve.wait_ge(pooled, b)
                    dve.tensor_reduce(kw_sum, kw.rearrange("p (i n) -> p n i", i=8), AXX, ALU.add
                                      ).then_inc(summed, 1)
                    sum_products(dve, b, 0)
                yield
            dve.wait_ge(pooled, NB)
            dve.tensor_copy(plk, self.ps[:, 6, 0:256]).then_inc(pool_copied, 1)
            dve.wait_ge(scored, U)
            dve.wait_ge(z_read, 2 * NB)
            dve.tensor_scalar(z, z, HD ** -0.5, None, ALU.mult).then_inc(z_ready, 1)
            dve.memset(p_new, 0.0)
            dve.memset(pt_cmp, 0.0).then_inc(opened, 1)
            dve.tensor_copy(pslc[:, 0:512], self.ps[0:R, 4, :])
            dve.tensor_copy(pslc[:, 512:1024], self.ps[0:R, 5, :]).then_inc(slc_read, 1)
            yield
            dve.wait_ge(mapped, 1)
            dve.tensor_copy(kct, self.ps[:, 6, 256:512]).then_inc(map_copied, 1)
            yield
            dve.wait_ge(few_mm, 1)
            own = self.c("seq_ind")[0:R]
            link(dve.tensor_tensor(masked.rearrange("p (b n) -> p b n", b=NB),
                                   self.ps[0:R, 6, 0:256].rearrange("p (b n) -> p b n", b=NB),
                                   own.unsqueeze(2).broadcast_to([R, NB, 32]), ALU.mult))
            link(dve.tensor_reduce(pcmp, masked.rearrange("p (b n) -> p n b", b=NB), AXX, ALU.add))
            link(dve.tensor_tensor(masked[:, 0:16].rearrange("p (j b) -> p j b", j=2),
                                   self.ps[0:R, 6, 256:272].rearrange("p (j b) -> p j b", j=2),
                                   own.unsqueeze(1).broadcast_to([R, 2, NB]), ALU.mult))
            dve.tensor_reduce(few, masked[:, 0:16].rearrange("p (j b) -> p j b", j=2), AXX, ALU.add
                              ).then_inc(few_read, 1)
            dve.wait_ge(few_read, 1)
            link(dve.tensor_reduce(sm(0), pcmp, AXX, ALU.max))
            dve.tensor_scalar(sm(1), sm(0), -1.0, None, ALU.mult).then_inc(cmax, 1)
            yield
            link(dve.tensor_copy(pwin[:, 512:513], few[:, 1:2]))
            link(dve.tensor_reduce(sm(2), pwin, AXX, ALU.max))
            dve.tensor_scalar(sm(3), sm(2), -1.0, None, ALU.mult).then_inc(w_max, 1)
            dve.wait_ge(cexp, 1)
            link(dve.reciprocal(sm(4), sm(5)))
            link(dve.tensor_scalar(pcmp, pcmp, sm(4), None, ALU.mult))
            dve.tensor_reduce(imp, pcmp.rearrange("p (n c) -> p n c", c=2), AXX, ALU.add).then_inc(c_norm, 1)
            dve.wait_ge(c_norm, 1)
            link(dve.tensor_scalar(pcmp, pcmp, gt[:, 0:1], None, ALU.mult))
            link(dve.tensor_tensor(pcmp_own.rearrange("p (b n) -> p b n", b=NB),
                                   pcmp.unsqueeze(1).broadcast_to([R, NB, 32]),
                                   own.unsqueeze(2).broadcast_to([R, NB, 32]), ALU.mult))
            dve.wait_ge(ln_r, 1)
            dve.scalar_tensor_tensor(out=lsb, in0=z, scalar=0.0, in1=esb, op0=ALU.max, op1=ALU.add
                                     ).then_inc(l_r, 1)
            yield
            dve.wait_ge(imp_mm, 1)
            link(dve.tensor_copy(imp, self.ps[0:R, 6, 0:16]))
            link(dve.tensor_reduce(sm(6), imp[:, 1:16], AXX, ALU.min))
            link(dve.tensor_scalar(t16[:, 1:16], imp[:, 1:16], sm(6), None, ALU.is_le))
            link(dve.tensor_tensor(t16[:, 1:16], t16[:, 1:16], self.c("blk_idx")[0:R, 1:16], ALU.mult))
            link(dve.tensor_reduce(sm(7), t16[:, 1:16], AXX, ALU.max))
            link(dve.tensor_scalar(pen, self.c("blk_idx")[0:R], sm(7), NEG, ALU.is_equal, ALU.mult))
            dve.wait_ge(slc_read, 1)
            pv = pslc[:, 0:1024].rearrange("p (i n q) -> p i n q", i=8, n=16)
            link(dve.tensor_tensor(pv, pv, pen.unsqueeze(1).unsqueeze(3).broadcast_to([R, 8, 16, 8]), ALU.add))
            link(dve.tensor_copy(pslc[:, 1024:1025], few[:, 0:1]))
            link(dve.tensor_reduce(sm(8), pslc, AXX, ALU.max))
            dve.tensor_scalar(sm(9), sm(8), -1.0, None, ALU.mult).then_inc(s_max, 1)
            yield
            dve.wait_ge(cum_r, 1)
            dve.tensor_tensor(z, z, cum, ALU.add).then_inc(cum_added, 1)
            dve.wait_ge(w_exp, 1)
            link(dve.reciprocal(sm(10), sm(11)))
            link(dve.tensor_tensor(sm(10), sm(10), gt[:, 2:3], ALU.mult))
            link(dve.tensor_scalar(pwin, pwin, sm(10), None, ALU.mult))
            dve.wait_ge(s_exp, 1)
            link(dve.reciprocal(sm(13), sm(14)))
            link(dve.tensor_tensor(sm(13), sm(13), gt[:, 1:2], ALU.mult))
            link(dve.tensor_scalar(pslc, pslc, sm(13), None, ALU.mult))
            dve.tensor_scalar(d_slc, ident[0:R, 0:R], pslc[:, 1024:1025], None, ALU.mult)
            dve.tensor_scalar(d_win, ident[0:R, 0:R], pwin[:, 512:513], None, ALU.mult).then_inc(p_ready, 1)
            yield
            dve.wait_ge(pt_done, 1)
            dve.tensor_copy(pt_slc, self.ps[:, 7, :]).then_inc(pt_read, 1)
            yield
            dve.wait_ge(pt_done, 2)
            dve.tensor_copy(pt_win, self.ps[:, 7, 0:256])
            dve.wait_ge(opened, 1)
            for half in range(2):
                dve.tensor_copy(
                    pt_cmp[:, half * P:(half + 1) * P].rearrange("p (b y) -> p b y", y=32)[:, :, 0:8],
                    self.ps[:, 7, 256 + half * 96:288 + half * 96].rearrange("p (b h) -> p b h", b=4))
            dve.tensor_copy(p_new.rearrange("p (k b y) -> p k b y", k=2, y=32)[:, :, :, 0:8],
                            self.ps[0:NB, 7, 384:512].rearrange("p (k b h) -> p k b h", k=2, b=NB)
                            ).then_inc(pt_read, 1)
            yield
            yield
            for step in range(2 * NB + 2):
                b, part = divmod(step, 2)
                if part == 0 and b < NB:
                    dve.wait_ge(v_weighted, b + 1)
                    if b >= 1:
                        dve.wait_ge(v_pooled, b)
                    dve.tensor_reduce(vw_sum, kw.rearrange("p (i n) -> p n i", i=8), AXX, ALU.add
                                      ).then_inc(v_summed, 1)
                yield
            dve.wait_ge(all_done, 1)
            own_head = self.c("own_head").unsqueeze(2).broadcast_to([P, 6, HD])
            for half in range(2):
                ins = dve.tensor_tensor(o_kept[:, half * 384:(half + 1) * 384].rearrange("p (j d) -> p j d", j=6),
                                        self.ps[:, 4 + half, 0:384].rearrange("p (j d) -> p j d", j=6), own_head,
                                        ALU.mult)
            ins.then_inc(kept, 1)
            yield
            yield
            dve.wait_ge(picked, 1)
            dve.tensor_copy(self.o_sample, self.ps[:, 6, 0:48])
            yield

        def act_steps(act):
            for u in range(U + 1):
                if u < U and u % 2 == 1:
                    copy_keys(act, u)
                yield
            yield
            act.wait_ge(scored, U)
            act.wait_ge(z_ready, 1)
            act.activation(esb, z, ACT.Abs).then_inc(abs_r, 1)
            act.wait_ge(abs_r, 1)
            act.activation(esb, esb, ACT.Exp, scale=-1.0).then_inc(e_r, 1)
            yield
            act.wait_ge(e_r, 1)
            act.activation(esb, esb, ACT.Ln, bias=1.0).then_inc(ln_r, 1)
            act.wait_ge(cmax, 1)
            act.activation(pcmp, pcmp, ACT.Exp, bias=sm(1), accum_out=sm(5)).then_inc(cexp, 1)
            yield
            act.wait_ge(w_max, 1)
            act.activation(pwin, pwin, ACT.Exp, bias=sm(3), accum_out=sm(11)).then_inc(w_exp, 1)
            yield
            act.wait_ge(s_max, 1)
            act.activation(pslc, pslc, ACT.Exp, bias=sm(9), accum_out=sm(14)).then_inc(s_exp, 1)
            yield
            act.wait_ge(cum_added, 1)
            act.activation(w_sb, z, ACT.Exp).then_inc(w_r, 1)
            yield
            yield
            yield
            yield
            for step in range(2 * NB + 2):
                b, part = divmod(step, 2)
                if b in (3, 7) and part == 1:
                    act.wait_ge(v_pooled, b + 1)
                    act.activation(plv[b // 4], self.ps[:, 6, b // 4 * P:(b // 4 + 1) * P], ACT.Copy
                                   ).then_inc(v_pool_copied, 1)
                if b in (4, 8) and part == 0:
                    act.wait_ge(v_mapped, b // 4)
                    act.activation(vc[b // 4 - 1], self.ps[:, 7, 0:P], ACT.Copy).then_inc(v_map_copied, 1)
                yield

        def pool_steps(pool):
            pool.memset(self.q_wide[:], 0.0).then_inc(q_cleared, 1)
            pool.wait_ge(q_cleared, 1)
            for b in range(NB):
                ins = pool.tensor_copy(q_slc[:, b, 8 * b:8 * b + 8], self.q_nsa[:, b, :])
            ins.then_inc(q_built, 1)
            for b in range(NB):
                self.wait_item(pool, IT_K + b, (0,))
                if b == 0:
                    pool.wait_ge(self.q_spread, 16)
                for half in range(2):
                    if b >= 1:
                        pool.wait_ge(z_read, 2 * b - 1 + half)
                    pool.tensor_tensor(prod[half].rearrange("p (i n) -> p i n", i=4),
                                       self.slot(IT_K + b)[:, half * 1024:(half + 1) * 1024].rearrange(
                                           "p (i n) -> p i n", i=4),
                                       self.q_everywhere[:, b * 256:(b + 1) * 256].unsqueeze(1).broadcast_to(
                                           [P, 4, 256]), ALU.mult).then_inc(multiplied, 1)
                if b + 2 < NB:
                    self.gather(pool, IT_K + b + 2)
                yield
            self.gather(pool, IT_V)
            self.gather(pool, IT_V + 1)
            for b in range(NB):
                self.wait_item(pool, IT_V + b, (2,))
                if b == 0:
                    pool.wait_ge(summed, NB)
                if b >= 1:
                    pool.wait_ge(v_summed, b)
                pool.tensor_tensor(kw.rearrange("p (i g d) -> p i g d", i=8, g=2),
                                   self.slot(IT_V + b)[:, 3072:4096].rearrange("p (i g d) -> p i g d", i=8, g=2),
                                   self.pos8_v[:].unsqueeze(2).broadcast_to([P, 8, 2, HD]), ALU.mult
                                   ).then_inc(v_weighted, 1)
                if b + 2 < NB:
                    self.gather(pool, IT_V + b + 2)
                yield

        return {"pe": pe_steps, "act": act_steps, "dve": dve_steps, "pool": pool_steps}

    def output_projection(self):
        nc, l, pj = self.nc, self.l, self.proj
        turned, t_copied, mm_done, added, s_placed = (
            self.sem(s) for s in ("op_turned", "op_copied", "op_mm", "op_added", "op_sample_placed"))
        for n in range(2):
            self.freed[IT_WO + n] = ((mm_done, TILES * (n + 1)),)
        src_cols = [SB_Q, SB_Q + P, R_Q, R_Q + P] + [N_Q + j * P for j in range(4)]
        with nc.Block() as block:
            @block.sync
            def _(sp):
                self.issue_until(sp, l, IT_UP + SLOTS)
                sp.wait_ge(self.shift_done, 32)

            @block.tensor
            def _(pe):
                ident = self.c("ident")
                for t in range(4):
                    if t >= 2:
                        pe.wait_ge(t_copied, 2 * (t - 1))
                    for k in range(KD):
                        ins = pe.transpose(self.ps[:, 2 * (t % 2) + k // 4, (k % 4) * P:(k % 4 + 1) * P],
                                           pj[:, t, src_cols[k]:src_cols[k] + P], ident)
                    ins.then_inc(turned, 1)
                pe.wait_ge(t_copied, 6)
                for x in range(2):
                    ins = pe.transpose(self.ps[:, 0, x * P:x * P + NB], pj[0:NB, 4, R_Q + x * P:R_Q + (x + 1) * P],
                                       ident[0:NB, 0:NB])
                ins.then_inc(turned, 1)
                pe.wait_ge(t_copied, 9)
                pe.wait_ge(s_placed, 1)
                for n in range(2):
                    self.wait_item(pe, IT_WO + n)
                    w = self.slot(IT_WO + n).rearrange("p (k n) -> p k n", k=KD)
                    for t in range(TILES):
                        u, m = n * TILES + t, rows(t)
                        if u >= 4:
                            pe.wait_ge(added, u - 3)
                        for k in range(KD):
                            ins = pe.matmul(self.ps[0:m, 4 + u % 4, :], self.xtv[:, k, cols(t)], w[:, k, :],
                                            start=(k == 0), stop=(k == KD - 1))
                        ins.then_inc(mm_done, 1)

            @block.gpsimd
            def _(pool):
                src = self.o_sample.rearrange("p (x j b) -> p j x b", x=2, j=6)
                for blocks, part in ((slice(0, 2), src[:, 0:2]), (slice(4, 8), src[:, 2:6])):
                    ins = pool.tensor_copy(self.xtv[:, blocks, SEQ:TOK].rearrange("p j (x b) -> p j x b", x=2), part)
                ins.then_inc(s_placed, 1)

            @block.scalar
            def _(act):
                for t in range(4):
                    act.wait_ge(turned, t + 1)
                    for j in range(2):
                        act.activation(self.xtv[:, 4 * j:4 * j + 4, cols(t)],
                                       self.ps[:, 2 * (t % 2) + j, :].rearrange("p (k n) -> p k n", k=4), ACT.Copy
                                       ).then_inc(t_copied, 1)
                act.wait_ge(turned, 5)
                act.activation(self.xtv[:, 2:4, SEQ:TOK],
                               self.ps[:, 0, 0:256].rearrange("p (k n) -> p k n", k=2)[:, :, 0:NB], ACT.Copy
                               ).then_inc(t_copied, 1)

            @block.vector
            def _(dve):
                for n in range(2):
                    for t in range(TILES):
                        u, m = n * TILES + t, rows(t)
                        dve.wait_ge(mm_done, u + 1)
                        x = self.x_res[0:m, t, n * 512:(n + 1) * 512]
                        dve.tensor_tensor(x, x, self.ps[0:m, 4 + u % 4, :], ALU.add).then_inc(added, 1)

    def mlp_up(self):
        nc, l = self.nc, self.l
        mm_done, relu_done, sq_done = (self.sem(s) for s in ("up_mm", "up_relu", "up_square"))
        H = TOK // 2
        for c in range(8):
            self.freed[IT_UP + c] = ((mm_done, 4 * (c + 1)),)
        rbuf = [self.scr[:, 0:TOK], self.scr[:, TOK:2 * TOK]]
        with nc.Block() as block:
            @block.sync
            def _(sp):
                self.issue_until(sp, l, IT_DN + SLOTS)

            @block.tensor
            def _(pe):
                for u in range(FF // P):
                    c, f = divmod(u, 4)
                    if f == 0:
                        self.wait_item(pe, IT_UP + c)
                    if u >= 4:
                        pe.wait_ge(relu_done, u - 3)
                    w = self.slot(IT_UP + c).rearrange("p (k n) -> p k n", k=KD)
                    for half in range(2):
                        for k in range(KD):
                            ins = pe.matmul(self.ps[:, 2 * (u % 4) + half, 0:H], w[:, k, f * P:(f + 1) * P],
                                            self.xtv[:, k, half * H:(half + 1) * H], start=(k == 0),
                                            stop=(k == KD - 1))
                    ins.then_inc(mm_done, 1)

            @block.scalar
            def _(act):
                for u in range(FF // P):
                    act.wait_ge(mm_done, u + 1)
                    if u >= 2:
                        act.wait_ge(sq_done, u - 1)
                    act.activation(rbuf[u % 2].rearrange("p (x n) -> p x n", x=2),
                                   self.ps[:, 2 * (u % 4):2 * (u % 4) + 2, 0:H], ACT.Relu).then_inc(relu_done, 1)

            @block.vector
            def _(dve):
                for u in range(FF // P):
                    dve.wait_ge(relu_done, u + 1)
                    dve.tensor_tensor(self.hid[:, u, :], rbuf[u % 2], rbuf[u % 2], ALU.mult).then_inc(sq_done, 1)

    def mlp_down(self):
        nc, l = self.nc, self.l
        part, f_done, copied, turned, added = (self.sem(s) for s in ("dn_part", "dn_features", "dn_copied",
                                                                     "dn_turned", "dn_added"))
        H = TOK // 2
        for i in range(8):
            self.freed[IT_DN + i] = ((part, i + 1),)
        with nc.Block() as block:
            @block.sync
            def _(sp):
                self.issue_until(sp, l, N_ITEMS)

            @block.tensor
            def _(pe):
                for n in range(2):
                    for q in range(4):
                        i = IT_DN + 4 * n + q
                        self.wait_item(pe, i)
                        w = self.slot(i).rearrange("p (k n) -> p k n", k=8)
                        for f in range(4):
                            if n == 1 and q == 0:
                                pe.wait_ge(added, f + 1)
                            for half in range(2):
                                for k in range(8):
                                    ins = pe.matmul(self.ps[:, 2 * f + half, 0:H], w[:, k, f * P:(f + 1) * P],
                                                    self.hid[:, q * 8 + k, half * H:(half + 1) * H],
                                                    start=(q == 0 and k == 0), stop=(q == 3 and k == 7),
                                                    skip_group_check=True)
                            if q == 3 and f < 3:
                                ins.then_inc(f_done, 1)
                        ins.then_inc(part, 1)
                    for f in range(4):
                        pe.wait_ge(copied, 4 * n + f + 1)
                        for t in range(TILES):
                            dst = self.ps[0:rows(t), 2 * f + t // 4, (t % 4) * P:(t % 4 + 1) * P]
                            ins = pe.transpose(dst, self.xtv[:, 4 * n + f, cols(t)], self.c("ident"))
                        ins.then_inc(turned, 1)

            @block.scalar
            def _(act):
                for n in range(2):
                    for f in range(4):
                        if f < 3:
                            act.wait_ge(f_done, 3 * n + f + 1)
                        else:
                            act.wait_ge(part, 4 * (n + 1))
                        act.activation(self.xtv[:, 4 * n + f, :].rearrange("p (x n) -> p x n", x=2),
                                       self.ps[:, 2 * f:2 * f + 2, 0:H], ACT.Copy).then_inc(copied, 1)

            @block.vector
            def _(dve):
                for u in range(8):
                    f = u % 4
                    dve.wait_ge(turned, u + 1)
                    x = self.x_res[:, 0:4, u * P:(u + 1) * P]
                    dve.tensor_tensor(x, x, self.ps[:, 2 * f, :].rearrange("p (t n) -> p t n", t=4), ALU.add)
                    x = self.x_res[0:NB, 4, u * P:(u + 1) * P]
                    dve.tensor_tensor(x, x, self.ps[0:NB, 2 * f + 1, 0:P], ALU.add).then_inc(added, 1)


_INS = ['x_prompt', 'x_sample', 'cache_sb_k', 'cache_sb_v', 'cache_cmp_k', 'cache_cmp_v', 'cache_slc_k',
        'cache_slc_v', 'state_win_k', 'state_win_v', 'state_ret', 'page_table', 'norm1_g', 'w_in', 'nsa_q_norm',
        'nsa_k_norm', 'cmp_pos_k', 'cmp_pos_v', 'cmp_w_k', 'cmp_w_v', 'w_out', 'norm2_g', 'w_up', 'w_down']
_OUTS = ([("y_prompt", (1, SEQ, D)), ("y_sample", (NB, 1, D))]
         + [(f"p_sb_{x}", (DEPTH, 1, SEQ, 4, HD)) for x in "kv"]
         + [(f"p_{n}_{x}", (DEPTH, 1, SEQ, 2, HD)) for n in ("cmp", "slc", "win") for x in "kv"]
         + [("p_ret", (DEPTH, 1, 4, HD, HD))]
         + [(f"s_sb_{x}", (DEPTH, NB, 1, 4, HD)) for x in "kv"]
         + [(f"s_{n}_{x}", (DEPTH, NB, 1, 2, HD)) for n in ("cmp", "slc") for x in "kv"]
         + [(f"s_win_{x}", (DEPTH, NB, WIN, 2, HD)) for x in "kv"]
         + [("s_ret", (DEPTH, NB, 4, HD, HD))])


def kernel(**inputs):
    import numpy as _np
    import concourse.bacc as _bacc
    from concourse import mybir as _mybir
    from concourse.bass_utils import run_bass_kernel_spmd as _run

    nc = _bacc.Bacc("TRN2", target_bir_lowering=False, num_devices=1)
    arrays, ins, outs = {}, {}, {}
    for name in _INS:
        a = _np.ascontiguousarray(inputs[name])
        arrays[f"in_{name}"] = a
        ins[name] = nc.dram_tensor(f"in_{name}", a.shape, _mybir.dt.from_np(a.dtype), kind="ExternalInput").ap()
    c = shape_constants()
    arrays["in_consts"] = c
    consts = nc.dram_tensor("in_consts", c.shape, _mybir.dt.from_np(c.dtype), kind="ExternalInput").ap()
    for name, shape in _OUTS:
        outs[name] = nc.dram_tensor(f"out_{name}", shape, F32, kind="ExternalOutput").ap()
    build(nc, ins, outs, consts)
    r = _run(nc, [arrays], core_ids=[0])
    return tuple(r.results[0][f"out_{name}"] for name, _ in _OUTS)
```

```python
import math
from contextlib import ExitStack

import numpy as np
import concourse.bass as bass
from concourse import mybir

F32 = mybir.dt.float32
BF16 = mybir.dt.bfloat16
I32 = mybir.dt.int32
ALU = mybir.AluOpType
ACT = mybir.ActivationFunctionType
AXX = mybir.AxisListType.X

P = 128
D = 1024
KD = D // P
SEQ, NB, DEPTH = 512, 8, 2
PAST, PAGE, NPAGE = 1024, 128, 8
HD = 64
TILES = SEQ // P + 1
TOK = SEQ + NB
FF = 4 * D
EPS = 1e-6
NEG = -1.0e30
WIN = 512
N_IN = 3096
SB_Q, SB_K, SB_V = 0, 256, 512
R_Q, R_K, R_V, R_G = 768, 1024, 1280, 1536
N_Q, C_K, C_V, S_K, S_V, W_K, W_V, N_G = 1792, 2304, 2432, 2560, 2688, 2816, 2944, 3072
T_SBQ, T_SBK, T_RQ, T_RK, T_NQ, T_SK, T_WK = 0, 2, 4, 6, 8, 12, 13
PACK = {0: 0, 1: 512, 3: 896, 2: 1024}
PACKED = 1280
IT_WIN, IT_KW, IT_K, IT_VW, IT_V, IT_WO, IT_UP, IT_DN, N_ITEMS = 0, 6, 7, 15, 16, 24, 26, 34, 42
CHUNKS = (3, 4, 5, 1, 2, 0)
SLOTS = 3
SLOT = 4096

CONST_COLS = [("ident", 128), ("neg_suffix", 128), ("neg_later", 128), ("neg_ones", 128), ("sb_mask", 128), ("ret_mask", 128),
              ("cos_r", TILES * 32), ("sin_r", TILES * 32), ("cos_n", TILES * 8), ("sin_n", TILES * 8),
              ("decay", TILES * 8), ("gam_last", 4), ("gam_one", 2), ("blk_ind", 4), ("blk_ind32", 32), ("sub_row", 1), ("grp", 64),
              ("seq_ind", 8), ("blk_idx", 16), ("cmp_any", 1), ("own_head", 6), ("own_row", 8), ("pick_head", 16),
              ("sb_neg", 128), ("nsa_neg", 128), ("cmp_neg", 64)]
CONST_AT = {}
_at = 0
for _n, _w in CONST_COLS:
    CONST_AT[_n] = (_at, _w)
    _at += _w
N_CONST = _at
N_KEEP = CONST_AT["sb_neg"][0]


def shape_constants():
    c = np.zeros((P, N_CONST), np.float32)

    def put(name, a):
        s, w = CONST_AT[name]
        c[:, s:s + w] = np.asarray(a, np.float32).reshape(P, w)

    i = np.arange(P)
    put("ident", np.eye(P))
    put("neg_suffix", -(i[:, None] >= i[None, :]).astype(np.float32))
    put("neg_later", -(i[:, None] > i[None, :]).astype(np.float32))
    put("neg_ones", -np.ones((P, P)))
    put("sb_mask", i[:, None] < i[None, :])
    put("ret_mask", i[:, None] <= i[None, :])
    put("sb_neg", np.where(i[:, None] < i[None, :], 0.0, NEG))
    put("nsa_neg", np.where(i[None, :] <= i[:, None], 0.0, NEG))
    pos = np.concatenate([np.arange(SEQ).reshape(4, P), np.full((1, P), PAST)]).astype(np.float32)
    for half, theta, cn, sn in ((32, 10000.0, "cos_r", "sin_r"), (8, 500000.0, "cos_n", "sin_n")):
        inv = np.exp(np.float32(-math.log(theta)) * np.arange(half, dtype=np.float32) / np.float32(half))
        ang = (pos[:, :, None] * inv.astype(np.float32)).astype(np.float32).transpose(1, 0, 2)
        put(cn, np.cos(ang))
        put(sn, np.sin(ang))
    lg = np.log1p(-np.exp2(-5.0 - np.arange(4)))
    dec = np.zeros((P, TILES, 8))
    for t in range(4):
        j = (t * P + i)[:, None]
        dec[:, t, 0:4] = np.exp(j * lg)
        dec[:, t, 4:8] = np.exp(-j * lg) / 8.0
    dec[:, 4, 0:4] = 1.0
    dec[:, 4, 4:8] = 1.0 / 8.0
    put("decay", dec)
    put("gam_last", np.broadcast_to(np.exp((SEQ - 1) * lg), (P, 4)))
    put("gam_one", np.exp(lg)[2 * np.arange(2)[None, :] + i[:, None] // 64])
    put("blk_ind", i[:, None] // 32 == np.arange(4)[None, :])
    put("blk_ind32", i[:, None] // 4 == np.arange(32)[None, :])
    put("sub_row", (i % 16)[:, None])
    put("grp", (i[:, None] // 4 == np.arange(64)[None, :] // 4))
    put("seq_ind", i[:, None] // 8 == np.arange(8)[None, :])
    put("blk_idx", np.broadcast_to(np.arange(16), (P, 16)))
    put("cmp_any", (i >= 31)[:, None])
    put("own_row", i[:, None] // 16 == np.arange(8))
    put("own_head", np.concatenate([i[:, None] % 32 == np.arange(4), i[:, None] % 32 // 4 == np.arange(2)], axis=1))
    put("pick_head", (i[:, None] // 32 == np.arange(16) % 4) & (i[:, None] % 4 == np.arange(16) // 4)
        & (i[:, None] % 32 < 8))
    q = np.arange(4)[None, :, None] * P + i[:, None, None]
    put("cmp_neg", np.where((np.arange(16)[None, None, :] + 1) * 32 - 1 <= q, 0.0, NEG))
    return c


def build(nc, ins, outs, consts):
    with ExitStack() as ctx:
        Decoder(nc, ctx, ins, outs, consts).program()


def rows(t):
    return P if t < 4 else NB


def cols(t):
    return slice(t * P, t * P + rows(t))


class Decoder:
    def __init__(self, nc, ctx, ins, outs, consts):
        self.nc, self.ctx, self.ins, self.outs, self.consts = nc, ctx, ins, outs, consts
        sb = self.sb
        self.x_res = sb("x_res", [P, TILES, D])
        self.xt = sb("xt", [P, KD * TOK])
        self.big = sb("big", [P, (FF // P) * TOK])
        self.tt = sb("tt", [P, 14, TOK])
        self.ring = sb("ring", [P, SLOTS, SLOT])
        self.cst = sb("cst", [P, N_KEEP])
        self.ident_b = sb("ident_b", [P, P], BF16)
        self.sb_neg_b = sb("sb_neg_b", [P, P], BF16)
        self.nsa_neg_b = sb("nsa_neg_b", [P, P], BF16)
        self.cmp_neg_b = sb("cmp_neg_b", [P, 64], BF16)
        self.g1 = sb("g1", [P, KD])
        self.g2 = sb("g2", [P, KD])
        self.gq = sb("gq", [P, HD])
        self.gk = sb("gk", [P, 3, HD])
        self.pos_k = sb("pos_k", [P, HD])
        self.pos_v = sb("pos_v", [P, HD])
        self.phi_k = sb("phi_k", [P, P])
        self.phi_v = sb("phi_v", [P, P])
        self.w_tail = sb("w_tail", [P, KD, 24])
        self.gates = sb("gates", [P, TILES, 24])
        self.pos8_k = sb("pos8_k", [P, 8, HD])
        self.pos8_v = sb("pos8_v", [P, 8, HD])
        self.q_nsa = sb("q_nsa", [P, NB, 8])
        self.q_wide = sb("q_wide", [P, 544])
        self.small = sb("small", [P, 104])
        self.few = sb("few", [P, 82])
        self.gate_rows = sb("gate_rows", [NB * 8, 3])
        self.stat = sb("stat", [P, 75])
        self.scr = sb("scr", [P, 3200])
        self.pages = sb("pages", [P, NB], I32)
        self.row_f = sb("row_f", [P, NB])
        self.row_i = sb("row_i", [P, NB], mybir.dt.uint32)
        self.ps = ctx.enter_context(nc.psum_tensor("ps", [P, 8, 512], F32))
        self.psf = self.ps[:].rearrange("p b n -> p (b n)")
        self.proj = self.big[:, 0:TILES * N_IN].rearrange("p (t n) -> p t n", n=N_IN)
        self.spare = self.big[:, TILES * N_IN:]
        self.hid = self.big[:].rearrange("p (f t) -> p f t", t=TOK)
        self.xtv = self.xt[:].rearrange("p (k t) -> p k t", t=TOK)
        self.layer_sems = []
        self.slot_ready = [self.sem(f"slot{s}_ready") for s in range(SLOTS)]
        self.gathered = [[self.sem(f"slot{s}_{kind}_gathered") for kind in ("sb", "slc", "cmp")]
                         for s in range(SLOTS)]
        self.outputs_done = self.sem("outputs_done")
        self.shift_done = self.sem("window_shift_done")
        self.small_ready = self.sem("small_ready")
        self.gain_ready = self.sem("norm1_gain_ready")
        self.ret_state_in = self.sem("ret_state_in")
        self.n_out = 0
        self.freed = [None] * N_ITEMS
        self.issued = 0

    def sb(self, name, shape, dt=F32):
        return self.ctx.enter_context(self.nc.sbuf_tensor(name, shape, dt))

    def sem(self, name):
        s = self.ctx.enter_context(self.nc.semaphore(name))
        self.layer_sems.append(s)
        return s

    def c(self, name):
        s, w = CONST_AT[name]
        return self.cst[:, s:s + w]

    def is_gather(self, i):
        return IT_K <= i < IT_VW or IT_V <= i < IT_WO

    def loads_of(self, i):
        return 0 if self.is_gather(i) else 3 if IT_WO <= i < IT_UP else 1

    def wait_item(self, eng, i, kinds=(0, 1, 2)):
        s = i % SLOTS
        if self.is_gather(i):
            n = sum(self.is_gather(j) for j in range(s, i + 1, SLOTS))
            for kind in kinds:
                eng.wait_ge(self.gathered[s][kind], 16 * n)
        else:
            eng.wait_ge(self.slot_ready[s], 16 * sum(self.loads_of(j) for j in range(s, i + 1, SLOTS)))

    def slot(self, i):
        return self.ring[:, i % SLOTS, :]

    def issue_until(self, sp, l, last):
        while self.issued < min(last, N_ITEMS):
            i = self.issued
            self.issued += 1
            if self.is_gather(i):
                continue
            if i >= SLOTS:
                for s, v in self.freed[i - SLOTS]:
                    sp.wait_ge(s, v)
            ready = self.slot_ready[i % SLOTS]
            dst, a = self.slot(i), self.ins
            lay = bass.ds(l, 1)
            if i < IT_KW:
                c = CHUNKS[i]
                src = a["w_in"][lay, :, c * 512:(c + 1) * 512].rearrange("o (k p) n -> p (o k) n", p=P)
                sp.dma_start(dst.rearrange("p (k n) -> p k n", k=KD), src).then_inc(ready, 16)
            elif i in (IT_KW, IT_VW):
                w = a["state_win_k" if i == IT_KW else "state_win_v"][lay]
                src = w.rearrange("o b (p j) g d -> p (o b) (j g d)", p=P)
                sp.dma_start(dst.rearrange("p (b n) -> p b n", b=NB), src).then_inc(ready, 16)
            elif i < IT_UP:
                n = i - IT_WO
                w = a["w_out"][lay, :, n * 512:(n + 1) * 512]
                d3 = dst.rearrange("p (k n) -> p k n", k=KD)
                sp.dma_start(d3[:, 0:4, :], w[:, 0:512].rearrange("o (k p) n -> p (o k) n", p=P)).then_inc(ready, 16)
                for g in range(2):
                    src = w[:, 512 + g * 256:768 + g * 256].rearrange("o (r d) n -> d (o r) n", d=HD)
                    sp.dma_start(d3[g * HD:(g + 1) * HD, 4:8, :], src).then_inc(ready, 16)
            elif i < IT_DN:
                c = i - IT_UP
                src = a["w_up"][lay, :, c * 512:(c + 1) * 512].rearrange("o (k p) n -> p (o k) n", p=P)
                sp.dma_start(dst.rearrange("p (k n) -> p k n", k=KD), src).then_inc(ready, 16)
            else:
                n, q = divmod(i - IT_DN, 4)
                src = a["w_down"][lay, q * D:(q + 1) * D, n * 512:(n + 1) * 512]
                sp.dma_start(dst.rearrange("p (k n) -> p k n", k=KD),
                             src.rearrange("o (k p) n -> p (o k) n", p=P)).then_inc(ready, 16)

    def gather(self, pool, i):
        for s, v in self.freed[i - SLOTS]:
            pool.wait_ge(s, v)
        kv = "k" if i < IT_VW else "v"
        b = i - (IT_K if kv == "k" else IT_V)
        for kind, (cache, off, w) in enumerate((("sb", 0, 256), ("slc", 2048, 128), ("cmp", 3072, 128))):
            src = self.ins[f"cache_{cache}_{kv}"].rearrange("l n (s i) h d -> (l n s) (i h d)", s=16)
            pool.indirect_dma_start(out=self.slot(i)[:, off:off + 8 * w], out_offset=None, in_=src,
                                    in_offset=bass.IndirectOffsetOnAxis(ap=self.row_i[:, b:b + 1], axis=0)
                                    ).then_inc(self.gathered[i % SLOTS][kind], 16)

    def program(self):
        nc = self.nc
        self.n_pool = self.ins["cache_sb_k"].shape[1]
        self.setup()
        with nc.Fori(0, DEPTH) as l:
            self.l = l
            self.norm("n1", self.g1, first=True)
            self.project()
            self.stick_breaking_and_retention()
            self.sparse_attention()
            self.output_projection()
            self.norm("n2", self.g2)
            self.mlp_up()
            self.mlp_down()
            nc.gpsimd.dma_reset()
            nc.all_engine_barrier()
            clearing = (nc.sync, nc.scalar, nc.vector, nc.tensor)
            for i, s in enumerate(self.layer_sems):
                clearing[i % len(clearing)].sem_clear(s)
            nc.all_engine_barrier()
        self.finish()

    def setup(self):
        nc, a = self.nc, self.ins
        loaded, zeroed = self.small_ready, self.sem("setup_zeroed")
        stage = self.xt[:, 0:N_CONST - N_KEEP]
        with nc.Block() as block:
            @block.sync
            def _(sp):
                sp.dma_start(self.cst[:], self.consts[:, 0:N_KEEP]).then_inc(loaded, 16)
                sp.dma_start(stage, self.consts[:, N_KEEP:N_CONST]).then_inc(loaded, 16)
                with nc.allow_non_contiguous_dma("page table"):
                    for j in range(NPAGE):
                        sp.dma_start(self.pages[16 * j:16 * (j + 1), :],
                                     a["page_table"].rearrange("b j -> j b")[j].partition_broadcast(16)
                                     ).then_inc(loaded, 16)
                sp.dma_start(self.x_res[:, 0:4, :], a["x_prompt"][0].rearrange("(t p) n -> p t n", p=P)
                             ).then_inc(loaded, 16)
                sp.dma_start(self.x_res[0:NB, 4, :], a["x_sample"].rearrange("b s n -> (b s) n")).then_inc(loaded, 16)
                sp.wait_ge(loaded, 192)

            @block.vector
            def _(dve):
                dve.memset(self.q_nsa[:], 0.0)
                dve.memset(self.phi_k[:], 0.0)
                dve.memset(self.phi_v[:], 0.0)
                dve.memset(self.stat[:], 1.0).then_inc(zeroed, 1)
                dve.wait_ge(loaded, 192)
                dve.tensor_copy(self.ident_b[:], self.c("ident"))
                dve.tensor_copy(self.sb_neg_b[:], stage[:, 0:128])
                dve.tensor_copy(self.nsa_neg_b[:], stage[:, 128:256])
                dve.tensor_copy(self.row_f[:], self.pages[:])
                dve.tensor_copy(self.cmp_neg_b[:], stage[:, 256:320]).then_inc(zeroed, 1)
                dve.wait_ge(zeroed, 2)
                dve.tensor_scalar(self.row_f[:], self.row_f[:], 16.0, self.c("sub_row"), ALU.mult, ALU.add
                                  ).then_inc(zeroed, 1)
                dve.wait_ge(zeroed, 3)
        for s in self.layer_sems:
            nc.sync.sem_clear(s)
        nc.all_engine_barrier()

    def finish(self):
        nc, o = self.nc, self.outs
        stored = self.outputs_done
        with nc.Block() as block:
            @block.sync
            def _(sp):
                sp.dma_start(o["y_prompt"][0].rearrange("(t p) n -> p t n", p=P), self.x_res[:, 0:4, :]
                             ).then_inc(stored, 16)
                sp.dma_start(o["y_sample"].rearrange("b s n -> (b s) n"), self.x_res[0:NB, 4, :]).then_inc(stored, 16)
                sp.wait_ge(stored, 32)

    def linker(self, eng, name):
        chain, n = self.sem(name), [0]

        def link(instr):
            n[0] += 1
            instr.then_inc(chain, 1)
            eng.wait_ge(chain, n[0])
        return link

    def refine_rsqrt(self, dve, link, r, v, tmp):
        link(dve.tensor_tensor(tmp, r, r, ALU.mult))
        link(dve.tensor_tensor(tmp, tmp, v, ALU.mult))
        link(dve.tensor_scalar(tmp, tmp, -0.5, 1.5, ALU.mult, ALU.add))
        link(dve.tensor_tensor(r, r, tmp, ALU.mult))

    def norm(self, name, gain, first=False):
        nc, l = self.nc, self.l
        x, ss = self.x_res, self.stat[:, 0:5]
        r, tmp = self.small[:, 8:13], self.small[:, 16:21]
        xn = self.scr[:, 0:2 * D].rearrange("p (i n) -> p i n", i=2)
        squares, var_ready, root = (self.sem(name + s) for s in ("_squares", "_var", "_root"))
        scaled, turned, copied = (self.sem(name + s) for s in ("_scaled", "_turned", "_copied"))
        with nc.Block() as block:
            if first:
                @block.sync
                def _(sp):
                    self.issued = 0
                    a, o, lay = self.ins, self.outs, bass.ds(l, 1)
                    n = 0
                    loads = [(self.g2[:], a["norm2_g"][lay].rearrange("o (k p) -> p (o k)", p=P)),
                             (self.w_tail[:], a["w_in"][lay, :, N_G:N_IN].rearrange("o (k p) n -> p (o k) n", p=P)),
                             (self.gq[:], a["nsa_q_norm"][lay].rearrange("o d -> (o d)").partition_broadcast(P)),
                             (self.gk[:].rearrange("p c d -> p (c d)"),
                              a["nsa_k_norm"][lay].rearrange("o c d -> (o c d)").partition_broadcast(P))]
                    for pos, pos8, phi, wp, wf in ((self.pos_k, self.pos8_k, self.phi_k, "cmp_pos_k", "cmp_w_k"),
                                                   (self.pos_v, self.pos8_v, self.phi_v, "cmp_pos_v", "cmp_w_v")):
                        loads += [(pos8[q:P:4].rearrange("p i d -> p (i d)"),
                                   a[wp][lay, 8 * q:8 * q + 8].rearrange("o i d -> (o i d)").partition_broadcast(32))
                                  for q in range(4)]
                        loads += [(pos[c * 32:(c + 1) * 32, :], a[wp][lay].rearrange("o j d -> (o j) d"))
                                  for c in range(4)]
                        loads += [(phi[g * HD:(g + 1) * HD, g * HD:(g + 1) * HD],
                                   a[wf][lay].rearrange("o d e -> (o d) e")) for g in range(2)]
                    with nc.allow_non_contiguous_dma("small gains"):
                        sp.dma_start(self.g1[:], a["norm1_g"][lay].rearrange("o (k p) -> p (o k)", p=P)
                                     ).then_inc(self.gain_ready, 16)
                        self.issue_until(sp, l, SLOTS)
                        for dst, src in loads:
                            sp.dma_start(dst, src).then_inc(self.small_ready, 16)
                            n += 1
                    self.n_small = 16 * n
                    for kv in "kv":
                        src = a[f"state_win_{kv}"][lay, :, 1:WIN].rearrange("o b w g d -> (o b) (w g d)")
                        dst = o[f"s_win_{kv}"][lay, :, 0:WIN - 1].rearrange("o b w g d -> (o b) (w g d)")
                        sp.dma_start(dst, src).then_inc(self.shift_done, 16)
            @block.scalar
            def _(act):
                junk = self.psf[:, 3072:4096]
                for t in range(TILES):
                    n = rows(t)
                    if t >= 1:
                        act.wait_ge(squares, t)
                    act.activation(junk[0:n], x[0:n, t, :], ACT.Square, accum_out=ss[0:n, t:t + 1]
                                   ).then_inc(squares, 1)
                act.wait_ge(var_ready, 1)
                act.activation(r, ss, ACT.Ln).then_inc(root, 1)
                act.wait_ge(root, 1)
                act.activation(r, r, ACT.Exp, scale=-0.5).then_inc(root, 1)

            @block.vector
            def _(dve):
                link = self.linker(dve, name + "_dve_chain")
                if first:
                    link(dve.tensor_copy(self.row_i[:], self.row_f[:]))
                    dve.tensor_scalar(self.row_f[:], self.row_f[:], float(16 * self.n_pool), None, ALU.add)
                dve.wait_ge(squares, TILES)
                dve.tensor_scalar(ss, ss, 1.0 / D, EPS, ALU.mult, ALU.add).then_inc(var_ready, 1)
                dve.wait_ge(root, 2)
                self.refine_rsqrt(dve, link, r, ss, tmp)
                if first:
                    dve.wait_ge(self.gain_ready, 16)
                for t in range(TILES + 1):
                    if t < TILES:
                        n = rows(t)
                        if t >= 2:
                            dve.wait_ge(turned, t - 1)
                        dve.tensor_scalar(xn[0:n, t % 2, :], x[0:n, t, :], r[0:n, t:t + 1], None, ALU.mult
                                          ).then_inc(scaled, 1)
                    if t >= 1:
                        s, n = t - 1, rows(t - 1)
                        dve.wait_ge(turned, s + 1)
                        for j in range(2):
                            src = self.ps[:, 2 * (s % 2) + j, :].rearrange("p (k n) -> p k n", k=4)[:, :, 0:n]
                            g = gain[:, 4 * j:4 * j + 4].unsqueeze(2).broadcast_to([P, 4, n])
                            ins = dve.tensor_tensor(self.xtv[:, 4 * j:4 * j + 4, cols(s)], src, g, ALU.mult)
                        ins.then_inc(copied, 1)

            @block.tensor
            def _(pe):
                ident = self.c("ident")
                for t in range(TILES):
                    n = rows(t)
                    pe.wait_ge(scaled, t + 1)
                    if t >= 2:
                        pe.wait_ge(copied, t - 1)
                    for k in range(KD):
                        ins = pe.transpose(self.ps[:, 2 * (t % 2) + k // 4, (k % 4) * P:(k % 4) * P + n],
                                           xn[0:n, t % 2, k * P:(k + 1) * P], ident[0:n, 0:n])
                    ins.then_inc(turned, 1)

    def rope(self, eng, link, x, half, cos, sin, tmp, shape):
        a, b = x[..., 0:half], x[..., half:2 * half]
        t = tmp
        eng.tensor_tensor(t[0], a, cos, ALU.mult)
        eng.tensor_tensor(t[1], b, sin, ALU.mult)
        eng.tensor_tensor(t[2], b, cos, ALU.mult)
        link(eng.tensor_tensor(t[3], a, sin, ALU.mult))
        eng.tensor_tensor(a, t[0], t[1], ALU.subtract)
        link(eng.tensor_tensor(b, t[2], t[3], ALU.add))

    def project(self):
        nc, l, pj = self.nc, self.l, self.proj
        mm_done, fm_ready = self.sem("proj_mm"), self.sem("proj_features_copied")
        back_done, out_ready = self.sem("proj_turned_back"), self.sem("proj_out")
        tail_mm, tail_read = self.sem("proj_tail_mm"), self.sem("proj_tail_copied")
        turned, t_copied = self.sem("qk_turned"), self.sem("qk_copied")
        ret_ready, q_ready, k_ready = self.sem("ret_roped"), self.sem("nsa_q_ready"), self.sem("nsa_k_ready")
        exps, var_ready, root, rs_ready = (self.sem(s) for s in ("gate_exp", "head_var", "head_root", "head_rstd"))
        H = TOK // 2
        units = [(c, f) for c in CHUNKS for f in range(4)]
        U, TAIL = len(units), 12
        for c in range(6):
            self.freed[c] = ((mm_done, 4 * (c + 1)),)
        fm = lambda u: self.tt[:, units[u][1] if units[u][0] == 0 else u % 2, :]
        ms = self.stat[:, 5:75]
        msv = ms.rearrange("p (t h) -> p t h", t=TILES)
        rs = self.scr[:, 2576:2646]
        rsv = rs.rearrange("p (t h) -> p t h", t=TILES)
        tmp70 = self.scr[:, 2496:2566]
        sq = self.spare[:, 0:896].rearrange("p (h d) -> p h d", d=HD)
        e_rg = self.scr[:, 0:1280].rearrange("p (t n) -> p t n", t=TILES)
        tq = [self.scr[:, 1280 + 256 * i:1536 + 256 * i] for i in range(4)]
        tk = [self.scr[:, 2304 + 48 * i:2352 + 48 * i] for i in range(4)]

        def kview(t, n):
            return pj[0:n, t, C_K:N_G].rearrange("p (c x) -> p c x", c=3)[:, :, 0:P].rearrange(
                "p c (g d) -> p c g d", g=2)

        with nc.Block() as block:
            @block.sync
            def _(sp):
                self.issue_until(sp, l, IT_KW + SLOTS)
                sp.wait_ge(self.small_ready, self.n_small)

            @block.tensor
            def _(pe):
                ident = self.c("ident")
                v = 0

                def turn(t, blocks):
                    nonlocal v
                    n = rows(t)
                    if v >= 2:
                        pe.wait_ge(t_copied, v - 1)
                    for j, c0 in enumerate(blocks):
                        ins = pe.transpose(self.ps[:, 4 + v % 2, j * P:j * P + n], pj[0:n, t, c0:c0 + P],
                                           ident[0:n, 0:n])
                    ins.then_inc(turned, 1)
                    v += 1

                def turn_back(u):
                    pe.wait_ge(fm_ready, u + 1)
                    if u >= 1:
                        pe.wait_ge(out_ready, u)
                    for t in range(TILES):
                        ins = pe.transpose(self.ps[0:rows(t), 6 + t // 4, (t % 4) * P:(t % 4 + 1) * P],
                                           fm(u)[:, cols(t)], ident)
                    ins.then_inc(back_done, 1)

                for u, (c, f) in enumerate(units):
                    if f == 0:
                        self.wait_item(pe, u // 4)
                    w = self.slot(u // 4).rearrange("p (k n) -> p k n", k=KD)
                    if u >= 2:
                        pe.wait_ge(fm_ready, u - 1)
                    for half in range(2):
                        for k in range(KD):
                            ins = pe.matmul(self.ps[:, 2 * (u % 2) + half, 0:H], w[:, k, f * P:(f + 1) * P],
                                            self.xtv[:, k, half * H:(half + 1) * H], start=(k == 0),
                                            stop=(k == KD - 1))
                    ins.then_inc(mm_done, 1)
                    if u >= 1:
                        turn_back(u - 1)
                    if u == TAIL - 1:
                        pe.wait_ge(self.small_ready, self.n_small)
                        for t in range(TILES):
                            for k in range(KD):
                                ins = pe.matmul(self.ps[0:rows(t), 4, t * 24:(t + 1) * 24], self.xtv[:, k, cols(t)],
                                                self.w_tail[:, k, :], start=(k == 0), stop=(k == KD - 1))
                        ins.then_inc(tail_mm, 1)
                    if u == 19:
                        pe.wait_ge(tail_read, 1)
                        for t in range(TILES):
                            pe.wait_ge(q_ready, t + 1)
                            turn(t, [N_Q + j * P for j in range(4)])
                            pe.wait_ge(k_ready, t + 1)
                            turn(t, [S_K, W_K])
                turn_back(U - 1)
                for t in range(TILES):
                    pe.wait_ge(ret_ready, t + 1)
                    turn(t, [R_Q, R_Q + P, R_K, R_K + P])

            @block.scalar
            def _(act):
                v = 0

                def copy_turned(t, dst, nblk, scaled):
                    nonlocal v
                    n = rows(t)
                    act.wait_ge(turned, v + 1)
                    src = self.ps[:, 4 + v % 2, 0:nblk * P].rearrange("p (j n) -> p j n", j=nblk)[:, :, 0:n]
                    if scaled:
                        ins = act.activation(self.tt[:, dst:dst + scaled, cols(t)], src[:, 0:scaled, :], ACT.Copy,
                                             scale=HD ** -0.5)
                    if scaled < nblk:
                        ins = act.activation(self.tt[:, dst + scaled:dst + nblk, cols(t)], src[:, scaled:nblk, :],
                                             ACT.Copy)
                    ins.then_inc(t_copied, 1)
                    v += 1

                def take_back(u):
                    c, f = units[u]
                    act.wait_ge(back_done, u + 1)
                    for n, tiles, bank, n_t in ((P, slice(0, 4), 6, 4), (NB, slice(4, 5), 7, 1)):
                        src = self.ps[0:n, bank, 0:n_t * P].rearrange("p (t n) -> p t n", t=n_t)
                        g = {3: 0, 4: 1}.get(c)
                        if (c == 3 and f >= 2) or (c == 4 and f < 2):
                            r0 = 2 * (f % 2)
                            dst = pj[0:n, tiles, N_Q + r0 * P:N_Q + (r0 + 2) * P].rearrange(
                                "p t (r g d) -> p t r g d", r=2, g=2)[:, :, :, g, :]
                            src = src.rearrange("p t (r d) -> p t r d", r=2)
                        else:
                            c0 = {3: R_G, 4: C_K - 2 * P}.get(c, c * 512) + f * P
                            dst = pj[0:n, tiles, c0:c0 + P]
                        ins = act.activation(dst, src, ACT.Copy)
                    ins.then_inc(out_ready, 1)

                for u, (c, f) in enumerate(units):
                    act.wait_ge(mm_done, u + 1)
                    if u >= 2:
                        act.wait_ge(back_done, u - 1)
                    act.activation(fm(u).rearrange("p (x n) -> p x n", x=2),
                                   self.ps[:, 2 * (u % 2):2 * (u % 2) + 2, 0:H], ACT.Copy,
                                   scale=HD ** -0.5 if c == 0 and f < 2 else 1.0).then_inc(fm_ready, 1)
                    if u >= 1:
                        take_back(u - 1)
                    if u == TAIL:
                        act.wait_ge(tail_mm, 1)
                        act.activation(pj[:, 0:4, N_G:N_IN],
                                       self.ps[:, 4, 0:96].rearrange("p (t n) -> p t n", t=4), ACT.Copy)
                        act.activation(pj[0:NB, 4, N_G:N_IN], self.ps[0:NB, 4, 96:120], ACT.Copy
                                       ).then_inc(tail_read, 1)
                        act.wait_ge(tail_read, 1)
                        act.wait_ge(out_ready, TAIL)
                        for t in range(TILES):
                            n = rows(t)
                            act.activation(self.gates[0:n, t, :], pj[0:n, t, N_G:N_IN], ACT.Exp, scale=-1.0)
                            act.activation(e_rg[0:n, t, :], pj[0:n, t, R_G:R_G + 256], ACT.Exp, scale=-1.0
                                           ).then_inc(exps, 1)
                        act.wait_ge(var_ready, 1)
                        act.activation(rs, ms, ACT.Ln).then_inc(root, 1)
                        act.wait_ge(root, 1)
                        act.activation(rs, rs, ACT.Exp, scale=-0.5).then_inc(root, 1)
                    if u == 19:
                        for t in range(TILES):
                            copy_turned(t, T_NQ, 4, 4)
                            copy_turned(t, T_SK, 2, 0)
                take_back(U - 1)
                for t in range(TILES):
                    copy_turned(t, T_RQ, 4, 0)

            @block.vector
            def _(dve):
                link = self.linker(dve, "proj_dve_chain")
                cosr = self.c("cos_r").rearrange("p (t x) -> p t x", t=TILES)
                sinr = self.c("sin_r").rearrange("p (t x) -> p t x", t=TILES)
                cosn = self.c("cos_n").rearrange("p (t x) -> p t x", t=TILES)
                sinn = self.c("sin_n").rearrange("p (t x) -> p t x", t=TILES)
                dec = self.c("decay").rearrange("p (t x) -> p t x", t=TILES)
                for t in range(TILES):
                    n = rows(t)
                    dve.wait_ge(out_ready, TAIL)
                    q = pj[0:n, t, N_Q:N_Q + 512].rearrange("p (h d) -> p h d", d=HD)
                    kk = kview(t, n)
                    dve.tensor_tensor(sq[0:n, 0:8, :], q, q, ALU.mult)
                    link(dve.tensor_tensor(sq[0:n, 8:14, :].rearrange("p (c g) d -> p c g d", c=3), kk, kk, ALU.mult))
                    link(dve.tensor_reduce(msv[0:n, t, :], sq[0:n], AXX, ALU.add))
                dve.tensor_scalar(ms, ms, 1.0 / HD, EPS, ALU.mult, ALU.add).then_inc(var_ready, 1)
                dve.wait_ge(root, 2)
                self.refine_rsqrt(dve, link, rs, ms, tmp70)
                dve.tensor_scalar(rs, rs, 1.0, None, ALU.mult).then_inc(rs_ready, 1)
                dve.wait_ge(rs_ready, 1)
                dve.wait_ge(self.small_ready, self.n_small)
                for t in range(TILES):
                    n = rows(t)
                    q = pj[0:n, t, N_Q:N_Q + 512].rearrange("p (h d) -> p h d", d=HD)
                    link(dve.tensor_tensor(q, q, rsv[0:n, t, 0:8].unsqueeze(2).broadcast_to([n, 8, HD]), ALU.mult))
                    link(dve.tensor_tensor(q, q, self.gq[0:n].unsqueeze(1).broadcast_to([n, 8, HD]), ALU.mult))
                    self.rope(dve, link, q, 8, cosn[0:n, t, :].unsqueeze(1).broadcast_to([n, 8, 8]),
                              sinn[0:n, t, :].unsqueeze(1).broadcast_to([n, 8, 8]),
                              [z[0:n, 0:64].rearrange("p (h d) -> p h d", h=8) for z in tq], [n, 8])
                    dve.tensor_scalar(q, q, 1.0, None, ALU.mult).then_inc(q_ready, 1)
                dve.wait_ge(exps, TILES)
                for t in range(TILES):
                    n = rows(t)
                    dve.tensor_scalar(e_rg[0:n, t, :], e_rg[0:n, t, :], 1.0, None, ALU.add)
                    link(dve.tensor_scalar(self.gates[0:n, t, :], self.gates[0:n, t, :], 1.0, None, ALU.add))
                    dve.reciprocal(self.gates[0:n, t, :], self.gates[0:n, t, :])
                    link(dve.reciprocal(e_rg[0:n, t, :], e_rg[0:n, t, :]))
                    link(dve.tensor_tensor(pj[0:n, t, R_G:R_G + 256], pj[0:n, t, R_G:R_G + 256], e_rg[0:n, t, :],
                                           ALU.mult))
                for t in range(TILES):
                    n = rows(t)
                    dve.wait_ge(out_ready, 20)
                    x = pj[0:n, t, R_Q:R_V].rearrange("p (h d) -> p h d", d=HD)
                    self.rope(dve, link, x, 32, cosr[0:n, t, :].unsqueeze(1).broadcast_to([n, 8, 32]),
                              sinr[0:n, t, :].unsqueeze(1).broadcast_to([n, 8, 32]),
                              [q[0:n].rearrange("p (h d) -> p h d", h=8) for q in tq], [n, 8])
                    dve.tensor_tensor(x, x, dec[0:n, t, :].unsqueeze(2).broadcast_to([n, 8, HD]), ALU.mult
                                      ).then_inc(ret_ready, 1)

            @block.gpsimd
            def _(pool):
                link = self.linker(pool, "proj_pool_chain")
                cosn = self.c("cos_n").rearrange("p (t x) -> p t x", t=TILES)
                sinn = self.c("sin_n").rearrange("p (t x) -> p t x", t=TILES)
                pool.wait_ge(rs_ready, 1)
                pool.wait_ge(self.small_ready, self.n_small)
                for t in range(TILES):
                    n = rows(t)
                    for j in range(3):
                        kk = kview(t, n)[:, j]
                        r = rsv[0:n, t, 8 + 2 * j:10 + 2 * j].unsqueeze(2).broadcast_to([n, 2, HD])
                        link(pool.tensor_tensor(kk, kk, r, ALU.mult))
                        link(pool.tensor_tensor(kk, kk, self.gk[0:n, j].unsqueeze(1).broadcast_to([n, 2, HD]),
                                                ALU.mult))
                        self.rope(pool, link, kk, 8, cosn[0:n, t, :].unsqueeze(1).broadcast_to([n, 2, 8]),
                                  sinn[0:n, t, :].unsqueeze(1).broadcast_to([n, 2, 8]),
                                  [z[0:n, 0:16].rearrange("p (g d) -> p g d", g=2) for z in tk], [n, 2])
                    pool.tensor_copy(tk[0][0:n, 0:1], tk[1][0:n, 0:1]).then_inc(k_ready, 1)

    def store_heads(self, sp):
        o, l, pj = self.outs, self.l, self.proj
        lay = bass.ds(l, 1)
        for name, c0, w in (("sb_k", SB_K, 256), ("sb_v", SB_V, 256), ("cmp_k", C_K, P), ("cmp_v", C_V, P),
                            ("slc_k", S_K, P), ("slc_v", S_V, P), ("win_k", W_K, P), ("win_v", W_V, P)):
            dst = o["p_" + name][lay].rearrange("o b (t p) h d -> p (o b t) (h d)", p=P)
            sp.dma_start(dst, pj[:, 0:4, c0:c0 + w]).then_inc(self.outputs_done, 16)
            if name.startswith("win"):
                dst = o["s_" + name][lay, :, WIN - 1:WIN].rearrange("o b w h d -> (o b w) (h d)")
            else:
                dst = o["s_" + name][lay].rearrange("o b s h d -> (o b s) (h d)")
            sp.dma_start(dst, pj[0:NB, 4, c0:c0 + w]).then_inc(self.outputs_done, 16)

    def stick_breaking_and_retention(self):
        nc, pj, o, a = self.nc, self.proj, self.outs, self.ins
        lay = bass.ds(self.l, 1)
        s_ready, copied, masked, pv_done = (self.sem(s) for s in ("ret_inner", "ret_copied", "ret_masked", "ret_pv"))
        st_mm, st_ready, var_ready, root = (self.sem(s) for s in ("ret_state_mm", "ret_state", "ret_var", "ret_root"))
        self.q_cleared, self.q_built = self.sem("stationary_q_cleared"), self.sem("stationary_q_built")
        v_stored, v_read, st_new, o_mm, o_copied, o_stored, o_read, s_var_ready, s_root = (
            self.sem(s) for s in ("rs_v_stored", "rs_v_read", "rs_state", "rs_mm",
                                  "rs_copied", "rs_o_stored", "rs_o_read", "rs_var", "rs_root"))
        z_ready, abs_ready, ln_ready, l_ready = (self.sem(s) for s in ("sb_z", "sb_abs", "sb_ln", "sb_softplus"))
        e_ready, cum_ready, w_ready, sb_done = (self.sem(s) for s in ("sb_e", "sb_cum", "sb_w", "sb_pv"))
        sb_o_read, o_taken = self.sem("sb_out_read"), self.sem("ret_out_read")
        weighted, pooled, p_copied, mapped = (self.sem(s) for s in ("cp_weighted", "cp_pooled", "cp_copied",
                                                                    "cp_mapped"))
        slot = self.slot(IT_K + 1)
        lbuf, wbuf, ibuf = (self.xt[:, i * PACKED:(i + 1) * PACKED] for i in range(3))
        ebuf = self.scr[:, 0:PACKED]
        sb_z, ret_z = self.psf[:, 0:PACKED], self.psf[:, 1536:1536 + PACKED]
        out_of = lambda bank, h, qb: self.ps[:, bank, (h % 2) * 256 + qb * HD:(h % 2) * 256 + (qb + 1) * HD]
        sq = slot[:, 2048:3072].rearrange("p (h d) -> p h d", d=HD)
        state = slot[0:HD, 3648:3904]
        mu, var, r, tmp = (self.small[:, 16 * i:16 * i + 16] for i in range(4))
        st = slot[:, 0:1024].rearrange("p (b x e) -> p b x e", b=NB, x=2)
        v_rows = slot[:, 1024:2048]
        vb = v_rows.rearrange("p (b x e) -> p b x e", b=NB, x=2)
        osb = slot[0:32, 3584:3648]
        orow = slot[0:NB, 3072:3328]
        s_sq = slot[0:NB, 3328:3584]
        s_mu, s_var, s_r, s_tmp = (self.small[0:NB, 64 + 4 * i:68 + 4 * i] for i in range(4))
        s_v = nc.dram_tensor("scratch_ret_v", [NB, 256], F32, kind="Internal").ap()
        s_o = nc.dram_tensor("scratch_ret_o", [32, HD], F32, kind="Internal").ap()
        s_g = nc.dram_tensor("scratch_gates", [NB, 24], F32, kind="Internal").ap()
        self.s_q = nc.dram_tensor("scratch_sb_q", [NB, 256], F32, kind="Internal").ap()
        kw = self.spare[:, 0:1024].rearrange("p (i n) -> p i n", i=8)
        pl = self.spare[:, 1024:1056]
        self.k_diag = self.scr[:, 2912:2944]
        vcmp = self.scr[0:16, 3072:3200]
        repeat = self.spare[0:16, 512:640]
        self.v_diag = self.spare[:, 0:512]
        v_taken, repeated = self.sem("cp_v_taken"), self.sem("cp_repeated")

        with nc.Block() as block:
            @block.tensor
            def _(pe):
                def scores(z, t_k, t_q, h):
                    p0 = (h % 2) * HD
                    for jb in (0, 1, 3, 2):
                        n = SEQ - jb * P
                        ins = pe.matmul(z[:, PACK[jb]:PACK[jb] + n],
                                        self.tt[p0:p0 + HD, t_k + h // 2, jb * P:(jb + 1) * P],
                                        self.tt[p0:p0 + HD, t_q + h // 2, jb * P:SEQ],
                                        start=(jb != 3), stop=True, skip_group_check=True)
                    return ins

                def products(bank, weights, v0, h):
                    for qb in range(4):
                        for jb in range(qb + 1):
                            a0 = PACK[jb] + (qb - jb) * P
                            ins = pe.matmul(out_of(bank, h, qb), weights[:, a0:a0 + P],
                                            pj[:, jb, v0 + h * HD:v0 + (h + 1) * HD],
                                            start=(jb == 0), stop=(jb == qb), skip_group_check=True)
                    return ins

                def sb_products(h):
                    if h >= 1:
                        pe.wait_ge(sb_o_read, h)
                    products(6, wbuf, SB_V, h).then_inc(sb_done, 1)

                for h in range(4):
                    if h >= 1:
                        pe.wait_ge(w_ready, h)
                    scores(sb_z, T_SBK, T_SBQ, h).then_inc(z_ready, 1)
                    if h >= 1:
                        pe.wait_ge(copied, h)
                    scores(ret_z, T_RK, T_RQ, h).then_inc(s_ready, 1)
                    if h >= 1:
                        sb_products(h - 1)
                    pe.wait_ge(l_ready, h + 1)
                    for jb in range(4):
                        a0 = PACK[jb]
                        pe.matmul(sb_z[:, a0:a0 + P], self.ident_b[:], self.sb_neg_b[:], start=False, stop=True,
                                  skip_group_check=True)
                        ins = pe.matmul(sb_z[:, a0:a0 + SEQ - jb * P], self.c("neg_suffix"),
                                        lbuf[:, a0:a0 + SEQ - jb * P], start=False, stop=True, skip_group_check=True)
                        for j2 in range(jb + 1, 4):
                            ins = pe.matmul(sb_z[:, a0 + (j2 - jb) * P:a0 + SEQ - jb * P], self.c("neg_ones"),
                                            lbuf[:, PACK[j2]:PACK[j2] + SEQ - j2 * P], start=False, stop=True,
                                            skip_group_check=True)
                    ins.then_inc(cum_ready, 1)
                    pe.wait_ge(masked, h + 1)
                    if h >= 1:
                        pe.wait_ge(o_taken, h)
                    products(7, ibuf, R_V, h).then_inc(pv_done, 1)
                pe.wait_ge(copied, 4)
                for h in range(4):
                    for t in range(4):
                        ins = pe.matmul(self.ps[0:HD, 3, h * HD:(h + 1) * HD],
                                        pj[:, t, R_K + h * HD:R_K + (h + 1) * HD],
                                        pj[:, t, R_V + h * HD:R_V + (h + 1) * HD], start=(t == 0), stop=(t == 3),
                                        skip_group_check=True)
                ins.then_inc(st_mm, 1)
                pe.wait_ge(self.q_built, 1)
                pe.wait_ge(st_new, 1)
                for b in range(NB):
                    for x in range(2):
                        ins = pe.matmul(self.ps[0:32, 4, 0:HD], self.q_wide[:, x * 256 + b * 32:x * 256 + b * 32 + 32],
                                        st[:, b, x, :], start=(b == 0 and x == 0), stop=(b == NB - 1 and x == 1))
                ins.then_inc(o_mm, 1)
                pe.wait_ge(weighted, 1)
                for i in range(8):
                    ins = pe.matmul(self.ps[:, 5, 4 * i:4 * i + 4], kw[:, i, :], self.c("blk_ind"), start=True,
                                    stop=True, skip_group_check=True)
                ins.then_inc(pooled, 1)
                pe.wait_ge(w_ready, 4)
                sb_products(3)
                pe.wait_ge(p_copied, 1)
                pe.matmul(self.ps[:, 0, 0:16], self.phi_k[:], pl[:, 0:16], start=True, stop=True)
                pe.matmul(self.ps[0:16, 1, 0:P], pl[:, 16:32], self.phi_v[:], start=True, stop=True
                          ).then_inc(mapped, 1)
                pe.wait_ge(v_taken, 1)
                pe.matmul(self.ps[:, 5, 0:P], repeat, vcmp, start=True, stop=True).then_inc(repeated, 1)

            @block.scalar
            def _(act):
                def take_sb_output(h):
                    act.wait_ge(sb_done, h + 1)
                    act.activation(pj[:, 0:4, SB_Q + h * HD:SB_Q + (h + 1) * HD],
                                   self.ps[:, 6, (h % 2) * 256:(h % 2 + 1) * 256].rearrange("p (q d) -> p q d", q=4),
                                   ACT.Copy).then_inc(sb_o_read, 1)

                for h in range(4):
                    act.wait_ge(z_ready, h + 1)
                    if h >= 1:
                        act.wait_ge(l_ready, h)
                    act.activation(ebuf, sb_z, ACT.Abs).then_inc(abs_ready, 1)
                    act.wait_ge(abs_ready, h + 1)
                    act.activation(ebuf, ebuf, ACT.Exp, scale=-1.0).then_inc(e_ready, 1)
                    act.wait_ge(e_ready, h + 1)
                    act.activation(ebuf, ebuf, ACT.Ln, bias=1.0).then_inc(ln_ready, 1)
                    act.wait_ge(s_ready, h + 1)
                    if h >= 1:
                        act.wait_ge(pv_done, h)
                    act.activation(ibuf, ret_z, ACT.Copy).then_inc(copied, 1)
                    if h >= 1:
                        take_sb_output(h - 1)
                    act.wait_ge(cum_ready, h + 1)
                    act.activation(wbuf, sb_z, ACT.Exp).then_inc(w_ready, 1)
                act.wait_ge(var_ready, 1)
                act.activation(r, var, ACT.Ln).then_inc(root, 1)
                act.wait_ge(root, 1)
                act.activation(r, r, ACT.Exp, scale=-0.5).then_inc(root, 1)
                take_sb_output(3)
                act.wait_ge(s_var_ready, 1)
                act.activation(s_r, s_var, ACT.Ln).then_inc(s_root, 1)
                act.wait_ge(s_root, 1)
                act.activation(s_r, s_r, ACT.Exp, scale=-0.5).then_inc(s_root, 1)

            @block.vector
            def _(dve):
                link = self.linker(dve, "ret_dve_chain")
                link(dve.memset(self.k_diag, 0.0))
                for i in range(8):
                    kv, t = divmod(i, 4)
                    src = pj[:, t, (C_K, C_V)[kv]:(C_K, C_V)[kv] + P].rearrange("p (g d) -> p g d", g=2)
                    pos = (self.pos_k, self.pos_v)[kv][:].unsqueeze(1).broadcast_to([P, 2, HD])
                    ins = dve.tensor_tensor(kw[:, i, :].rearrange("p (g d) -> p g d", g=2), src, pos, ALU.mult)
                ins.then_inc(weighted, 1)
                def sample_states():
                    dve.wait_ge(v_read, 48)
                    kt = self.tt[:, T_RK:T_RK + 2, SEQ:TOK].rearrange("p x b -> p b x").unsqueeze(3).broadcast_to(
                        [P, NB, 2, HD])
                    link(dve.tensor_tensor(vb, vb, kt, ALU.mult))
                    dve.wait_ge(self.ret_state_in, 32)
                    for x in range(2):
                        ins = dve.scalar_tensor_tensor(out=st[:, :, x, :], in0=st[:, :, x, :],
                                                       scalar=self.c("gam_one")[:, x:x + 1], in1=vb[:, :, x, :],
                                                       op0=ALU.mult, op1=ALU.add)
                    ins.then_inc(st_new, 1)

                def blocks_masked(buf, mask):
                    for jb in range(4):
                        d = buf[:, PACK[jb]:PACK[jb] + P]
                        ins = dve.tensor_tensor(d, d, self.c(mask), ALU.mult)
                    return ins

                for h in range(4):
                    dve.wait_ge(ln_ready, h + 1)
                    if h >= 1:
                        dve.wait_ge(cum_ready, h)
                    link(dve.scalar_tensor_tensor(out=lbuf, in0=sb_z, scalar=0.0, in1=ebuf, op0=ALU.max,
                                                  op1=ALU.add))
                    blocks_masked(lbuf, "sb_mask").then_inc(l_ready, 1)
                    dve.wait_ge(copied, h + 1)
                    blocks_masked(ibuf, "ret_mask").then_inc(masked, 1)
                    if h == 1:
                        sample_states()
                    dve.wait_ge(pv_done, h + 1)
                    dve.tensor_copy(
                        sq.rearrange("p (t h) d -> p t h d", t=4)[:, :, h, :],
                        self.ps[:, 7, (h % 2) * 256:(h % 2 + 1) * 256].rearrange("p (q d) -> p q d", q=4)
                        ).then_inc(o_taken, 1)
                    dve.wait_ge(o_taken, h + 1)
                    link(dve.tensor_reduce(mu.rearrange("p (t h) -> p t h", t=4)[:, :, h],
                                           sq.rearrange("p (t h) d -> p t h d", t=4)[:, :, h, :], AXX, ALU.add))
                link(dve.tensor_scalar(mu, mu, 1.0 / HD, None, ALU.mult))
                link(dve.tensor_tensor(sq, sq, mu.unsqueeze(2).broadcast_to([P, 16, HD]), ALU.subtract))
                dve.wait_ge(o_mm, 1)
                dve.tensor_copy(osb, self.ps[0:32, 4, 0:HD]).then_inc(o_copied, 1)
                xc = pj[:, 0:4, R_Q:R_Q + 256].rearrange("p t (h d) -> p t h d", h=4)
                link(dve.tensor_copy(xc, sq.rearrange("p (t h) d -> p t h d", t=4)))
                link(dve.tensor_tensor(sq, sq, sq, ALU.mult))
                link(dve.tensor_reduce(var, sq, AXX, ALU.add))
                dve.tensor_scalar(var, var, 1.0 / HD, EPS, ALU.mult, ALU.add).then_inc(var_ready, 1)
                dve.wait_ge(pooled, 1)
                dve.tensor_copy(pl, self.ps[:, 5, 0:32]).then_inc(p_copied, 1)
                dve.wait_ge(st_mm, 1)
                dve.tensor_tensor(state.rearrange("p (h e) -> p h e", h=4),
                                  self.ps[0:HD, 3, 0:256].rearrange("p (h e) -> p h e", h=4),
                                  self.c("gam_last")[0:HD].unsqueeze(2).broadcast_to([HD, 4, HD]), ALU.mult
                                  ).then_inc(st_ready, 1)
                dve.wait_ge(root, 2)
                self.refine_rsqrt(dve, link, r, var, tmp)
                link(dve.tensor_tensor(xc, xc, r.rearrange("p (t h) -> p t h", t=4).unsqueeze(3).broadcast_to(
                    [P, 4, 4, HD]), ALU.mult))
                link(dve.tensor_tensor(pj[:, 0:4, R_Q:R_Q + 256], pj[:, 0:4, R_Q:R_Q + 256],
                                       pj[:, 0:4, R_G:R_G + 256], ALU.mult))
                dve.wait_ge(mapped, 1)
                for g in range(2):
                    p0 = g * HD
                    dve.tensor_copy(self.k_diag[p0:p0 + HD, g * 16:(g + 1) * 16], self.ps[p0:p0 + HD, 0, 0:16])
                dve.tensor_copy(repeat.rearrange("p (h j) -> p h j", h=8),
                                self.c("ident")[0:16, 0:16].unsqueeze(1).broadcast_to([16, 8, 16]))
                dve.tensor_copy(vcmp, self.ps[0:16, 1, 0:P]).then_inc(v_taken, 1)
                dve.wait_ge(repeated, 1)
                dve.tensor_tensor(
                    self.v_diag.rearrange("p (g r d) -> p g r d", g=2, r=4),
                    self.ps[:, 5, 0:P].rearrange("p (g d) -> p g d", g=2).unsqueeze(2).broadcast_to([P, 2, 4, HD]),
                    self.c("own_row").rearrange("p (g r) -> p g r", g=2).unsqueeze(3).broadcast_to([P, 2, 4, HD]),
                    ALU.mult)
                dve.wait_ge(o_read, 16)
                ov = orow.rearrange("p (h d) -> p h d", h=4)
                sv = s_sq.rearrange("p (h d) -> p h d", h=4)
                link(dve.tensor_reduce(s_mu, ov, AXX, ALU.add))
                link(dve.tensor_scalar(s_mu, s_mu, 1.0 / HD, None, ALU.mult))
                link(dve.tensor_tensor(ov, ov, s_mu.unsqueeze(2).broadcast_to([NB, 4, HD]), ALU.subtract))
                link(dve.tensor_tensor(s_sq, orow, orow, ALU.mult))
                link(dve.tensor_reduce(s_var, sv, AXX, ALU.add))
                dve.tensor_scalar(s_var, s_var, 1.0 / HD, EPS, ALU.mult, ALU.add).then_inc(s_var_ready, 1)
                dve.wait_ge(s_root, 2)
                self.refine_rsqrt(dve, link, s_r, s_var, s_tmp)
                link(dve.tensor_tensor(ov, ov, s_r.unsqueeze(2).broadcast_to([NB, 4, HD]), ALU.mult))
                link(dve.tensor_tensor(pj[0:NB, 4, R_Q:R_Q + 256], orow, pj[0:NB, 4, R_G:R_G + 256], ALU.mult))

            @block.sync
            def _(sp):
                src = a["state_ret"][lay].rearrange("o b (x h) d e -> (h d) (o b) x e", h=2)
                for x in range(2):
                    sp.dma_start(st[:, :, x, :], src[:, :, x, :]).then_inc(self.ret_state_in, 16)
                sp.dma_start(s_v, pj[0:NB, 4, R_V:R_V + 256]).then_inc(v_stored, 16)
                sp.dma_start(s_g, self.gates[0:NB, 4, :]).then_inc(v_stored, 16)
                sp.dma_start(self.s_q, pj[0:NB, 4, SB_Q:SB_Q + 256]).then_inc(v_stored, 16)
                self.store_heads(sp)
                self.n_out = 16 * 16
                sp.wait_ge(v_stored, 48)
                for h in range(2):
                    src = s_v.rearrange("b (x h e) -> h (b x) e", x=2, h=2)[h]
                    sp.dma_start(v_rows[h * HD:(h + 1) * HD].rearrange("p (y e) -> p y e", e=HD),
                                 src.partition_broadcast(HD)).then_inc(v_read, 16)
                with nc.allow_non_contiguous_dma("sample gates"):
                    sp.dma_start(self.gate_rows[:], s_g.rearrange("b (h c) -> (b h) c", c=3)).then_inc(v_read, 16)
                sp.wait_ge(v_read, 48)
                sp.wait_ge(st_new, 1)
                dst = o["s_ret"][lay].rearrange("o b (x h) d e -> (h d) (o b) x e", h=2)
                for x in range(2):
                    sp.dma_start(dst[:, :, x, :], st[:, :, x, :]).then_inc(self.outputs_done, 16)
                sp.wait_ge(o_copied, 1)
                sp.dma_start(s_o, osb).then_inc(o_stored, 16)
                sp.wait_ge(o_stored, 16)
                sp.dma_start(orow, s_o.rearrange("(b h) d -> b (h d)", b=NB)).then_inc(o_read, 16)
                sp.wait_ge(st_ready, 1)
                dst = o["p_ret"][lay].rearrange("o b h d e -> d (o b h) e")
                sp.dma_start(dst, state.rearrange("p (h e) -> p h e", h=4)).then_inc(self.outputs_done, 16)
                self.n_out += 48
                sp.wait_ge(o_read, 16)
                sp.wait_ge(self.outputs_done, self.n_out)

            @block.gpsimd
            def _(pool):
                pool.memset(self.q_wide[:], 0.0).then_inc(self.q_cleared, 1)
                pool.wait_ge(self.q_cleared, 1)
                for g in range(2):
                    p = slice(g * HD, (g + 1) * HD)
                    pool.tensor_copy(self.q_nsa[p, :, 4 * g:4 * g + 4],
                                     self.tt[p, T_NQ:T_NQ + 4, SEQ:TOK].rearrange("p r b -> p b r"))
                    for x in range(2):
                        dst = self.q_wide[p, x * 256:x * 256 + 288].rearrange("p (b y) -> p b y", y=36)[:, :, 2 * x + g]
                        ins = pool.tensor_copy(dst, self.tt[p, T_RQ + x, SEQ:TOK])
                ins.then_inc(self.q_built, 1)
                pool.wait_ge(self.q_built, 1)
                self.gather(pool, IT_K)

    def sparse_attention(self):
        nc, l = self.nc, self.l
        prompt, sample = self.prompt_sparse(), self.sample_cached()

        def in_turn(eng, name):
            a, b = prompt[name](eng), sample[name](eng)
            live = [a, b]
            while live:
                for g in list(live):
                    if next(g, live) is live:
                        live.remove(g)

        with nc.Block() as block:
            @block.sync
            def _(sp):
                sp.dma_start(self.q_everywhere, self.s_q.rearrange("b n -> (b n)").partition_broadcast(P)
                             ).then_inc(self.q_spread, 16)
                self.issue_until(sp, l, IT_WO + SLOTS)

            @block.tensor
            def _(pe):
                in_turn(pe, "pe")

            @block.scalar
            def _(act):
                in_turn(act, "act")

            @block.vector
            def _(dve):
                in_turn(dve, "dve")

            @block.gpsimd
            def _(pool):
                for _ in sample["pool"](pool):
                    pass

    def prompt_sparse(self):
        pj = self.proj
        qk_done, nmax_ready, exp_done, turned = (self.sem(s) for s in ("ns_qk", "ns_negmax", "ns_exp", "ns_turned"))
        copied = [self.sem("ns_copied_dve"), self.sem("ns_copied_act")]
        pv_done, o_read = self.sem("ns_pv"), self.sem("ns_o_read")
        prob = [self.xt[:, 0:512], self.xt[:, 512:1024]]
        pt = [self.xt[:, 1024:1536], self.xt[:, 1536:2048]]
        otmp = self.xt[:, 2048:2560]
        nmax = [self.small[:, 0:1], self.small[:, 1:2]]
        rsum = [self.small[:, 8:16], self.small[:, 16:24]]
        wgt = self.small[:, 24:32]
        max8 = self.small[:, 80:88]
        units, group, closes = [], [], []
        for qt in (3, 2, 1, 0):
            for br in range(3):
                heads = (None,) if br == 0 else range(8)
                group += [group[-1] + 1 if group else 0] * len(heads)
                units += [(qt, br, h) for h in heads]
                closes += [h in (None, 7) for h in heads]
        U = len(units)

        def copied_of(u):
            return copied[u % 2], u // 2 + 1

        def pe_steps(pe):
            for u in range(U + 2):
                if u < U:
                    qt, br, h = units[u]
                    s = self.ps[:, u % 2, :]
                    if u >= 2:
                        pe.wait_ge(exp_done, u - 1)
                    if br == 0:
                        mask = self.cmp_neg_b[:, qt * 16:qt * 16 + 16].unsqueeze(1).broadcast_to([P, 8, 16])
                        pe.matmul(s[:, 0:P], self.ident_b[:], mask, start=True, stop=True, skip_group_check=True)
                        for r in range(4):
                            ins = pe.matmul(s[:, 0:P].rearrange("p (g r n) -> p r g n", g=2, r=4)[:, r],
                                            self.tt[:, T_NQ + r, qt * P:(qt + 1) * P], self.k_diag, start=False,
                                            stop=True, skip_group_check=True)
                    else:
                        nk, p0 = (qt + 1) * P, h // 4 * HD
                        pe.matmul(s[:, nk - P:nk], self.ident_b[:], self.nsa_neg_b[:], start=True, stop=True,
                                  skip_group_check=True)
                        ins = pe.matmul(s[:, 0:nk], self.tt[p0:p0 + HD, T_NQ + h % 4, qt * P:(qt + 1) * P],
                                        self.tt[p0:p0 + HD, (T_SK, T_WK)[br - 1], 0:nk], start=False, stop=True,
                                        skip_group_check=True)
                    ins.then_inc(qk_done, 1)
                if 1 <= u <= U:
                    w = u - 1
                    qt, br, h = units[w]
                    pe.wait_ge(exp_done, w + 1)
                    if w >= 1:
                        pe.wait_ge(*copied_of(w - 1))
                    for b in range(1 if br == 0 else qt + 1):
                        ins = pe.transpose(self.ps[:, 2, b * P:(b + 1) * P], prob[w % 2][:, b * P:(b + 1) * P],
                                           self.c("ident"))
                    ins.then_inc(turned, 1)
                if u >= 2:
                    w = u - 2
                    qt, br, h = units[w]
                    grp = group[w]
                    pe.wait_ge(*copied_of(w))
                    if h in (None, 0) and grp >= 1:
                        pe.wait_ge(o_read, grp)
                    if br == 0:
                        ins = pe.matmul(self.ps[:, 3, :], pt[w % 2][:, 0:P], self.v_diag, start=True, stop=True,
                                        skip_group_check=True)
                    else:
                        out = self.ps[:, 3, h * HD:(h + 1) * HD]
                        v0 = (S_V, W_V)[br - 1] + h // 4 * HD
                        for b in range(qt + 1):
                            ins = pe.matmul(out, pt[w % 2][:, b * P:(b + 1) * P], pj[:, b, v0:v0 + HD],
                                            start=(b == 0), stop=(b == qt), skip_group_check=True)
                    ins.then_inc(pv_done, 1)
                yield

        def copy_probs(eng, w):
            qt, br, _ = units[w]
            eng.wait_ge(turned, w + 1)
            if w >= 2:
                eng.wait_ge(pv_done, w - 1)
            n = P if br == 0 else (qt + 1) * P
            dst, src = pt[w % 2][:, 0:n], self.ps[:, 2, 0:n]
            if w % 2 == 0:
                eng.tensor_copy(dst, src).then_inc(copied[0], 1)
            else:
                eng.activation(dst, src, ACT.Copy).then_inc(copied[1], 1)

        def act_steps(act):
            for u in range(U + 2):
                if u < U:
                    qt, br, h = units[u]
                    nk, grp = (qt + 1) * P, group[u]
                    act.wait_ge(nmax_ready, u + 1)
                    if u >= 2:
                        act.wait_ge(turned, u - 1)
                    if br == 0:
                        act.activation(prob[u % 2][:, 0:P], prob[u % 2][:, 0:P], ACT.Exp).then_inc(exp_done, 1)
                    else:
                        if h == 0 and grp >= 2:
                            act.wait_ge(o_read, grp - 1)
                        act.activation(prob[u % 2][:, 0:nk], self.ps[:, u % 2, 0:nk], ACT.Exp, bias=nmax[u % 2],
                                       accum_out=rsum[grp % 2][:, h:h + 1]).then_inc(exp_done, 1)
                if 1 <= u <= U and (u - 1) % 2 == 1:
                    copy_probs(act, u - 1)
                yield

        def dve_steps(dve):
            link = self.linker(dve, "ns_dve_chain")
            for u in range(U + 2):
                if u < U:
                    qt, br, h = units[u]
                    dve.wait_ge(qk_done, u + 1)
                    if u >= 2:
                        dve.wait_ge(exp_done, u - 1)
                    if br == 0:
                        src = self.ps[:, u % 2, 0:P].rearrange("p (h n) -> p h n", h=8)
                        link(dve.tensor_reduce(max8, src, AXX, ALU.max))
                        if u >= 2:
                            dve.wait_ge(turned, u - 1)
                        dve.tensor_tensor(prob[u % 2][:, 0:P].rearrange("p (h n) -> p h n", h=8), src,
                                          max8.unsqueeze(2).broadcast_to([P, 8, 16]), ALU.subtract
                                          ).then_inc(nmax_ready, 1)
                    else:
                        link(dve.tensor_reduce(nmax[u % 2], self.ps[:, u % 2, 0:(qt + 1) * P], AXX, ALU.max))
                        dve.tensor_scalar(nmax[u % 2], nmax[u % 2], -1.0, None, ALU.mult).then_inc(nmax_ready, 1)
                if 1 <= u <= U and units[u - 1][1] == 0:
                    dve.wait_ge(exp_done, u)
                    link(dve.tensor_reduce(rsum[group[u - 1] % 2],
                                           prob[(u - 1) % 2][:, 0:P].rearrange("p (h n) -> p h n", h=8), AXX,
                                           ALU.add))
                if 1 <= u <= U and (u - 1) % 2 == 0:
                    copy_probs(dve, u - 1)
                if u >= 2 and closes[u - 2]:
                    w = u - 2
                    qt, br, _ = units[w]
                    grp = group[w]
                    gate = self.gates[:, qt, :].rearrange("p (h c) -> p h c", c=3)[:, :, br]
                    dve.wait_ge(exp_done, w + 1)
                    link(dve.reciprocal(wgt, rsum[grp % 2]))
                    if br == 0 and qt == 0:
                        link(dve.tensor_scalar(wgt, wgt, self.c("cmp_any"), None, ALU.mult))
                    link(dve.tensor_tensor(wgt, wgt, gate, ALU.mult))
                    dve.wait_ge(pv_done, w + 1)
                    acc = pj[:, qt, N_Q:N_Q + 512].rearrange("p (r g d) -> p g r d", r=4, g=2)
                    src = self.ps[:, 3, :].rearrange("p (g r d) -> p g r d", g=2, r=4)
                    wb = wgt.rearrange("p (g r) -> p g r", g=2).unsqueeze(3).broadcast_to([P, 2, 4, HD])
                    ot = otmp.rearrange("p (g r d) -> p g r d", g=2, r=4)
                    if br == 0:
                        dve.tensor_tensor(acc, src, wb, ALU.mult).then_inc(o_read, 1)
                        dve.wait_ge(o_read, grp + 1)
                    else:
                        dve.tensor_tensor(ot, src, wb, ALU.mult).then_inc(o_read, 1)
                        dve.wait_ge(o_read, grp + 1)
                        link(dve.tensor_tensor(acc, acc, ot, ALU.add))
                yield

        return {"pe": pe_steps, "act": act_steps, "dve": dve_steps}

    def sample_cached(self):
        pj, ident = self.proj, self.c("ident")
        sem = self.sem
        turned, scored, pooled = sem("sk_turned"), sem("sk_scored"), sem("sk_pooled")
        copied = [sem("sk_copied_dve"), sem("sk_copied_act")]
        win_read = sem("sk_win_read")
        multiplied, z_read = sem("sk_multiplied"), sem("sk_z_summed")
        self.q_spread = sem("sk_q_spread")
        weighted, summed, pool_copied, mapped, map_copied, few_mm, few_read = (
            sem(n) for n in ("sk_weighted", "sk_summed", "sk_pool_copied", "sk_mapped", "sk_map_copied", "sk_few",
                             "sk_few_read"))
        slc_read, cum_added = sem("sx_slc_read"), sem("sx_cum_added")
        cmax, cexp, c_norm, imp_mm = sem("sx_cmp_max"), sem("sx_cmp_exp"), sem("sx_cmp_norm"), sem("sx_importance")
        w_max, w_exp, s_max, s_exp = sem("sx_win_max"), sem("sx_win_exp"), sem("sx_slc_max"), sem("sx_slc_exp")
        abs_r, e_r, ln_r, l_r, cum_r, w_r = (sem(n) for n in ("sx_abs", "sx_e", "sx_ln", "sx_softplus", "sx_cum",
                                                              "sx_sb_w"))
        p_ready, pt_done, pt_read = sem("sx_probs"), sem("sx_pt"), sem("sx_pt_read")
        v_weighted, v_summed, v_pooled, v_pool_copied, v_mapped, v_map_copied, v_item_done, all_done, kept, picked = (
            sem(n) for n in ("sv_weighted", "sv_summed", "sv_pooled", "sv_pool_copied", "sv_mapped",
                             "sv_map_copied", "sv_item_done", "sv_all_done", "sv_kept", "sv_picked"))
        opened = sem("sx_zeroed")
        self.freed[IT_KW] = ((turned, NB),)
        self.freed[IT_VW] = ((v_item_done, 1),)
        for b in range(NB):
            self.freed[IT_K + b] = ((turned, NB + 2 * (b + 1)), (weighted, b + 1), (multiplied, 2 * (b + 1)))
            self.freed[IT_V + b] = ((v_item_done, b + 2), (v_weighted, b + 1))

        scr = self.scr
        kt = [scr[:, 0:512], scr[:, 512:1024]]
        kw = scr[:, 1024:2048]
        kw_sum = scr[:, 2048:2176]
        plk, kct = scr[:, 2048:2304], scr[:, 2304:2560]
        R = NB * 8
        xs = self.xt[:, 2560:4160]
        pslc, pwin = xs[0:R, 0:1025], xs[0:R, 1026:1539]
        d_slc, d_win = scr[0:R, 2944:3008], scr[0:R, 3008:3072]
        pcmp, few = self.few[0:R, 0:32], self.few[0:R, 32:34]
        imp, t16, pen = self.few[0:R, 34:50], self.few[0:R, 50:66], self.few[0:R, 66:82]
        masked = scr[0:R, 2048:2304]
        z, lsb, esb = scr[:, 2560:2816], scr[:, 2304:2560], scr[:, 0:256]
        pt_slc = scr[:, 0:512]
        pt_win = scr[:, 512:768]
        w_sb = scr[:, 2048:2304]
        vw_sum = scr[:, 2432:2560]
        sm = lambda i: self.small[0:R, 40 + i:41 + i]
        gt = self.gate_rows
        cum = self.ps[:, 5, 0:256]
        self.o_sample = scr[:, 960:1008]
        unused = self.tt[:, 0:8, :].rearrange("p j t -> p (j t)")
        prod = [unused[:, 0:1024], unused[:, 1024:2048]]
        self.q_everywhere = unused[:, 2048:4096]
        pcmp_own = unused[0:R, 0:256]
        p_new = unused[0:NB, 256:768]
        pt_cmp = unused[:, 768:1024]
        plv = [unused[:, 1024:1152], unused[:, 1152:1280]]
        vc = [unused[:, 1280:1408], unused[:, 1408:1536]]
        o_kept = unused[:, 1536:2304]
        out_sb = lambda b, m: self.ps[32 * (b % 4):32 * (b % 4) + m, 4 + b // 4, 0:256]
        out_nsa = lambda b, m: self.ps[32 * (b % 4):32 * (b % 4) + m, 4 + b // 4, 256:384]
        q_slc = self.q_wide[:, 0:512].rearrange("p (b n) -> p b n", b=NB)

        units = []
        for b in range(NB):
            s = self.slot(IT_KW)
            units.append((IT_KW, [s[:, (b * 4 + j) * P:(b * 4 + j + 1) * P] for j in range(4)], 6, b, None))
        for b in range(NB):
            s = self.slot(IT_K + b)
            for half in range(2):
                units.append((IT_K + b, [s[:, 2048 + i * P:2048 + (i + 1) * P]
                                         for i in range(4 * half, 4 * half + 4)], 4 + half, b,
                              b if half == 1 else None))
        U = len(units)

        def key_copied(u):
            return copied[u % 2], u // 2 + 1

        def pe_steps(pe):
            for u in range(U + 1):
                if u < U:
                    item, pieces = units[u][:2]
                    self.wait_item(pe, item, (1,))
                    if u >= 1:
                        pe.wait_ge(*key_copied(u - 1))
                    for j, piece in enumerate(pieces):
                        ins = pe.transpose(self.ps[:, 7, j * P:(j + 1) * P], piece, ident)
                    ins.then_inc(turned, 1)
                if u == 1:
                    pe.wait_ge(self.q_built, 2)
                if u >= 1:
                    w = u - 1
                    _, _, bank, b, pool_b = units[w]
                    pe.wait_ge(*key_copied(w))
                    pe.matmul(self.ps[0:R, bank, :], q_slc[:, b, :], kt[w % 2], start=(b == 0), stop=(b == NB - 1),
                              skip_group_check=True).then_inc(scored, 1)
                    if pool_b is not None:
                        if pool_b == 0:
                            pe.wait_ge(win_read, 1)
                        pe.wait_ge(summed, pool_b + 1)
                        pe.matmul(self.ps[:, 6, pool_b * 32:(pool_b + 1) * 32], kw_sum, self.c("blk_ind32"),
                                  start=True, stop=True, skip_group_check=True).then_inc(pooled, 1)
                yield
            pe.wait_ge(pool_copied, 1)
            pe.matmul(self.ps[:, 6, 256:512], self.phi_k[:], plk, start=True, stop=True,
                      skip_group_check=True).then_inc(mapped, 1)
            yield
            q64 = self.q_nsa[:].rearrange("p b h -> p (b h)")
            pe.wait_ge(map_copied, 1)
            pe.matmul(self.ps[0:R, 6, 0:256], q64, kct, start=True, stop=True, skip_group_check=True)
            for j, blk in enumerate((T_SK, T_WK)):
                ins = pe.matmul(self.ps[0:R, 6, 256 + 8 * j:264 + 8 * j], q64, self.tt[:, blk, SEQ:TOK], start=True,
                                stop=True, skip_group_check=True)
            ins.then_inc(few_mm, 1)
            yield
            yield
            pe.wait_ge(c_norm, 1)
            pe.wait_ge(few_read, 1)
            pe.matmul(self.ps[0:R, 6, 0:16], self.c("grp")[0:R], imp, start=True, stop=True,
                      skip_group_check=True).then_inc(imp_mm, 1)
            yield
            pe.wait_ge(l_r, 1)
            pe.wait_ge(slc_read, 1)
            for i in range(7, -1, -1):
                row = lsb[:, i * 32:(i + 1) * 32].unsqueeze(1)
                ins = pe.matmul(cum[:, 0:(i + 1) * 32], self.c("neg_suffix"), row.broadcast_to([P, i + 1, 32]),
                                start=(i == 7), stop=True, skip_group_check=True)
                if i < 7:
                    ins = pe.matmul(cum[:, (i + 1) * 32:256], self.c("neg_later"), row.broadcast_to([P, 7 - i, 32]),
                                    start=False, stop=True, skip_group_check=True)
            ins.then_inc(cum_r, 1)
            yield
            pe.wait_ge(p_ready, 1)
            for i in range(8):
                ins = pe.transpose(self.ps[:, 7, i * R:(i + 1) * R], pslc[:, i * P:(i + 1) * P], ident[0:R, 0:R])
            ins.then_inc(pt_done, 1)
            yield
            pe.wait_ge(pt_read, 1)
            for j in range(4):
                pe.transpose(self.ps[:, 7, j * R:(j + 1) * R], pwin[:, j * P:(j + 1) * P], ident[0:R, 0:R])
            for half in range(2):
                pe.transpose(self.ps[:, 7, 256 + half * R:256 + (half + 1) * R],
                             pcmp_own[:, half * P:(half + 1) * P], ident[0:R, 0:R])
            for j, dg in enumerate((d_slc, d_win)):
                ins = pe.matmul(self.ps[0:NB, 7, 384 + j * R:384 + (j + 1) * R], self.c("seq_ind")[0:R], dg,
                                start=True, stop=True, skip_group_check=True)
            ins.then_inc(pt_done, 1)
            yield
            pe.wait_ge(pt_read, 2)
            pe.wait_ge(w_r, 1)
            zero_row = self.c("neg_later")[0:1]
            for half in range(2):
                pe.matmul(self.ps[:, 4 + half, 0:384], zero_row, zero_row.unsqueeze(1).broadcast_to([1, 3, P]),
                          start=True, stop=False, skip_group_check=True)
                for k, v0 in enumerate((S_V, W_V)):
                    pe.matmul(self.ps[:, 4 + half, 256:384], p_new[:, k * 256 + half * P:k * 256 + (half + 1) * P],
                              pj[0:NB, 4, v0:v0 + P], start=False, stop=False, skip_group_check=True)
            self.wait_item(pe, IT_VW)
            w = self.slot(IT_VW)
            for b in range(NB):
                for j in range(4):
                    ins = pe.matmul(out_nsa(b, 8), pt_win[:, j * 64 + b * 8:j * 64 + b * 8 + 8],
                                    w[:, (b * 4 + j) * P:(b * 4 + j + 1) * P], start=False, stop=False,
                                    skip_group_check=True)
                if b == 3:
                    yield
            ins.then_inc(v_item_done, 1)
            yield
            for step in range(2 * NB + 2):
                b, part = divmod(step, 2)
                half = b // 4 - 1
                if b % 4 == 0 and half >= 0 and part == 0:
                    pe.wait_ge(v_pool_copied, half + 1)
                    pe.matmul(self.ps[:, 7, 0:P], plv[half], self.phi_v[:], start=True, stop=True,
                              skip_group_check=True).then_inc(v_mapped, 1)
                if b % 4 == 0 and half >= 0 and part == 1:
                    pe.wait_ge(v_map_copied, half + 1)
                    ins = pe.matmul(self.ps[:, 4 + half, 256:384], pt_cmp[:, half * P:(half + 1) * P], vc[half],
                                    start=False, stop=(half == 1), skip_group_check=True)
                    if half == 1:
                        ins.then_inc(all_done, 1)
                if b < NB:
                    self.wait_item(pe, IT_V + b, (0, 1))
                    w = self.slot(IT_V + b)
                    for i in range(4 * part, 4 * part + 4):
                        pe.matmul(out_sb(b, 4), w_sb[:, i * 32 + b * 4:i * 32 + b * 4 + 4],
                                  w[:, i * 256:(i + 1) * 256], start=False, stop=False, skip_group_check=True)
                        ins = pe.matmul(out_nsa(b, 8), pt_slc[:, i * 64 + b * 8:i * 64 + b * 8 + 8],
                                        w[:, 2048 + i * P:2048 + (i + 1) * P], start=False, stop=False,
                                        skip_group_check=True)
                    if part == 1:
                        ins.then_inc(v_item_done, 1)
                        pe.wait_ge(v_summed, b + 1)
                        if b == 4:
                            pe.wait_ge(v_pool_copied, 1)
                        pe.matmul(self.ps[:, 6, b * 32:(b + 1) * 32], vw_sum, self.c("blk_ind32"), start=True,
                                  stop=True, skip_group_check=True).then_inc(v_pooled, 1)
                yield
            yield
            pe.wait_ge(kept, 1)
            for half in range(2):
                k0, c0 = half * 384, half * 24
                for x in range(2):
                    pe.matmul(self.ps[:, 6, c0 + 4 * x:c0 + 4 * x + 4], o_kept[:, k0 + x * P:k0 + (x + 1) * P],
                              self.c("blk_ind"), start=True, stop=True, skip_group_check=True)
                ins = pe.matmul(self.ps[:, 6, c0 + 8:c0 + 24], o_kept[:, k0 + 256:k0 + 384], self.c("pick_head"),
                                start=True, stop=True, skip_group_check=True)
            ins.then_inc(picked, 1)
            yield

        def copy_keys(eng, u):
            eng.wait_ge(turned, u + 1)
            if u >= 2:
                eng.wait_ge(scored, u - 1)
            if u % 2 == 0:
                eng.tensor_copy(kt[0], self.ps[:, 7, :]).then_inc(copied[0], 1)
            else:
                eng.activation(kt[1], self.ps[:, 7, :], ACT.Copy).then_inc(copied[1], 1)

        def sum_products(dve, b, half):
            dve.wait_ge(multiplied, 2 * b + half + 1)
            dst = z.rearrange("p (i b h) -> p i b h", i=8, b=NB)[:, 4 * half:4 * half + 4, b, :]
            dve.tensor_reduce(dst, prod[half].rearrange("p (i h d) -> p i h d", i=4, h=4), AXX, ALU.add
                              ).then_inc(z_read, 1)

        def dve_steps(dve):
            link = self.linker(dve, "sx_dve_chain")
            for u in range(U + 1):
                if u < U and u % 2 == 0:
                    copy_keys(dve, u)
                if u == NB:
                    dve.wait_ge(scored, NB)
                    dve.tensor_copy(pwin[:, 0:512], self.ps[0:R, 6, :]).then_inc(win_read, 1)
                b, odd = divmod(u - NB, 2)
                if u > NB and odd == 0:
                    sum_products(dve, b - 1, 1)
                if u > NB and odd == 1:
                    self.wait_item(dve, IT_K + b, (2,))
                    dve.tensor_tensor(kw.rearrange("p (i g d) -> p i g d", i=8, g=2),
                                      self.slot(IT_K + b)[:, 3072:4096].rearrange("p (i g d) -> p i g d", i=8, g=2),
                                      self.pos8_k[:].unsqueeze(2).broadcast_to([P, 8, 2, HD]), ALU.mult
                                      ).then_inc(weighted, 1)
                    dve.wait_ge(weighted, b + 1)
                    if b >= 1:
                        dve.wait_ge(pooled, b)
                    dve.tensor_reduce(kw_sum, kw.rearrange("p (i n) -> p n i", i=8), AXX, ALU.add
                                      ).then_inc(summed, 1)
                    sum_products(dve, b, 0)
                yield
            dve.wait_ge(pooled, NB)
            dve.tensor_copy(plk, self.ps[:, 6, 0:256]).then_inc(pool_copied, 1)
            dve.wait_ge(scored, U)
            dve.wait_ge(z_read, 2 * NB)
            dve.memset(p_new, 0.0)
            dve.memset(pt_cmp, 0.0).then_inc(opened, 1)
            dve.tensor_copy(pslc[:, 0:512], self.ps[0:R, 4, :])
            dve.tensor_copy(pslc[:, 512:1024], self.ps[0:R, 5, :]).then_inc(slc_read, 1)
            yield
            dve.wait_ge(mapped, 1)
            dve.tensor_copy(kct, self.ps[:, 6, 256:512]).then_inc(map_copied, 1)
            yield
            dve.wait_ge(few_mm, 1)
            own = self.c("seq_ind")[0:R]
            link(dve.tensor_tensor(masked.rearrange("p (b n) -> p b n", b=NB),
                                   self.ps[0:R, 6, 0:256].rearrange("p (b n) -> p b n", b=NB),
                                   own.unsqueeze(2).broadcast_to([R, NB, 32]), ALU.mult))
            link(dve.tensor_reduce(pcmp, masked.rearrange("p (b n) -> p n b", b=NB), AXX, ALU.add))
            link(dve.tensor_tensor(masked[:, 0:16].rearrange("p (j b) -> p j b", j=2),
                                   self.ps[0:R, 6, 256:272].rearrange("p (j b) -> p j b", j=2),
                                   own.unsqueeze(1).broadcast_to([R, 2, NB]), ALU.mult))
            dve.tensor_reduce(few, masked[:, 0:16].rearrange("p (j b) -> p j b", j=2), AXX, ALU.add
                              ).then_inc(few_read, 1)
            dve.wait_ge(few_read, 1)
            link(dve.tensor_reduce(sm(0), pcmp, AXX, ALU.max))
            dve.tensor_scalar(sm(1), sm(0), -1.0, None, ALU.mult).then_inc(cmax, 1)
            yield
            link(dve.tensor_copy(pwin[:, 512:513], few[:, 1:2]))
            link(dve.tensor_reduce(sm(2), pwin, AXX, ALU.max))
            dve.tensor_scalar(sm(3), sm(2), -1.0, None, ALU.mult).then_inc(w_max, 1)
            dve.wait_ge(cexp, 1)
            link(dve.reciprocal(sm(4), sm(5)))
            link(dve.tensor_scalar(pcmp, pcmp, sm(4), None, ALU.mult))
            dve.tensor_reduce(imp, pcmp.rearrange("p (n c) -> p n c", c=2), AXX, ALU.add).then_inc(c_norm, 1)
            dve.wait_ge(c_norm, 1)
            link(dve.tensor_scalar(pcmp, pcmp, gt[:, 0:1], None, ALU.mult))
            link(dve.tensor_tensor(pcmp_own.rearrange("p (b n) -> p b n", b=NB),
                                   pcmp.unsqueeze(1).broadcast_to([R, NB, 32]),
                                   own.unsqueeze(2).broadcast_to([R, NB, 32]), ALU.mult))
            dve.wait_ge(ln_r, 1)
            dve.scalar_tensor_tensor(out=lsb, in0=z, scalar=0.0, in1=esb, op0=ALU.max, op1=ALU.add
                                     ).then_inc(l_r, 1)
            yield
            dve.wait_ge(imp_mm, 1)
            link(dve.tensor_copy(imp, self.ps[0:R, 6, 0:16]))
            link(dve.tensor_reduce(sm(6), imp[:, 1:16], AXX, ALU.min))
            link(dve.tensor_scalar(t16[:, 1:16], imp[:, 1:16], sm(6), None, ALU.is_le))
            link(dve.tensor_tensor(t16[:, 1:16], t16[:, 1:16], self.c("blk_idx")[0:R, 1:16], ALU.mult))
            link(dve.tensor_reduce(sm(7), t16[:, 1:16], AXX, ALU.max))
            link(dve.tensor_scalar(pen, self.c("blk_idx")[0:R], sm(7), NEG, ALU.is_equal, ALU.mult))
            dve.wait_ge(slc_read, 1)
            pv = pslc[:, 0:1024].rearrange("p (i n q) -> p i n q", i=8, n=16)
            link(dve.tensor_tensor(pv, pv, pen.unsqueeze(1).unsqueeze(3).broadcast_to([R, 8, 16, 8]), ALU.add))
            link(dve.tensor_copy(pslc[:, 1024:1025], few[:, 0:1]))
            link(dve.tensor_reduce(sm(8), pslc, AXX, ALU.max))
            dve.tensor_scalar(sm(9), sm(8), -1.0, None, ALU.mult).then_inc(s_max, 1)
            yield
            dve.wait_ge(cum_r, 1)
            dve.tensor_tensor(z, z, cum, ALU.add).then_inc(cum_added, 1)
            dve.wait_ge(w_exp, 1)
            link(dve.reciprocal(sm(10), sm(11)))
            link(dve.tensor_tensor(sm(10), sm(10), gt[:, 2:3], ALU.mult))
            link(dve.tensor_scalar(pwin, pwin, sm(10), None, ALU.mult))
            dve.wait_ge(s_exp, 1)
            link(dve.reciprocal(sm(13), sm(14)))
            link(dve.tensor_tensor(sm(13), sm(13), gt[:, 1:2], ALU.mult))
            link(dve.tensor_scalar(pslc, pslc, sm(13), None, ALU.mult))
            dve.tensor_scalar(d_slc, ident[0:R, 0:R], pslc[:, 1024:1025], None, ALU.mult)
            dve.tensor_scalar(d_win, ident[0:R, 0:R], pwin[:, 512:513], None, ALU.mult).then_inc(p_ready, 1)
            yield
            dve.wait_ge(pt_done, 1)
            dve.tensor_copy(pt_slc, self.ps[:, 7, :]).then_inc(pt_read, 1)
            yield
            dve.wait_ge(pt_done, 2)
            dve.tensor_copy(pt_win, self.ps[:, 7, 0:256])
            dve.wait_ge(opened, 1)
            for half in range(2):
                dve.tensor_copy(
                    pt_cmp[:, half * P:(half + 1) * P].rearrange("p (b y) -> p b y", y=32)[:, :, 0:8],
                    self.ps[:, 7, 256 + half * 96:288 + half * 96].rearrange("p (b h) -> p b h", b=4))
            dve.tensor_copy(p_new.rearrange("p (k b y) -> p k b y", k=2, y=32)[:, :, :, 0:8],
                            self.ps[0:NB, 7, 384:512].rearrange("p (k b h) -> p k b h", k=2, b=NB)
                            ).then_inc(pt_read, 1)
            yield
            yield
            for step in range(2 * NB + 2):
                b, part = divmod(step, 2)
                if part == 0 and b < NB:
                    dve.wait_ge(v_weighted, b + 1)
                    if b >= 1:
                        dve.wait_ge(v_pooled, b)
                    dve.tensor_reduce(vw_sum, kw.rearrange("p (i n) -> p n i", i=8), AXX, ALU.add
                                      ).then_inc(v_summed, 1)
                yield
            dve.wait_ge(all_done, 1)
            own_head = self.c("own_head").unsqueeze(2).broadcast_to([P, 6, HD])
            for half in range(2):
                ins = dve.tensor_tensor(o_kept[:, half * 384:(half + 1) * 384].rearrange("p (j d) -> p j d", j=6),
                                        self.ps[:, 4 + half, 0:384].rearrange("p (j d) -> p j d", j=6), own_head,
                                        ALU.mult)
            ins.then_inc(kept, 1)
            yield
            yield
            dve.wait_ge(picked, 1)
            dve.tensor_copy(self.o_sample, self.ps[:, 6, 0:48])
            yield

        def act_steps(act):
            for u in range(U + 1):
                if u < U and u % 2 == 1:
                    copy_keys(act, u)
                yield
            yield
            act.wait_ge(scored, U)
            act.wait_ge(z_read, 2 * NB)
            act.activation(esb, z, ACT.Abs).then_inc(abs_r, 1)
            act.wait_ge(abs_r, 1)
            act.activation(esb, esb, ACT.Exp, scale=-1.0).then_inc(e_r, 1)
            yield
            act.wait_ge(e_r, 1)
            act.activation(esb, esb, ACT.Ln, bias=1.0).then_inc(ln_r, 1)
            act.wait_ge(cmax, 1)
            act.activation(pcmp, pcmp, ACT.Exp, bias=sm(1), accum_out=sm(5)).then_inc(cexp, 1)
            yield
            act.wait_ge(w_max, 1)
            act.activation(pwin, pwin, ACT.Exp, bias=sm(3), accum_out=sm(11)).then_inc(w_exp, 1)
            yield
            act.wait_ge(s_max, 1)
            act.activation(pslc, pslc, ACT.Exp, bias=sm(9), accum_out=sm(14)).then_inc(s_exp, 1)
            yield
            act.wait_ge(cum_added, 1)
            act.activation(w_sb, z, ACT.Exp).then_inc(w_r, 1)
            yield
            yield
            yield
            yield
            for step in range(2 * NB + 2):
                b, part = divmod(step, 2)
                if b in (3, 7) and part == 1:
                    act.wait_ge(v_pooled, b + 1)
                    act.activation(plv[b // 4], self.ps[:, 6, b // 4 * P:(b // 4 + 1) * P], ACT.Copy
                                   ).then_inc(v_pool_copied, 1)
                if b in (4, 8) and part == 0:
                    act.wait_ge(v_mapped, b // 4)
                    act.activation(vc[b // 4 - 1], self.ps[:, 7, 0:P], ACT.Copy).then_inc(v_map_copied, 1)
                yield

        def pool_steps(pool):
            self.gather(pool, IT_K + 1)
            pool.memset(self.q_wide[:], 0.0).then_inc(self.q_cleared, 1)
            pool.wait_ge(self.q_cleared, 2)
            for b in range(NB):
                ins = pool.tensor_copy(q_slc[:, b, 8 * b:8 * b + 8], self.q_nsa[:, b, :])
            ins.then_inc(self.q_built, 1)
            for b in range(NB):
                self.wait_item(pool, IT_K + b, (0,))
                if b == 0:
                    pool.wait_ge(self.q_spread, 16)
                for half in range(2):
                    if b >= 1:
                        pool.wait_ge(z_read, 2 * b - 1 + half)
                    pool.tensor_tensor(prod[half].rearrange("p (i n) -> p i n", i=4),
                                       self.slot(IT_K + b)[:, half * 1024:(half + 1) * 1024].rearrange(
                                           "p (i n) -> p i n", i=4),
                                       self.q_everywhere[:, b * 256:(b + 1) * 256].unsqueeze(1).broadcast_to(
                                           [P, 4, 256]), ALU.mult).then_inc(multiplied, 1)
                if b + 2 < NB:
                    self.gather(pool, IT_K + b + 2)
                yield
            self.gather(pool, IT_V)
            self.gather(pool, IT_V + 1)
            for b in range(NB):
                self.wait_item(pool, IT_V + b, (2,))
                if b == 0:
                    pool.wait_ge(summed, NB)
                if b >= 1:
                    pool.wait_ge(v_summed, b)
                pool.tensor_tensor(kw.rearrange("p (i g d) -> p i g d", i=8, g=2),
                                   self.slot(IT_V + b)[:, 3072:4096].rearrange("p (i g d) -> p i g d", i=8, g=2),
                                   self.pos8_v[:].unsqueeze(2).broadcast_to([P, 8, 2, HD]), ALU.mult
                                   ).then_inc(v_weighted, 1)
                if b + 2 < NB:
                    self.gather(pool, IT_V + b + 2)
                yield

        return {"pe": pe_steps, "act": act_steps, "dve": dve_steps, "pool": pool_steps}

    def output_projection(self):
        nc, l, pj = self.nc, self.l, self.proj
        turned, t_copied, mm_done, added, s_placed = (
            self.sem(s) for s in ("op_turned", "op_copied", "op_mm", "op_added", "op_sample_placed"))
        fm_ready, back_done = self.sem("op_features_copied"), self.sem("op_turned_back")
        H = TOK // 2
        fm = lambda u: self.tt[:, u % 2, :]
        for n in range(2):
            self.freed[IT_WO + n] = ((mm_done, 4 * (n + 1)),)
        src_cols = [SB_Q, SB_Q + P, R_Q, R_Q + P] + [N_Q + j * P for j in range(4)]
        with nc.Block() as block:
            @block.sync
            def _(sp):
                self.issue_until(sp, l, IT_UP + SLOTS)
                sp.wait_ge(self.shift_done, 32)

            @block.tensor
            def _(pe):
                ident = self.c("ident")
                for t in range(4):
                    if t >= 2:
                        pe.wait_ge(t_copied, 2 * (t - 1))
                    for k in range(KD):
                        ins = pe.transpose(self.ps[:, 2 * (t % 2) + k // 4, (k % 4) * P:(k % 4 + 1) * P],
                                           pj[:, t, src_cols[k]:src_cols[k] + P], ident)
                    ins.then_inc(turned, 1)
                pe.wait_ge(t_copied, 6)
                for x in range(2):
                    ins = pe.transpose(self.ps[:, 0, x * P:x * P + NB], pj[0:NB, 4, R_Q + x * P:R_Q + (x + 1) * P],
                                       ident[0:NB, 0:NB])
                ins.then_inc(turned, 1)
                pe.wait_ge(t_copied, 9)
                pe.wait_ge(s_placed, 1)
                for u in range(9):
                    if u < 8:
                        n, f = divmod(u, 4)
                        if f == 0:
                            self.wait_item(pe, IT_WO + n)
                        w = self.slot(IT_WO + n).rearrange("p (k n) -> p k n", k=KD)
                        if u >= 2:
                            pe.wait_ge(fm_ready, u - 1)
                        for half in range(2):
                            for k in range(KD):
                                ins = pe.matmul(self.ps[:, 4 + 2 * (u % 2) + half, 0:H], w[:, k, f * P:(f + 1) * P],
                                                self.xtv[:, k, half * H:(half + 1) * H], start=(k == 0),
                                                stop=(k == KD - 1))
                        ins.then_inc(mm_done, 1)
                    if u >= 1:
                        v = u - 1
                        pe.wait_ge(fm_ready, v + 1)
                        if v >= 2:
                            pe.wait_ge(added, v - 1)
                        for t in range(TILES):
                            dst = self.ps[0:rows(t), 2 * (v % 2) + t // 4, (t % 4) * P:(t % 4 + 1) * P]
                            ins = pe.transpose(dst, fm(v)[:, cols(t)], ident)
                        ins.then_inc(back_done, 1)

            @block.gpsimd
            def _(pool):
                src = self.o_sample.rearrange("p (x j b) -> p j x b", x=2, j=6)
                for blocks, part in ((slice(0, 2), src[:, 0:2]), (slice(4, 8), src[:, 2:6])):
                    ins = pool.tensor_copy(self.xtv[:, blocks, SEQ:TOK].rearrange("p j (x b) -> p j x b", x=2), part)
                ins.then_inc(s_placed, 1)

            @block.scalar
            def _(act):
                for t in range(4):
                    act.wait_ge(turned, t + 1)
                    for j in range(2):
                        act.activation(self.xtv[:, 4 * j:4 * j + 4, cols(t)],
                                       self.ps[:, 2 * (t % 2) + j, :].rearrange("p (k n) -> p k n", k=4), ACT.Copy
                                       ).then_inc(t_copied, 1)
                act.wait_ge(turned, 5)
                act.activation(self.xtv[:, 2:4, SEQ:TOK],
                               self.ps[:, 0, 0:256].rearrange("p (k n) -> p k n", k=2)[:, :, 0:NB], ACT.Copy
                               ).then_inc(t_copied, 1)
                for u in range(8):
                    act.wait_ge(mm_done, u + 1)
                    if u >= 2:
                        act.wait_ge(back_done, u - 1)
                    act.activation(fm(u).rearrange("p (x n) -> p x n", x=2),
                                   self.ps[:, 4 + 2 * (u % 2):6 + 2 * (u % 2), 0:H], ACT.Copy).then_inc(fm_ready, 1)

            @block.vector
            def _(dve):
                for u in range(8):
                    dve.wait_ge(back_done, u + 1)
                    x = self.x_res[:, 0:4, u * P:(u + 1) * P]
                    dve.tensor_tensor(x, x, self.ps[:, 2 * (u % 2), :].rearrange("p (t n) -> p t n", t=4), ALU.add)
                    x = self.x_res[0:NB, 4, u * P:(u + 1) * P]
                    dve.tensor_tensor(x, x, self.ps[0:NB, 2 * (u % 2) + 1, 0:P], ALU.add).then_inc(added, 1)

    def mlp_up(self):
        nc, l = self.nc, self.l
        mm_done, relu_done, sq_done = (self.sem(s) for s in ("up_mm", "up_relu", "up_square"))
        H = TOK // 2
        for c in range(8):
            self.freed[IT_UP + c] = ((mm_done, 4 * (c + 1)),)
        rbuf = [self.scr[:, 0:TOK], self.scr[:, TOK:2 * TOK]]
        with nc.Block() as block:
            @block.sync
            def _(sp):
                self.issue_until(sp, l, IT_DN + SLOTS)

            @block.tensor
            def _(pe):
                for u in range(FF // P):
                    c, f = divmod(u, 4)
                    if f == 0:
                        self.wait_item(pe, IT_UP + c)
                    if u >= 4:
                        pe.wait_ge(relu_done, u - 3)
                    w = self.slot(IT_UP + c).rearrange("p (k n) -> p k n", k=KD)
                    for half in range(2):
                        for k in range(KD):
                            ins = pe.matmul(self.ps[:, 2 * (u % 4) + half, 0:H], w[:, k, f * P:(f + 1) * P],
                                            self.xtv[:, k, half * H:(half + 1) * H], start=(k == 0),
                                            stop=(k == KD - 1))
                    ins.then_inc(mm_done, 1)

            @block.scalar
            def _(act):
                for u in range(FF // P):
                    act.wait_ge(mm_done, u + 1)
                    if u >= 2:
                        act.wait_ge(sq_done, u - 1)
                    act.activation(rbuf[u % 2].rearrange("p (x n) -> p x n", x=2),
                                   self.ps[:, 2 * (u % 4):2 * (u % 4) + 2, 0:H], ACT.Relu).then_inc(relu_done, 1)

            @block.vector
            def _(dve):
                for u in range(FF // P):
                    dve.wait_ge(relu_done, u + 1)
                    dve.tensor_tensor(self.hid[:, u, :], rbuf[u % 2], rbuf[u % 2], ALU.mult).then_inc(sq_done, 1)

    def mlp_down(self):
        nc, l = self.nc, self.l
        part, f_done, copied, turned, added = (self.sem(s) for s in ("dn_part", "dn_features", "dn_copied",
                                                                     "dn_turned", "dn_added"))
        H = TOK // 2
        for i in range(8):
            self.freed[IT_DN + i] = ((part, i + 1),)
        with nc.Block() as block:
            @block.sync
            def _(sp):
                self.issue_until(sp, l, N_ITEMS)

            @block.tensor
            def _(pe):
                for n in range(2):
                    for q in range(4):
                        i = IT_DN + 4 * n + q
                        self.wait_item(pe, i)
                        w = self.slot(i).rearrange("p (k n) -> p k n", k=8)
                        for f in range(4):
                            if n == 1 and q == 0:
                                pe.wait_ge(added, f + 1)
                            for half in range(2):
                                for k in range(8):
                                    ins = pe.matmul(self.ps[:, 2 * f + half, 0:H], w[:, k, f * P:(f + 1) * P],
                                                    self.hid[:, q * 8 + k, half * H:(half + 1) * H],
                                                    start=(q == 0 and k == 0), stop=(q == 3 and k == 7),
                                                    skip_group_check=True)
                            if q == 3 and f < 3:
                                ins.then_inc(f_done, 1)
                        ins.then_inc(part, 1)
                    for f in range(4):
                        pe.wait_ge(copied, 4 * n + f + 1)
                        for t in range(TILES):
                            dst = self.ps[0:rows(t), 2 * f + t // 4, (t % 4) * P:(t % 4 + 1) * P]
                            ins = pe.transpose(dst, self.xtv[:, 4 * n + f, cols(t)], self.c("ident"))
                        ins.then_inc(turned, 1)

            @block.scalar
            def _(act):
                for n in range(2):
                    for f in range(4):
                        if f < 3:
                            act.wait_ge(f_done, 3 * n + f + 1)
                        else:
                            act.wait_ge(part, 4 * (n + 1))
                        act.activation(self.xtv[:, 4 * n + f, :].rearrange("p (x n) -> p x n", x=2),
                                       self.ps[:, 2 * f:2 * f + 2, 0:H], ACT.Copy).then_inc(copied, 1)

            @block.vector
            def _(dve):
                for u in range(8):
                    f = u % 4
                    dve.wait_ge(turned, u + 1)
                    x = self.x_res[:, 0:4, u * P:(u + 1) * P]
                    dve.tensor_tensor(x, x, self.ps[:, 2 * f, :].rearrange("p (t n) -> p t n", t=4), ALU.add)
                    x = self.x_res[0:NB, 4, u * P:(u + 1) * P]
                    dve.tensor_tensor(x, x, self.ps[0:NB, 2 * f + 1, 0:P], ALU.add).then_inc(added, 1)


_INS = ['x_prompt', 'x_sample', 'cache_sb_k', 'cache_sb_v', 'cache_cmp_k', 'cache_cmp_v', 'cache_slc_k',
        'cache_slc_v', 'state_win_k', 'state_win_v', 'state_ret', 'page_table', 'norm1_g', 'w_in', 'nsa_q_norm',
        'nsa_k_norm', 'cmp_pos_k', 'cmp_pos_v', 'cmp_w_k', 'cmp_w_v', 'w_out', 'norm2_g', 'w_up', 'w_down']
_OUTS = ([("y_prompt", (1, SEQ, D)), ("y_sample", (NB, 1, D))]
         + [(f"p_sb_{x}", (DEPTH, 1, SEQ, 4, HD)) for x in "kv"]
         + [(f"p_{n}_{x}", (DEPTH, 1, SEQ, 2, HD)) for n in ("cmp", "slc", "win") for x in "kv"]
         + [("p_ret", (DEPTH, 1, 4, HD, HD))]
         + [(f"s_sb_{x}", (DEPTH, NB, 1, 4, HD)) for x in "kv"]
         + [(f"s_{n}_{x}", (DEPTH, NB, 1, 2, HD)) for n in ("cmp", "slc") for x in "kv"]
         + [(f"s_win_{x}", (DEPTH, NB, WIN, 2, HD)) for x in "kv"]
         + [("s_ret", (DEPTH, NB, 4, HD, HD))])


def kernel(**inputs):
    import numpy as _np
    import concourse.bacc as _bacc
    from concourse import mybir as _mybir
    from concourse.bass_utils import run_bass_kernel_spmd as _run

    nc = _bacc.Bacc("TRN2", target_bir_lowering=False, num_devices=1)
    arrays, ins, outs = {}, {}, {}
    for name in _INS:
        a = _np.ascontiguousarray(inputs[name])
        arrays[f"in_{name}"] = a
        ins[name] = nc.dram_tensor(f"in_{name}", a.shape, _mybir.dt.from_np(a.dtype), kind="ExternalInput").ap()
    c = shape_constants()
    arrays["in_consts"] = c
    consts = nc.dram_tensor("in_consts", c.shape, _mybir.dt.from_np(c.dtype), kind="ExternalInput").ap()
    for name, shape in _OUTS:
        outs[name] = nc.dram_tensor(f"out_{name}", shape, F32, kind="ExternalOutput").ap()
    build(nc, ins, outs, consts)
    r = _run(nc, [arrays], core_ids=[0])
    return tuple(r.results[0][f"out_{name}"] for name, _ in _OUTS)
```
